# Optimizing a Trainium2 kernel written in Bass

```python
import math
import jax, jax.numpy as jnp
from jax import lax
import numpy as np

D_MODEL = 1024
BATCH = 1
SEQ = 256
DEPTH = 1

CHUNK = 64
Q_BLOCK = 128
EPS = 1e-6

SB_HEADS = 8
SB_HEAD_DIM = 64
SB_WIDTH = SB_HEADS * SB_HEAD_DIM

MLA_HEADS = 8
MLA_NOPE_DIM = 64
MLA_ROPE_DIM = 32
MLA_QK_DIM = MLA_NOPE_DIM + MLA_ROPE_DIM
MLA_V_DIM = 64
MLA_Q_LORA = 384
MLA_KV_LORA = 256
MLA_WIDTH = MLA_HEADS * MLA_V_DIM
ROPE_THETA = 10000.0

IN_COLS = (SB_WIDTH, SB_WIDTH, SB_WIDTH,
           MLA_Q_LORA, MLA_KV_LORA, MLA_ROPE_DIM,
           D_MODEL, D_MODEL)
IN_WIDTH = sum(IN_COLS)
IN_SPLITS = tuple(int(c) for c in np.cumsum(IN_COLS)[:-1])

N_EXPERTS = 32
TOP_K = 4
D_FF = 1024
SWIGLU_LIMIT = 7.0
SWIGLU_ALPHA = 1.702
EXPERT_BLOCK = 256

kernel_name = "hybrid_stickbreak_mla_moe_block"

def rmsnorm(x, g):
    xf = x.astype(jnp.float32)
    xf = xf * lax.rsqrt(jnp.mean(xf * xf, axis=-1, keepdims=True) + EPS)
    return (xf * g.astype(jnp.float32)).astype(x.dtype)

def apply_rope(x, positions):
    half = MLA_ROPE_DIM // 2
    inv_freq = ROPE_THETA ** (-jnp.arange(half, dtype=jnp.float32) / half)
    ang = positions.astype(jnp.float32)[:, :, None, None] * inv_freq
    cos = jnp.cos(ang).astype(x.dtype)
    sin = jnp.sin(ang).astype(x.dtype)
    x1, x2 = x[..., :half], x[..., half:]
    return jnp.concatenate([x1 * cos - x2 * sin, x2 * cos + x1 * sin], axis=-1)

def stick_breaking_attention(q, k, v):
    seq = q.shape[2]
    scale = 1.0 / math.sqrt(q.shape[-1])
    outs = []
    for i in range(seq // Q_BLOCK):
        q0 = i * Q_BLOCK
        kn = q0 + Q_BLOCK
        z = jnp.einsum('bhqd,bhkd->bhqk', q[:, :, q0:kn], k[:, :, :kn]).astype(jnp.float32) * scale
        t_idx = q0 + jnp.arange(Q_BLOCK)[:, None]
        s_idx = jnp.arange(kn)[None, :]
        strict = s_idx < t_idx
        log_beta = jax.nn.log_sigmoid(z)
        log_stay = jnp.where(strict, log_beta - z, 0.0)
        later = lax.cumsum(log_stay, axis=3, reverse=True) - log_stay
        a = jnp.where(strict, jnp.exp(log_beta + later), 0.0)
        outs.append(jnp.einsum('bhqk,bhkd->bhqd', a.astype(v.dtype), v[:, :, :kn]))
    return jnp.concatenate(outs, axis=2)

def chunk_causal_softmax_attention(q, k, v):
    seq = q.shape[2]
    scale = 1.0 / math.sqrt(q.shape[-1])
    outs = []
    for i in range(seq // Q_BLOCK):
        q0 = i * Q_BLOCK
        kn = q0 + Q_BLOCK
        s = jnp.einsum('bhqd,bhkd->bhqk', q[:, :, q0:kn], k[:, :, :kn]).astype(jnp.float32) * scale
        q_chunk = (q0 + jnp.arange(Q_BLOCK))[:, None] // CHUNK
        k_chunk = jnp.arange(kn)[None, :] // CHUNK
        s = jnp.where(k_chunk <= q_chunk, s, -jnp.inf)
        p = jax.nn.softmax(s, axis=-1)
        outs.append(jnp.einsum('bhqk,bhkd->bhqd', p.astype(v.dtype), v[:, :, :kn]))
    return jnp.concatenate(outs, axis=2)

def moe_ffn(h, w_router, b_router, w_up, b_up, w_down, b_down):
    n_tok, d = h.shape
    logits = (h @ w_router + b_router).astype(jnp.float32)
    top_logit, top_idx = lax.top_k(logits, TOP_K)
    top_w = jax.nn.softmax(top_logit, axis=-1)
    n_assign = n_tok * TOP_K
    e_flat = top_idx.reshape(n_assign).astype(jnp.int32)
    tok_flat = jnp.repeat(jnp.arange(n_tok, dtype=jnp.int32), TOP_K)
    w_flat = top_w.reshape(n_assign)
    order = jnp.argsort(e_flat)
    e_sorted = e_flat[order]
    counts = jnp.bincount(e_flat, length=N_EXPERTS)
    padded = (counts + EXPERT_BLOCK - 1) // EXPERT_BLOCK * EXPERT_BLOCK
    starts = jnp.cumsum(counts) - counts
    pad_starts = jnp.cumsum(padded) - padded
    dest = pad_starts[e_sorted] + jnp.arange(n_assign, dtype=jnp.int32) - starts[e_sorted]
    n_blocks = -(-(n_assign + N_EXPERTS * (EXPERT_BLOCK - 1)) // EXPERT_BLOCK)
    n_rows = n_blocks * EXPERT_BLOCK
    row_tok = jnp.full((n_rows,), n_tok, jnp.int32).at[dest].set(tok_flat[order])
    row_w = jnp.zeros((n_rows,), jnp.float32).at[dest].set(w_flat[order])
    block_start = jnp.arange(n_blocks, dtype=jnp.int32) * EXPERT_BLOCK
    block_expert = jnp.minimum(jnp.searchsorted(pad_starts + padded, block_start, side='right'),
                               N_EXPERTS - 1).astype(jnp.int32)
    h_pad = jnp.concatenate([h, jnp.zeros((1, d), h.dtype)], axis=0)
    xb = h_pad[row_tok].reshape(n_blocks, EXPERT_BLOCK, d)

    def expert_block(args):
        xblk, e = args
        gu = xblk @ w_up[e] + b_up[e]
        x_glu = jnp.minimum(gu[:, 0::2], SWIGLU_LIMIT)
        x_lin = jnp.clip(gu[:, 1::2], -SWIGLU_LIMIT, SWIGLU_LIMIT)
        act = x_glu * jax.nn.sigmoid(SWIGLU_ALPHA * x_glu) * (x_lin + 1.0)
        return act @ w_down[e] + b_down[e]

    yb = lax.map(expert_block, (xb, block_expert))
    y_rows = yb.reshape(n_rows, d) * row_w[:, None].astype(yb.dtype)
    return jax.ops.segment_sum(y_rows, row_tok, num_segments=n_tok + 1)[:n_tok].astype(h.dtype)

def setup_inputs(seed: int = 0) -> dict:
    key = jax.random.key(seed)
    ks = jax.random.split(key, 22)

    def dense(k, shape, fan_in):
        return jax.random.normal(k, shape, jnp.float32) * (fan_in ** -0.5)

    def gain(k, shape):
        return 1.0 + 0.05 * jax.random.normal(k, shape, jnp.float32)

    def small(k, shape):
        return 0.01 * jax.random.normal(k, shape, jnp.float32)

    offsets = jax.random.randint(ks[1], (BATCH, 1), 0, 1024, dtype=jnp.int32)
    positions = jnp.arange(SEQ, dtype=jnp.int32)[None, :] + offsets
    return {
        "x": jax.random.normal(ks[0], (BATCH, SEQ, D_MODEL), jnp.float32),
        "positions": positions,
        "g_mix": gain(ks[2], (DEPTH, D_MODEL)),
        "w_in": dense(ks[3], (DEPTH, D_MODEL, IN_WIDTH), D_MODEL),
        "g_cq": gain(ks[4], (DEPTH, MLA_Q_LORA)),
        "w_uq": dense(ks[5], (DEPTH, MLA_Q_LORA, MLA_HEADS * MLA_QK_DIM), MLA_Q_LORA),
        "g_ckv": gain(ks[6], (DEPTH, MLA_KV_LORA)),
        "w_ukv": dense(ks[7], (DEPTH, MLA_KV_LORA, MLA_HEADS * (MLA_NOPE_DIM + MLA_V_DIM)), MLA_KV_LORA),
        "g_qnorm": gain(ks[8], (DEPTH, MLA_QK_DIM)),
        "g_knorm": gain(ks[9], (DEPTH, MLA_QK_DIM)),
        "w_o_sb": dense(ks[10], (DEPTH, SB_WIDTH, D_MODEL), SB_WIDTH),
        "w_o_mla": dense(ks[11], (DEPTH, MLA_WIDTH, D_MODEL), MLA_WIDTH),
        "w_out": dense(ks[12], (DEPTH, D_MODEL, D_MODEL), D_MODEL),
        "g_ffn": gain(ks[13], (DEPTH, D_MODEL)),
        "w_router": dense(ks[14], (DEPTH, D_MODEL, N_EXPERTS), D_MODEL),
        "b_router": small(ks[15], (DEPTH, N_EXPERTS)),
        "w_up": dense(ks[16], (DEPTH, N_EXPERTS, D_MODEL, 2 * D_FF), D_MODEL),
        "b_up": small(ks[17], (DEPTH, N_EXPERTS, 2 * D_FF)),
        "w_down": dense(ks[18], (DEPTH, N_EXPERTS, D_FF, D_MODEL), D_FF),
        "b_down": small(ks[19], (DEPTH, N_EXPERTS, D_MODEL)),
    }

def reference(x, positions, g_mix, w_in, g_cq, w_uq, g_ckv, w_ukv, g_qnorm, g_knorm,
              w_o_sb, w_o_mla, w_out, g_ffn, w_router, b_router, w_up, b_up, w_down, b_down):
    bsz, seq, d = x.shape
    for l in range(DEPTH):
        h = rmsnorm(x, g_mix[l])
        proj = h @ w_in[l]
        sb_q, sb_k, sb_v, c_q, c_kv, k_rope, gate_sb, gate_mla = jnp.split(proj, IN_SPLITS, axis=-1)

        def sb_heads(t):
            return t.reshape(bsz, seq, SB_HEADS, SB_HEAD_DIM).transpose(0, 2, 1, 3)
        o_sb = stick_breaking_attention(sb_heads(sb_q), sb_heads(sb_k), sb_heads(sb_v))
        o_sb = o_sb.transpose(0, 2, 1, 3).reshape(bsz, seq, SB_WIDTH)

        q = (rmsnorm(c_q, g_cq[l]) @ w_uq[l]).reshape(bsz, seq, MLA_HEADS, MLA_QK_DIM)
        q = rmsnorm(q, g_qnorm[l])
        q = jnp.concatenate([q[..., :MLA_NOPE_DIM], apply_rope(q[..., MLA_NOPE_DIM:], positions)], axis=-1)
        kv = (rmsnorm(c_kv, g_ckv[l]) @ w_ukv[l]).reshape(bsz, seq, MLA_HEADS, MLA_NOPE_DIM + MLA_V_DIM)
        k_nope, v = kv[..., :MLA_NOPE_DIM], kv[..., MLA_NOPE_DIM:]
        k_r = jnp.broadcast_to(k_rope[:, :, None, :], (bsz, seq, MLA_HEADS, MLA_ROPE_DIM))
        k = rmsnorm(jnp.concatenate([k_nope, k_r], axis=-1), g_knorm[l])
        k = jnp.concatenate([k[..., :MLA_NOPE_DIM], apply_rope(k[..., MLA_NOPE_DIM:], positions)], axis=-1)
        o_mla = chunk_causal_softmax_attention(q.transpose(0, 2, 1, 3), k.transpose(0, 2, 1, 3),
                                               v.transpose(0, 2, 1, 3))
        o_mla = o_mla.transpose(0, 2, 1, 3).reshape(bsz, seq, MLA_WIDTH)

        mixed = (jax.nn.sigmoid(gate_sb) * (o_sb @ w_o_sb[l])
                 + jax.nn.sigmoid(gate_mla) * (o_mla @ w_o_mla[l]))
        x = x + mixed @ w_out[l]

        h2 = rmsnorm(x, g_ffn[l]).reshape(bsz * seq, d)
        y = moe_ffn(h2, w_router[l], b_router[l], w_up[l], b_up[l], w_down[l], b_down[l])
        x = x + y.reshape(bsz, seq, d)
    return x


_drawn_inputs = setup_inputs


def setup_inputs(seed=0):
    import zlib

    import numpy as np

    out = dict(_drawn_inputs(seed))
    spreads = {}
    factors = {'g_qnorm': 3.212, 'g_knorm': 3.319, 'b_up': 8.0, 'b_down': 8.0}
    for name, (base, spread) in spreads.items():
        noise = np.random.default_rng([zlib.crc32(name.encode()), seed]).standard_normal(out[name].shape)
        drawn = base * np.exp(spread * noise) if base else spread * noise
        out[name] = __import__('jax').numpy.asarray(drawn.astype(out[name].dtype))
    for name, factor in factors.items():
        out[name] = (out[name] * factor).astype(out[name].dtype)
    return out
```

```python
from contextlib import ExitStack
import math

import numpy as np
from concourse import mybir
from concourse.bass import ds

ALU = mybir.AluOpType
ACT = mybir.ActivationFunctionType
AX = mybir.AxisListType
F32 = mybir.dt.float32
F32R = mybir.dt.float32r
I32 = mybir.dt.int32

P = 128
D = 1024
KD = D // P
SEQ = 256
NT = SEQ // P
EPS = 1e-6
HEADS = 8
DH = 64
SBW = HEADS * DH
ROPE = 32
HALF = ROPE // 2
DQK = DH + ROPE
CQ, CKV = 384, 256
QT, KVT = CQ // P, CKV // P
THETA = 10000.0
CHUNK = 64
TOPK = 4
NE = 32
FF = 1024
LIMIT = 7.0
ALPHA = 1.702
NEG = -1.0e30

C_Q, C_K, C_V = 0, SBW, 2 * SBW
C_CQ = 3 * SBW
C_CKV = C_CQ + CQ
C_KR = C_CKV + CKV
C_GA = C_KR + ROPE
C_GB = C_GA + D

SLOTS = 12
SLOT = 2048
PER_EXPERT = 12
CAP = 64
COLS = 64
ROUNDS = SEQ // CAP
MAX_EXTRA = SEQ * TOPK // CAP
RING = 6
STAGE = 2

BIG_RANK = 3.0e38
TWO_PI_1 = 6.28125
TWO_PI_2 = float(np.float32(0.0019350051879882812))
TWO_PI_3 = float(2 * math.pi - TWO_PI_1 - TWO_PI_2)
ROUNDER = 12582912.0


def plan_chunks():
    return ([("lat", i) for i in range(3)] + [("uq", i) for i in range(2)] + [("ukv", 0)]
            + [("qkv", i) for i in range(6)] + [("gate", i) for i in range(8)] + [("bup", 0)]
            + [("osb", 0), ("omla", 0), ("osb", 1), ("omla", 1)]
            + [("wout", i) for i in range(4)] + [("router", 0), ("bdown", 0)])


def encoder_block(nc, x, positions, g_mix, w_in, g_cq, w_uq, g_ckv, w_ukv, g_qnorm, g_knorm, w_o_sb,
                  w_o_mla, w_out, g_ffn, w_router, b_router, w_up, b_up, w_down, b_down, out):
    chunks = plan_chunks()
    NCH = len(chunks)
    number = {c: n for n, c in enumerate(chunks)}

    ctx = ExitStack()
    att = ExitStack()

    def sb(name, shape, dt=F32, stack=ctx):
        return stack.enter_context(nc.sbuf_tensor(name, shape, dt))

    def sem(name):
        return ctx.enter_context(nc.semaphore(name))

    class VisitSemaphores:
        pass

    def visit_semaphores(tag, spare):
        q = VisitSemaphores()
        q.spare = spare
        q.hi, q.lo = sem(tag + "_w_hi"), sem(tag + "_w_lo")
        q.w_used = sem(tag + "_w_used")
        q.p_read = sem(tag + "_product_read")
        q.ht_hi, q.ht_lo = sem(tag + "_ht_hi"), sem(tag + "_ht_lo")
        q.pick, q.put = sem(tag + "_pick"), sem(tag + "_put")
        q.gathered, q.put_turned, q.putT = sem(tag + "_gathered"), sem(tag + "_put_turned"), sem(tag + "_putT")
        q.gu_turned, q.u = sem(tag + "_gu_turned"), sem(tag + "_u")
        q.glu, q.lin, q.gated = sem(tag + "_glu"), sem(tag + "_lin"), sem(tag + "_gated")
        q.sig, q.act = sem(tag + "_sig"), sem(tag + "_act")
        q.act_hi, q.act_lo = sem(tag + "_act_hi"), sem(tag + "_act_lo")
        q.summed = sem(tag + "_summed")
        return q

    with ctx:
        ps = ctx.enter_context(nc.psum_tensor("ps", [P, 8, 512], F32))

        lo_parts = ExitStack()
        slot_lo = [sb(f"slot{s}_lo", [P, SLOT], F32R, lo_parts) for s in range(SLOTS)]
        lo_parts.close()
        slot = [sb(f"slot{s}", [P, SLOT]) for s in range(SLOTS)]
        ident = sb("ident", [P, P])
        ones = sb("ones", [P, P])
        before = sb("before", [P, P])
        xin = sb("xin", [P, NT, D])
        hn = sb("hn", [P, NT, D])
        slot_no = sb("slot_no", [P, 2, COLS])
        fold = sb("fold", [P, COLS])
        b_upT = sb("b_upT", [P, 2, 2, 4, NE])
        rank_in = sb("rank_in", [P, NT, ROUNDS, NE])
        gate_w = sb("gate_w", [P, NT, NE])
        count = sb("count", [P, NE])
        visit_f = sb("visit_f", [1, 3, MAX_EXTRA])
        visit_i = sb("visit_i", [1, 3, MAX_EXTRA], I32)
        var, inv, half_vy = sb("var", [P, 40]), sb("inv", [P, 40]), sb("half_vy", [P, 40])
        br_bc = sb("br_bc", [P, NE])

        def sa(name, shape, dt=F32):
            return sb(name, shape, dt, att)

        hT = sa("hT", [P, KD, SEQ])
        qT = sa("qT", [P, 4, SEQ])
        kT = sa("kT", [P, 4, SEQ])
        v_sb = sa("v_sb", [P, NT, SBW])
        gates = sa("gates", [P, KD, 2, SEQ])
        q_mla = sa("q_mla", [P, NT, HEADS, DQK])
        kv = sa("kv", [P, NT, HEADS, 2 * DH])
        qkT = sa("qkT", [P, HEADS, 2, SEQ])
        stick = sa("stick", [P, 2, 384])
        stay = sa("stay", [P, 2, 384])
        prob = sa("prob", [P, 2, 384])
        probT = sa("probT", [P, 2, 384])
        neg_from = sa("neg_from", [P, P])
        neg_ones = sa("neg_ones", [P, P])
        cap_mask = sa("cap_mask", [P, 384])
        row_lo = sa("row_lo", [P, P])
        col_hi = sa("col_hi", [P, P])
        gains = sa("gains", [KD + QT + KVT, P])
        gT = sa("gT", [P, KD + QT + KVT])
        gq_bc = sa("gq_bc", [P, DQK])
        gk_bc = sa("gk_bc", [P, DQK])
        inv_freq = sa("inv_freq", [P, HALF])
        pos_i = sa("pos_i", [P, NT], I32)
        pos_f = sa("pos_f", [P, NT])
        ang = sa("ang", [P, NT, HALF])
        turns = sa("turns", [P, 2, NT, HALF])
        red = sa("red", [P, 2, NT, HALF])
        cs = sa("cs", [P, 2, NT, HALF])
        kr = sa("kr", [P, NT, ROPE])
        krr = sa("krr", [P, NT, ROPE])
        st = sa("st", [P, 160])
        lg = sa("lg", [P, NT, NE + 4])
        marked = sa("marked", [P, NT, NE + 4])
        top = sa("top", [P, NT, 8])
        key = sa("key", [P, NT, 8])
        chosen = sa("chosen", [P, NT, NE])
        expl = sa("expl", [P, NT, NE])
        o_sb = q_mla[:, :, :, :].rearrange("p t h d -> p (t h d)")[:, 0:4 * SEQ].rearrange("p (j s) -> p j s", j=4)
        o_mla_sb = hn[:, 0, :].rearrange("p (j s) -> p j s", j=4)
        k_mla = hn[:, :, 0:HEADS * DQK].rearrange("p t (h d) -> p t h d", h=HEADS)
        gates_flat = gates[:, :, :, :].rearrange("p k a s -> p (k a) s")
        cT, sqT = gates_flat[:, 0:5, :], gates_flat[:, 5:10, :]
        g_ffn_bc = kv[:, 0, :, :].rearrange("p h d -> p (h d)")
        h2T = hT
        att_bytes = nc.sbuf_bytes_remaining
        att.close()

        w_hi = sb("w_hi", [P, RING, SLOT], F32R)
        hTs = sb("hTs", [P, KD, 2, COLS], F32R)
        actT = sb("actT", [P, 8, 2, COLS], F32R)
        gu_sb = sb("gu_sb", [P, 2, 1024])
        y_sb = sb("y_sb", [P, D])
        pick = sb("pick", [P, NT, COLS])
        put = sb("put", [P, NT, 2, COLS])
        putT = sb("putT", [P, SEQ])
        u = sb("u", [P, 2, 4, COLS])
        gated = sb("gated", [P, 4, COLS])
        sig = sb("sig", [P, 4, COLS])
        act32 = sb("act32", [P, 4, COLS])
        gate_wT = sb("gate_wT", [NE, SEQ])
        more = sb("more", [1, 3, (ROUNDS - 1) * NE])
        codes = sb("codes", [1, 2, (ROUNDS - 1) * NE])
        found = sb("found", [1, (ROUNDS - 1) * NE])

        loaded = [sem(f"slot{s}_loaded") for s in range(SLOTS)]
        x_in, small_in, gffn_in, out_done = sem("x_in"), sem("small_in"), sem("gffn_in"), sem("out_done")
        consts = sem("consts")
        filled = sem("filled")
        emptied = [sem(f"bank{b}_emptied") for b in range(2)]
        dve_s, act_s = sem("dve_steps"), sem("act_steps")
        ssq_s, xhat_s, gt_ps, gt_s = sem("sumsq"), sem("xhat"), sem("gains_turned"), sem("gains_ready")
        lat_ss, lat_rs = sem("latent_sumsq"), sem("latent_rstd")
        red_s, cs_s = sem("angles_reduced"), sem("sincos")
        mla_q_s, mla_k_s = sem("mla_q_ready"), sem("mla_k_ready")
        turn_s = sem("qk_turned")
        turn_e = [sem(f"qk_bank{b}_emptied") for b in range(4)]
        z_s, bound_s, ln_s, sp_s, r_s, cap_s, a_s, av_s = (sem(n) for n in (
            "sb_scores", "sb_bounded", "sb_log", "sb_softplus", "sb_logweights", "sb_capped", "sb_weights", "sb_pv"))
        s_s, max_s, p_s, pn_s, pt_s, pte_s, mv_s = (sem(n) for n in (
            "mla_scores", "mla_max", "mla_exp", "mla_probs", "mla_probs_turned", "mla_probsT", "mla_pv"))
        oe_s = sem("heads_out")
        recip_s, root_s = sem("rms_recip"), sem("rms_root")
        mix_s, x1_s, h2_s = sem("mixed"), sem("x1_ready"), sem("h2_ready")
        top_s, expl_s, chosen_s, rank_s, count_s, wt_s = (sem(n) for n in (
            "logits_shifted", "logits_exp", "chosen_ready", "ranks_ready", "counts_ready", "gate_w_turned"))
        acc_s, pool_s, visits_s, out_s = sem("bias_summed"), sem("pool_steps"), sem("visits_ready"), sem("out_ready")
        gw_s, sum_in = sem("gate_w_ready"), sem("x1_squares")
        main = visit_semaphores("v", 0)
        extra = visit_semaphores("x", 1)
        again = [sem(f"chunk{c}_again") for c in range(PER_EXPERT)]

        w_upv = w_up.rearrange("l e (k p) n -> (l e) p k n", p=P)
        w_downv = w_down.rearrange("l e (k p) n -> (l e) p k n", p=P)

        xv = x.rearrange("b (t p) d -> p (b t) d", p=P)
        ov = out.rearrange("b (t p) d -> p (b t) d", p=P)
        posv = positions.rearrange("b (t p) -> p (b t)", p=P)
        w_inv = w_in.rearrange("l (k p) n -> p (l k) n", p=P)
        w_uqv = w_uq.rearrange("l (k p) n -> p (l k) n", p=P)
        w_ukvv = w_ukv.rearrange("l (k p) n -> p (l k) n", p=P)
        w_osv = w_o_sb.rearrange("l (k p) n -> p (l k) n", p=P)
        w_omv = w_o_mla.rearrange("l (k p) n -> p (l k) n", p=P)
        w_outv = w_out.rearrange("l (k p) n -> p (l k) n", p=P)
        w_rv = w_router.rearrange("l (k p) n -> p (l k) n", p=P)

        def chunk(c):
            name, i = c
            t = slot[number[c] % SLOTS]

            def view(k, n):
                return t[:, 0:k * n].rearrange("p (k n) -> p k n", k=k)
            if name == "lat":
                n = 256 if i < 2 else 160
                return view(KD, n), w_inv[:, :, C_CQ + 256 * i:C_CQ + 256 * i + n]
            if name == "uq":
                return view(QT, 384), w_uqv[:, :, 384 * i:384 * i + 384]
            if name == "ukv":
                return view(KVT, 1024), w_ukvv
            if name == "qkv":
                return view(KD, 256), w_inv[:, :, 256 * i:256 * i + 256]
            if name == "gate":
                c0 = (C_GA, C_GB)[i % 2] + 256 * (i // 2)
                return view(KD, 256), w_inv[:, :, c0:c0 + 256]
            if name == "osb":
                return view(4, 512), w_osv[:, :, 512 * i:512 * i + 512]
            if name == "omla":
                return view(4, 512), w_omv[:, :, 512 * i:512 * i + 512]
            if name == "wout":
                return view(KD, 256), w_outv[:, :, 256 * i:256 * i + 256]
            if name == "router":
                return view(KD, NE), w_rv
            if name == "bup":
                return t[0:NE, 0:2 * FF], b_up.rearrange("l e n -> (l e) n")
            return t[0:NE, 0:D], b_down.rearrange("l e n -> (l e) n")

        FILL_X = 0
        FILL_LAT = 4
        FILL_UP = 7
        FILL_QKV = 15
        FILL_GATE = 21
        FILL_BUP = 29
        FILL_MIX = 30
        FILL_OUT = 38
        FILL_H2 = 42
        FILL_LOGIT = 46
        FILL_RANK = 47
        FILL_WT = 48

        def last_fill(c):
            name, i = c
            return {"lat": FILL_LAT + i, "uq": FILL_UP + 2 * i + 1, "ukv": FILL_UP + 7, "qkv": FILL_QKV + i,
                    "gate": FILL_GATE + i, "bup": FILL_BUP, "osb": FILL_MIX + 4 * i + 3,
                    "omla": FILL_MIX + 4 * i + 3, "wout": FILL_OUT + i, "router": FILL_LOGIT,
                    }[name]

        def bank(n):
            return ps[:, n % 2, :]

        def up_piece(m):
            b = bank(FILL_UP + m)
            if m < 4:
                i, t = m // 2, m % 2
                return (q_mla[:, t, 4 * i:4 * i + 4, :], b[:, 0:384].rearrange("p (h d) -> p h d", h=4),
                        inv[:, 2 + t:3 + t])
            t, i = (m - 4) // 2, m % 2
            return (kv[:, t, 4 * i:4 * i + 4, :], b.rearrange("p (h d) -> p h d", h=4), inv[:, 4 + t:5 + t])


        PASSES = ("a", "b", "d")

        def expert_slot(kind, k, last=False):
            return (NCH + 4 * PASSES.index("a" if last else kind) + k) % SLOTS

        def load_chunk(sp, kind, k, e, s, signal):
            dst = slot[s][:, :].rearrange("p (k n) -> p k n", k=2)
            if kind == "d":
                src = w_downv[e, :, 2 * k:2 * k + 2, :]
            else:
                c0 = 1024 * (kind == "b")
                src = w_upv[e, :, 2 * k:2 * k + 2, c0:c0 + 1024]
            sp.dma_start(dst, src).then_inc(signal, 16)

        def split_hi(act, q, s, n, at, arrived, times):
            act.wait_ge(arrived, 16 * times)
            free(act, q.w_used, n - RING + 1, q.spare * RING)
            act.activation(w_hi[:, at, :], slot[s][:, :], ACT.Copy).then_inc(q.hi, 1)

        def split_lo(dve, q, s, n, at, arrived, times):
            dve.wait_ge(arrived, 16 * times)
            dve.wait_ge(q.hi, n + 1)
            dve.tensor_tensor(slot_lo[s][:, :], slot[s][:, :], w_hi[:, at, :].bitcast(F32),
                              ALU.subtract).then_inc(q.lo, 1)

        def free(eng, s, n, spare):
            if isinstance(n, int) and n + spare <= 0:
                return
            eng.wait_ge(s, n + spare)

        def gather(pe, q, v, puts):
            pe.wait_ge(q.pick, v + 1)
            free(pe, q.ht_hi, v, q.spare)
            free(pe, q.ht_lo, v, q.spare)
            free(pe, q.putT, puts, q.spare)
            for k in range(KD):
                for t in range(NT):
                    mm = pe.matmul(ps[:, 2, COLS * k:COLS * k + COLS], hn[:, t, P * k:P * k + P], pick[:, t, :],
                                   start=t == 0, stop=t == NT - 1)
            mm.then_inc(q.gathered, 1)

        def product(pe, q, kind, v, first, at, pn, last=False):
            free(pe, q.p_read, pn, q.spare)
            if kind == "d":
                x2 = actT
            else:
                x2 = hTs
                pe.wait_ge(q.ht_hi, v + 1 + q.spare)
                pe.wait_ge(q.ht_lo, v + 1 + q.spare)
            for k in range(4):
                if kind == "d" and k % 2 == 0:
                    pe.wait_ge(q.act_hi, 2 * v + k // 2 + 1)
                    pe.wait_ge(q.act_lo, 2 * v + k // 2 + 1)
                pe.wait_ge(q.hi, first + k + 1)
                for i in range(2):
                    lhs = x2[:, 2 * k + i, :, :].rearrange("p a c -> p (a c)")
                    for part, w in enumerate((w_hi[:, (at + k) % RING, :], slot_lo[expert_slot(kind, k, last)])):
                        if i == 0 and part == 1:
                            pe.wait_ge(q.lo, first + k + 1)
                        for b in range(2):
                            c0 = 1024 * i + 512 * b
                            mm = pe.matmul(ps[:, b, :], lhs, w[:, c0:c0 + 512],
                                           start=k + i + part == 0, stop=k + i + part == 5)
                mm.then_inc(q.w_used, 1)

        def turn_up(pe, q, half, v, pn):
            pe.wait_ge(q.p_read, pn + 1 + q.spare)
            free(pe, q.u, 2 * v + half, q.spare)
            for g in range(2):
                for j in range(4):
                    c0 = 2 * P * j + g
                    o = COLS * (4 * g + j)
                    mm = pe.matmul(ps[:, 3, o:o + COLS], gu_sb[:, half, c0:c0 + 2 * P - 1:2], fold[:, :],
                                   start=True, stop=True)
            mm.then_inc(q.gu_turned, 1)

        def turn_put(pe, q, v, gathers):
            pe.wait_ge(q.put, v + 1)
            pe.wait_ge(q.ht_hi, gathers + q.spare)
            pe.wait_ge(q.ht_lo, gathers + q.spare)
            free(pe, q.putT, v, q.spare)
            for t in range(NT):
                mm = pe.transpose(ps[:, 2, P * t:P * t + P], put[:, t, :, :].rearrange("p a c -> p (a c)"), ident[:, :])
            mm.then_inc(q.put_turned, 1)

        def add_visit(pe, q, v, pn):
            pe.wait_ge(q.p_read, pn + 1 + q.spare)
            pe.wait_ge(q.putT, v + 1 + q.spare)
            for t in range(NT):
                for b in range(2):
                    mm = pe.matmul(ps[:, 4 + 2 * t + b, :], putT[:, P * t:P * t + P], y_sb[:, 512 * b:512 * b + 512],
                                   start=False, stop=False, skip_group_check=True)
            mm.then_inc(q.summed, 1)

        def copy_up(act, q, half, v, last):
            act.wait_ge(q.w_used, last + q.spare * RING)
            free(act, q.gu_turned, 2 * v + half - 1, 2 * q.spare)
            act.activation(gu_sb[:, half, :], ps[:, 0:2, :].rearrange("p b n -> p (b n)"), ACT.Copy).then_inc(q.p_read, 1)

        def copy_down(act, q, v, last):
            act.wait_ge(q.w_used, last + q.spare * RING)
            free(act, q.summed, v, q.spare)
            act.activation(y_sb[:, :], ps[:, 0:2, :].rearrange("p b n -> p (b n)"), ACT.Copy).then_inc(q.p_read, 1)

        def copy_put(act, q, v):
            act.wait_ge(q.put_turned, v + 1 + q.spare)
            free(act, q.summed, v, q.spare)
            act.activation(putT[:, :], ps[:, 2, 0:SEQ], ACT.Copy).then_inc(q.putT, 1)

        def tokens_hi(act, q, v):
            act.wait_ge(q.gathered, v + 1 + q.spare)
            act.activation(hTs[:, :, 0, :], ps[:, 2, :].rearrange("p (k c) -> p k c", k=KD), ACT.Copy
                           ).then_inc(q.ht_hi, 1)

        def sigmoid(act, q, m):
            act.wait_ge(q.glu, m + 1)
            act.activation(sig[:, :, :], u[:, 0, :, :], ACT.Sigmoid, scale=ALPHA).then_inc(q.sig, 1)

        def act_hi(act, q, half, m):
            act.wait_ge(q.act, m + 1)
            act.activation(actT[:, 4 * half:4 * half + 4, 0, :], act32[:, :, :], ACT.Copy).then_inc(q.act_hi, 1)

        def build_pick(dve, q, v, column):
            free(dve, q.gathered, v, q.spare)
            for t in range(NT):
                ins = dve.tensor_scalar(pick[:, t, :], slot_no[:, 0, :], rank_v[:, t, ds(column, 1)], None, ALU.is_equal)
            ins.then_inc(q.pick, 1)

        def build_put(dve, q, v, column, e):
            free(dve, q.put_turned, v, q.spare)
            for t in range(NT):
                ins = dve.tensor_scalar(put[:, t, :, :], slot_no[:, :, :], rank_v[:, t, ds(column, 1)],
                                        gate_w[:, t, ds(e, 1)], ALU.is_equal, ALU.mult)
            ins.then_inc(q.put, 1)

        def tokens_lo(dve, q, v):
            dve.wait_ge(q.ht_hi, v + 1 + q.spare)
            dve.tensor_tensor(hTs[:, :, 1, :], ps[:, 2, :].rearrange("p (k c) -> p k c", k=KD),
                              hTs[:, :, 0, :].bitcast(F32), ALU.subtract).then_inc(q.ht_lo, 1)

        def gate_up(dve, q, half, m, e):
            dve.wait_ge(q.gu_turned, m + 1 + 2 * q.spare)
            bias = b_upT[:, half, :, :, ds(e, 1)].to_broadcast([P, 2, 4, COLS])
            dve.tensor_tensor(u[:, :, :, :], ps[:, 3, :].rearrange("p (g j c) -> p g j c", g=2, j=4), bias, ALU.add
                              ).then_inc(q.u, 1)
            dve.wait_ge(q.u, m + 1 + q.spare)
            dve.tensor_scalar(u[:, 0, :, :], u[:, 0, :, :], LIMIT, None, ALU.min).then_inc(q.glu, 1)
            dve.tensor_scalar(u[:, 1, :, :], u[:, 1, :, :], LIMIT, -LIMIT, ALU.min, ALU.max).then_inc(q.lin, 1)
            dve.wait_ge(q.glu, m + 1)
            dve.wait_ge(q.lin, m + 1)
            dve.scalar_tensor_tensor(out=gated[:, :, :], in0=u[:, 1, :, :], scalar=1.0, in1=u[:, 0, :, :],
                                     op0=ALU.add, op1=ALU.mult).then_inc(q.gated, 1)

        def times_sigmoid(dve, q, m):
            dve.wait_ge(q.sig, m + 1)
            dve.wait_ge(q.gated, m + 1)
            dve.tensor_tensor(act32[:, :, :], gated[:, :, :], sig[:, :, :], ALU.mult).then_inc(q.act, 1)

        def act_lo(dve, q, half, m):
            dve.wait_ge(q.act_hi, m + 1)
            dve.tensor_tensor(actT[:, 4 * half:4 * half + 4, 1, :], act32[:, :, :],
                              actT[:, 4 * half:4 * half + 4, 0, :].bitcast(F32), ALU.subtract).then_inc(q.act_lo, 1)

        rank_v = rank_in[:, :, :, :].rearrange("p t r e -> p t (r e)")
        PASS_AT = {"a": 0, "b": 4, "d": 8}

        def first_chunk(i, kind):
            if isinstance(i, int) and i == 0:
                return PASS_AT[kind]
            if isinstance(i, int) and i == NE:
                return 12 * NE - 4
            return 12 * i - 4 + PASS_AT[kind]

        def place(i, kind):
            return (PASS_AT[kind] - 4 * (not (isinstance(i, int) and i == 0))
                    - 8 * (isinstance(i, int) and i == NE)) % RING

        def pass_number(i, kind):
            if isinstance(i, int) and i == 0:
                return PASS_AT[kind] // 4
            if isinstance(i, int) and i == NE:
                return 3 * NE - 1
            return 3 * i - 1 + PASS_AT[kind] // 4

        def arrival(i, kind, k):
            last = isinstance(i, int) and i == NE
            s = expert_slot(kind, k, last)
            before_experts = len(range(s, NCH, SLOTS))
            return s, loaded[s], before_experts + (NE + 1 if last else i if kind == "d" else i + 1)

        def pe_body(pe, q, i, cur, prev, prev2, nxt):
            if cur:
                product(pe, q, "a", i, first_chunk(i, "a"), place(i, "a"), pass_number(i, "a"))
            if prev:
                turn_up(pe, q, 1, i - 1, pass_number(i - 1, "b"))
            if prev2:
                add_visit(pe, q, i - 2, pass_number(i - 1, "d"))
            if cur:
                product(pe, q, "b", i, first_chunk(i, "b"), place(i, "b"), pass_number(i, "b"))
            if nxt:
                gather(pe, q, i + 1, i - 1)
            if prev:
                product(pe, q, "d", i - 1, first_chunk(i, "d"), place(i, "d"), pass_number(i, "d"),
                        last=isinstance(i, int) and i == NE)
            if cur:
                turn_up(pe, q, 0, i, pass_number(i, "a"))
            if prev:
                turn_put(pe, q, i - 1, i + 2 if nxt else NE)

        def act_body(act, q, i, cur, prev, prev2, nxt):
            def hi(kind, k):
                s, arrived, times = arrival(i, kind, k)
                split_hi(act, q, s, first_chunk(i, kind) + k, (place(i, kind) + k) % RING, arrived, times)
            if cur:
                hi("a", 0)
                hi("a", 1)
            if prev2:
                copy_down(act, q, i - 2, first_chunk(i - 1, "d") + 4)
                copy_put(act, q, i - 2)
            if cur:
                hi("a", 2)
            if prev:
                sigmoid(act, q, 2 * (i - 1))
            if cur:
                hi("a", 3)
            if prev:
                act_hi(act, q, 0, 2 * (i - 1))
            if cur:
                hi("b", 0)
                hi("b", 1)
                copy_up(act, q, 0, i, first_chunk(i, "a") + 4)
                hi("b", 2)
            if prev:
                sigmoid(act, q, 2 * (i - 1) + 1)
            if cur:
                hi("b", 3)
            if prev:
                act_hi(act, q, 1, 2 * (i - 1) + 1)
                hi("d", 0)
                hi("d", 1)
                hi("d", 2)
            if cur:
                copy_up(act, q, 1, i, first_chunk(i, "b") + 4)
            if nxt:
                tokens_hi(act, q, i + 1)
            if prev:
                hi("d", 3)

        def dve_body(dve, q, i, cur, prev, prev2, nxt):
            def lo(kind, k):
                s, arrived, times = arrival(i, kind, k)
                split_lo(dve, q, s, first_chunk(i, kind) + k, (place(i, kind) + k) % RING, arrived, times)
            if cur:
                lo("a", 0)
                lo("a", 1)
            if prev:
                gate_up(dve, q, 0, 2 * (i - 1), i - 1)
            if cur:
                lo("a", 2)
            if prev:
                times_sigmoid(dve, q, 2 * (i - 1))
            if cur:
                lo("a", 3)
            if prev:
                act_lo(dve, q, 0, 2 * (i - 1))
            if cur:
                lo("b", 0)
                lo("b", 1)
            if prev:
                gate_up(dve, q, 1, 2 * (i - 1) + 1, i - 1)
            if cur:
                lo("b", 2)
            if prev:
                times_sigmoid(dve, q, 2 * (i - 1) + 1)
            if nxt:
                build_pick(dve, q, i + 1, i + 1)
            if cur:
                lo("b", 3)
            if prev:
                act_lo(dve, q, 1, 2 * (i - 1) + 1)
                lo("d", 0)
                build_put(dve, q, i - 1, i - 1, i - 1)
                lo("d", 1)
                lo("d", 2)
            if nxt:
                tokens_lo(dve, q, i + 1)
            if prev:
                lo("d", 3)

        def bodies(eng, body):
            body(eng, main, 0, True, False, False, True)
            body(eng, main, 1, True, True, False, True)
            with eng.Fori(2, NE - 1) as i:
                body(eng, main, i, True, True, True, True)
            body(eng, main, NE - 1, True, True, True, False)
            body(eng, main, NE, False, True, True, False)

        def further(eng, start, body):
            eng.wait_ge(visits_s, 1)
            n = eng.value_load(visit_i[0:1, 2, 0:1], min_val=0, max_val=MAX_EXTRA)
            with eng.If(n > 0):
                start()
                with eng.Fori(0, n) as j:
                    column = eng.value_load(visit_i[0:1, 0, ds(j, 1)], min_val=0, max_val=ROUNDS * NE - 1)
                    e = eng.value_load(visit_i[0:1, 1, ds(j, 1)], min_val=0, max_val=NE - 1)
                    body(j, column, e)
            return n

        block = ctx.enter_context(nc.Block())

        @block.sync
        def _(sp):
            def leave(sp, n):
                if n - SLOTS >= NCH - 1:
                    sp.wait_ge(acc_s, 1)
                elif n >= SLOTS:
                    sp.wait_ge(filled, last_fill(chunks[n - SLOTS]) + 1)

            for t in range(NT):
                sp.dma_start(xin[:, t, :], xv[:, t, :]).then_inc(x_in, 16)
            for n, c in enumerate(chunks):
                leave(sp, n)
                dst, src = chunk(c)
                sp.dma_start(dst, src).then_inc(loaded[n % SLOTS], 16)
            for kind in ("a", "b"):
                for k in range(4):
                    leave(sp, NCH + 4 * PASSES.index(kind) + k)
                    s, arrived, _ = arrival(0, kind, k)
                    load_chunk(sp, kind, k, 0, s, arrived)

            def body(i, kinds, before_kind=None):
                for kind in kinds:
                    e = i - 1 if kind == "d" else i
                    for k in range(4):
                        if isinstance(i, int) and i == 1 and kind == "d":
                            leave(sp, NCH + 8 + k)
                        else:
                            sp.wait_ge(main.w_used, first_chunk(i - 1, before_kind or kind) + k + 1)
                        s, arrived, _ = arrival(i, kind, k)
                        load_chunk(sp, kind, k, e, s, arrived)
            body(1, "dab")
            with sp.Fori(2, NE) as i:
                body(i, PASSES)
            body(NE, "d", "a")

            def start():
                sp.wait_ge(main.summed, NE)

            def load_again(j, column, e):
                sp.wait_ge(extra.summed, j + extra.spare)
                for kind in PASSES:
                    for k in range(4):
                        load_chunk(sp, kind, k, e, expert_slot(kind, k), again[4 * PASSES.index(kind) + k])
            further(sp, start, load_again)

            for t in range(NT):
                sp.wait_ge(out_s, 2 * (t + 1))
                sp.dma_start(ov[:, t, :], xin[:, t, :]).then_inc(out_done, 16)
            sp.wait_ge(out_done, 16 * NT)

        @block.gpsimd
        def _(pool):
            def const(ins):
                const.n += 1
                ins.then_inc(consts, 1)
                pool.wait_ge(consts, const.n)
            const.n = 0
            const(pool.memset(ident[:, :], 0.0))
            const(pool.affine_select(out=ident[:, :], in_=ident[:, :], compare_op=ALU.not_equal, fill=1.0,
                                     base=0, pattern=[[-1, P]], channel_multiplier=1))
            const(pool.memset(ones[:, :], 1.0))
            for i in range(HALF):
                f = float(np.float32(THETA) ** (-np.float32(i) / np.float32(HALF)))
                const(pool.memset(inv_freq[:, i:i + 1], f))
            const(pool.memset(neg_ones[:, :], -1.0))
            const(pool.affine_select(out=before[:, :], in_=ones[:, :], compare_op=ALU.is_gt, fill=0.0,
                                     base=0, pattern=[[1, P]], channel_multiplier=-1))
            const(pool.affine_select(out=neg_from[:, :], in_=neg_ones[:, :], compare_op=ALU.is_ge, fill=0.0,
                                     base=0, pattern=[[-1, P]], channel_multiplier=1))
            const(pool.memset(cap_mask[:, :], 0.0))
            for c in (0, 256):
                const(pool.affine_select(out=cap_mask[:, c:c + P], in_=cap_mask[:, c:c + P],
                                         compare_op=ALU.is_gt, fill=-1.0e5, base=0, pattern=[[1, P]],
                                         channel_multiplier=-1))
            const(pool.memset(row_lo[:, :], 0.0))
            const(pool.memset(col_hi[:, :], 0.0))
            const(pool.memset(row_lo[0:1, 0:CHUNK], 1.0))
            const(pool.memset(col_hi[0:1, CHUNK:P], NEG))
            const(pool.memset(fold[:, :], 0.0))
            for b in (0, COLS):
                const(pool.affine_select(out=fold[:, :], in_=fold[:, :], compare_op=ALU.not_equal, fill=1.0,
                                         base=-b, pattern=[[-1, COLS]], channel_multiplier=1))
            const(pool.memset(slot_no[:, :, :], 1.0e6))
            const(pool.iota(slot_no[:, :, 0:CAP], pattern=[[0, 2], [1, CAP]], base=0, channel_multiplier=0,
                            allow_small_or_imprecise_dtypes=True))
            assert const.n == CONSTS, const.n

            steps = [0]

            def link(ins):
                steps[0] += 1
                ins.then_inc(pool_s, 1)
                pool.wait_ge(pool_s, steps[0])

            pool.wait_ge(count_s, 1)
            W = (ROUNDS - 1) * NE
            link(pool.iota(codes[:, 0, :], pattern=[[1, W]], base=NE, channel_multiplier=0,
                           allow_small_or_imprecise_dtypes=True))
            link(pool.iota(codes[:, 1, :], pattern=[[0, ROUNDS - 1], [1, NE]], base=0, channel_multiplier=0,
                           allow_small_or_imprecise_dtypes=True))
            for r in range(1, ROUNDS):
                c = NE * (r - 1)
                last = pool.tensor_scalar(more[:, 0, c:c + NE], count[0:1, :], float(CAP * r), None, ALU.is_gt)
            link(last)
            link(pool.tensor_copy(more[:, 1, :], more[:, 0, :]))
            a, b, shift = 1, 2, 1
            while shift < W:
                pool.tensor_copy(more[:, b, 0:shift], more[:, a, 0:shift])
                link(pool.tensor_tensor(more[:, b, shift:W], more[:, a, shift:W], more[:, a, 0:W - shift], ALU.add))
                a, b, shift = b, a, 2 * shift
            link(pool.tensor_copy(visit_f[:, 2, :], more[:, a, W - 1:W].to_broadcast([1, MAX_EXTRA])))
            link(pool.tensor_tensor(more[:, a, :], more[:, a, :], more[:, 0, :], ALU.mult))
            for v in range(MAX_EXTRA):
                for i in range(2):
                    link(pool.tensor_scalar(found[:, :], more[:, a, :], float(v + 1), None, ALU.is_equal))
                    link(pool.tensor_tensor(found[:, :], found[:, :], codes[:, i, :], ALU.mult))
                    link(pool.tensor_reduce(visit_f[:, i, v:v + 1], found[:, :], AX.XYZWC, ALU.add))
            pool.tensor_copy(visit_i[:, :, :], visit_f[:, :, :]).then_inc(visits_s, 1)

        @block.scalar
        def _(act):
            act.dma_start(gains[0:KD, :], g_mix.rearrange("l (k p) -> (l k) p", p=P)).then_inc(small_in, 16)
            act.dma_start(gains[KD:KD + QT, :], g_cq.rearrange("l (k p) -> (l k) p", p=P)).then_inc(small_in, 16)
            act.dma_start(gains[KD + QT:, :], g_ckv.rearrange("l (k p) -> (l k) p", p=P)).then_inc(small_in, 16)
            act.dma_start(pos_i[:, :], posv, allow_slow_non_contiguous=True).then_inc(small_in, 16)
            act.dma_start(gq_bc[:, :], g_qnorm[0, :].partition_broadcast(P)).then_inc(small_in, 16)
            act.dma_start(gk_bc[:, :], g_knorm[0, :].partition_broadcast(P)).then_inc(small_in, 16)
            act.dma_start(br_bc[:, :], b_router[0, :].partition_broadcast(P)).then_inc(small_in, 16)

            steps = [0]

            def link(ins):
                steps[0] += 1
                ins.then_inc(act_s, 1)
                act.wait_ge(act_s, steps[0])

            def root(i):
                a, b = RMS[i]
                act.wait_ge(recip_s, i + 1)
                act.activation(inv[:, a:b], inv[:, a:b], ACT.Sqrt).then_inc(root_s, 1)

            act.wait_ge(x_in, 16 * NT)
            for t in range(NT):
                act.activation(hn[:, t, :], xin[:, t, :], ACT.Square, accum_out=st[:, t:t + 1]).then_inc(ssq_s, 1)
            root(0)
            act.wait_ge(gt_ps, 1)
            act.activation(gT[:, :], ps[:, 7, 0:KD + QT + KVT], ACT.Copy).then_inc(gt_s, 1)
            act.wait_ge(gt_s, 1)
            for n in (0, 2):
                act.wait_ge(filled, FILL_X + n + 1)
                for i in range(2):
                    k = 2 * n + i
                    last = act.activation(hT[:, k, :], bank(n)[:, SEQ * i:SEQ * i + SEQ], ACT.Copy,
                                          scale=gT[:, k:k + 1])
                last.then_inc(emptied[n % 2], 1)
            for n in range(3):
                b = bank(FILL_LAT + n)
                act.wait_ge(filled, FILL_LAT + n + 1)
                w = 2 if n < 2 else 1
                act.activation(sqT[:, 2 * n:2 * n + w, :], b[:, 0:w * SEQ].rearrange("p (j s) -> p j s", j=w),
                               ACT.Square)
                if n == 2:
                    act.activation(kr[:, :, :], b[:, SEQ:SEQ + NT * ROPE].rearrange("p (t d) -> p t d", t=NT),
                                   ACT.Copy)
                for i in range(w):
                    j = 2 * n + i
                    last = act.activation(cT[:, j, :], b[:, SEQ * i:SEQ * i + SEQ], ACT.Copy,
                                          scale=gT[:, KD + j:KD + j + 1])
                last.then_inc(emptied[(FILL_LAT + n) % 2], 1)
            root(1)
            act.wait_ge(red_s, 1)
            act.activation(cs[:, :, :, :], red[:, :, :, :], ACT.Sin).then_inc(cs_s, 1)
            act.wait_ge(lat_rs, 1)
            for m in range(8):
                n = FILL_UP + m
                if n % 2:
                    continue
                act.wait_ge(filled, n + 1)
                dst, src, scale = up_piece(m)
                act.activation(dst, src, ACT.Copy, scale=scale).then_inc(emptied[0], 1)
            for m in range(6):
                if m in (1, 3):
                    root(m // 2 + 2)
                n = FILL_QKV + m
                act.wait_ge(filled, n + 1)
                src = bank(n).rearrange("p (j s) -> p j s", j=2)
                if m < 2:
                    ins = act.activation(qT[:, 2 * m:2 * m + 2, :], src, ACT.Copy, scale=DH ** -0.5)
                elif m < 4:
                    ins = act.activation(kT[:, 2 * m - 4:2 * m - 2, :], src, ACT.Copy)
                else:
                    ins = act.activation(v_sb[:, :, 256 * (m - 4):256 * (m - 4) + 256], src, ACT.Copy)
                ins.then_inc(emptied[n % 2], 1)
            for h in range(0, HEADS, 2):
                act.wait_ge(turn_s, h + 1)
                act.activation(qkT[0:DQK, h, :, :], ps[0:DQK, TURN[h % 4], :].rearrange("p (a s) -> p a s", a=2),
                               ACT.Copy).then_inc(turn_e[h % 4], 1)
            for h in range(HEADS):
                e = stick[:, h % 2, :]
                act.wait_ge(bound_s, h + 1)
                link(act.activation(e, e, ACT.Exp))
                act.activation(e, e, ACT.Ln, bias=1.0).then_inc(ln_s, 1)
                act.wait_ge(max_s, h + 1)
                act.activation(prob[:, h % 2, 0:P], ps[:, 5, 0:P], ACT.Exp, scale=DQK ** -0.5,
                               bias=st[:, 36:37], accum_out=st[:, 40:41])
                act.activation(prob[:, h % 2, P:384], ps[:, 5, P:384], ACT.Exp, scale=DQK ** -0.5,
                               bias=st[:, 37:38], accum_out=st[:, 41:42]).then_inc(p_s, 1)
                act.wait_ge(cap_s, h + 1)
                act.activation(stay[:, h % 2, :], stay[:, h % 2, :], ACT.Exp).then_inc(a_s, 1)
                act.wait_ge(pt_s, h + 1)
                if h >= 2:
                    act.wait_ge(mv_s, h - 1)
                act.activation(probT[:, h % 2, :], ps[:, 6, 0:384], ACT.Copy).then_inc(pte_s, 1)
                n = FILL_GATE + h
                act.wait_ge(filled, n + 1)
                act.activation(gates[:, h - h % 2:h - h % 2 + 2, h % 2, :], bank(n).rearrange("p (j s) -> p j s", j=2),
                               ACT.Copy).then_inc(emptied[n % 2], 1)
                if h % 2:
                    j = h // 2
                    act.wait_ge(av_s, h + 1)
                    act.wait_ge(mv_s, h + 1)
                    c = SEQ * (j % 2)
                    act.activation(o_sb[:, j, :], ps[:, 4, c:c + SEQ], ACT.Copy)
                    act.activation(o_mla_sb[:, j, :], ps[:, 7, c:c + SEQ], ACT.Copy).then_inc(oe_s, 1)
            act.wait_ge(emptied[0], FILL_BUP // 2 + 1)
            act.wait_ge(emptied[1], FILL_BUP // 2)
            act.activation(gates[:, :, :, :], gates[:, :, :, :], ACT.Sigmoid).then_inc(mix_s, 1)
            n = FILL_BUP
            act.wait_ge(filled, n + 1)
            act.activation(b_upT[:, :, :, :, :], bank(n).rearrange("p (a b j e) -> p a b j e", a=2, b=2, j=4),
                           ACT.Copy).then_inc(emptied[n % 2], 1)
            act.dma_start(g_ffn_bc, g_ffn[0, :].partition_broadcast(P)).then_inc(gffn_in, 16)
            for i in range(4):
                act.wait_ge(x1_s, i + 1)
                for t in range(NT):
                    c = 120 + 4 * t + i
                    last = act.activation(hn[:, t, 256 * i:256 * i + 256], xin[:, t, 256 * i:256 * i + 256],
                                          ACT.Square, accum_out=st[:, c:c + 1])
                last.then_inc(sum_in, 1)
            root(4)
            for n in (FILL_H2, FILL_H2 + 2):
                act.wait_ge(filled, n + 1)
                k = 2 * (n - FILL_H2)
                act.activation(h2T[:, k:k + 2, :], bank(n).rearrange("p (j s) -> p j s", j=2), ACT.Copy
                               ).then_inc(emptied[0], 1)
            act.wait_ge(top_s, 1)
            act.activation(expl[:, :, :], expl[:, :, :], ACT.Exp).then_inc(expl_s, 1)
            tokens_hi(act, main, 0)
            act.wait_ge(filled, FILL_WT + 1)
            act.activation(gate_wT[:, :], ps[0:NE, 0, 0:SEQ], ACT.Copy).then_inc(wt_s, 1)
            bodies(act, act_body)
            copy_down(act, main, NE - 1, first_chunk(NE, "d") + 4)
            copy_put(act, main, NE - 1)

            def start():
                act.sem_inc(extra.p_read, 1)
                act.sem_inc(extra.ht_hi, 1)
                act.sem_inc(extra.putT, 1)

            def visit(j, column, e):
                def hi(kind):
                    for k in range(4):
                        c = 4 * PASSES.index(kind) + k
                        split_hi(act, extra, expert_slot(kind, k), 12 * j + c, c % RING, again[c], j + 1)
                tokens_hi(act, extra, j)
                hi("a")
                copy_up(act, extra, 0, j, 12 * j + 4)
                hi("b")
                sigmoid(act, extra, 2 * j)
                act_hi(act, extra, 0, 2 * j)
                copy_up(act, extra, 1, j, 12 * j + 8)
                sigmoid(act, extra, 2 * j + 1)
                act_hi(act, extra, 1, 2 * j + 1)
                hi("d")
                copy_down(act, extra, j, 12 * j + 12)
                copy_put(act, extra, j)
            further(act, start, visit)

        @block.vector
        def _(dve):
            steps = [0]

            def link(ins):
                steps[0] += 1
                ins.then_inc(dve_s, 1)
                dve.wait_ge(dve_s, steps[0])

            def rstd(i, parts, ready=None):
                a, b = RMS[i]
                v, y, t = var[:, a:b], inv[:, a:b], half_vy[:, a:b]
                for src, width, c0, c1 in parts:
                    last = dve.tensor_scalar(var[:, c0:c1], src, 1.0 / width, EPS, ALU.mult, ALU.add)
                link(last)
                dve.reciprocal(y, v).then_inc(recip_s, 1)
                dve.wait_ge(root_s, i + 1)
                link(dve.scalar_tensor_tensor(out=t, in0=v, scalar=-0.5, in1=y, op0=ALU.mult, op1=ALU.mult))
                link(dve.tensor_tensor(t, t, y, ALU.mult))
                ins = dve.scalar_tensor_tensor(out=y, in0=t, scalar=1.5, in1=y, op0=ALU.add, op1=ALU.mult)
                if ready is None:
                    link(ins)
                else:
                    ins.then_inc(ready, 1)

            dve.wait_ge(ssq_s, NT)
            rstd(0, ((st[:, 0:2], D, 0, 2),))
            for t in range(NT):
                dve.tensor_scalar(hn[:, t, :], xin[:, t, :], inv[:, t:t + 1], None, ALU.mult).then_inc(xhat_s, 1)
            dve.wait_ge(small_in, 16 * 7)
            dve.wait_ge(consts, CONSTS)
            link(dve.tensor_copy(pos_f[:, :], pos_i[:, :]))
            for t in range(NT):
                last = dve.tensor_scalar(ang[:, t, :], inv_freq[:, :], pos_f[:, t:t + 1], None, ALU.mult)
            link(last)
            dve.tensor_scalar(turns[:, 0, :, :], ang[:, :, :], 1.0 / (2 * math.pi), None, ALU.mult)
            link(dve.tensor_scalar(turns[:, 1, :, :], ang[:, :, :], 1.0 / (2 * math.pi), 0.25, ALU.mult, ALU.add))
            link(dve.tensor_scalar(turns[:, :, :, :], turns[:, :, :, :], ROUNDER, ROUNDER, ALU.add, ALU.subtract))
            for a in range(2):
                last = dve.scalar_tensor_tensor(out=red[:, a, :, :], in0=turns[:, a, :, :], scalar=-TWO_PI_1,
                                                in1=ang[:, :, :], op0=ALU.mult, op1=ALU.add)
            link(last)
            for part in (TWO_PI_2, TWO_PI_3):
                link(dve.scalar_tensor_tensor(out=red[:, :, :, :], in0=turns[:, :, :, :], scalar=-part,
                                              in1=red[:, :, :, :], op0=ALU.mult, op1=ALU.add))
            link(dve.tensor_scalar(red[:, 1, :, :], red[:, 1, :, :], math.pi / 2, None, ALU.add))
            lim = 3.1415925
            dve.tensor_scalar(red[:, :, :, :], red[:, :, :, :], lim, -lim, ALU.min, ALU.max).then_inc(red_s, 1)
            dve.wait_ge(gt_s, 1)
            for n in (1, 3):
                dve.wait_ge(filled, FILL_X + n + 1)
                for i in range(2):
                    k = 2 * n + i
                    last = dve.tensor_scalar(hT[:, k, :], bank(n)[:, SEQ * i:SEQ * i + SEQ], gT[:, k:k + 1], None,
                                             ALU.mult)
                last.then_inc(emptied[1], 1)
            dve.wait_ge(lat_ss, 1)
            rstd(1, ((ps[:, 7, 0:2], CQ, 2, 4), (ps[:, 7, 2:4], CKV, 4, 6)), lat_rs)
            dve.wait_ge(lat_rs, 1)
            for m in range(8):
                n = FILL_UP + m
                if n % 2 == 0:
                    continue
                dve.wait_ge(filled, n + 1)
                dst, src, scale = up_piece(m)
                dve.tensor_scalar(dst, src, scale, None, ALU.mult).then_inc(emptied[1], 1)
            sq = qkT[:, :, :, :].rearrange("p h a s -> p (h a s)")
            qf = q_mla[:, :, :, :].rearrange("p t h d -> p (t h) d")
            sqq = sq[:, 0:NT * HEADS * DQK].rearrange("p (h d) -> p h d", d=DQK)
            dve.wait_ge(emptied[0], (FILL_QKV + 1) // 2)
            dve.wait_ge(emptied[1], FILL_QKV // 2)
            link(dve.tensor_tensor(sqq, qf, qf, ALU.mult))
            link(dve.tensor_reduce(st[:, 48:64], sqq, AX.X, ALU.add))
            rstd(2, ((st[:, 48:64], DQK, 6, 22),))
            link(dve.tensor_tensor(qf, qf, inv[:, 6:22].unsqueeze(2).to_broadcast([P, 16, DQK]), ALU.mult))
            link(dve.tensor_tensor(qf, qf, gq_bc[:, :].unsqueeze(1).to_broadcast([P, 16, DQK]), ALU.mult))
            dve.wait_ge(cs_s, 1)
            t4 = sq[:, 2048:4096].rearrange("p (a t h d) -> p a t h d", a=8, t=NT, h=HEADS)

            def rotate(vec, heads, ready):
                def trig(a, t):
                    c = cs[:, a, t, :]
                    return c.unsqueeze(1).to_broadcast([P, heads, HALF]) if heads else c
                for t in range(NT):
                    tmp = [t4[:, i, t, :, :] if heads else t4[:, i, t, 0, :] for i in range(4)]
                    x1, x2 = (vec[:, t, :, 0:HALF], vec[:, t, :, HALF:ROPE]) if heads else (
                        vec[:, t, 0:HALF], vec[:, t, HALF:ROPE])
                    dve.tensor_tensor(tmp[0], x1, trig(1, t), ALU.mult)
                    dve.tensor_tensor(tmp[1], x2, trig(0, t), ALU.mult)
                    dve.tensor_tensor(tmp[2], x2, trig(1, t), ALU.mult)
                    link(dve.tensor_tensor(tmp[3], x1, trig(0, t), ALU.mult))
                    dve.tensor_tensor(x1, tmp[0], tmp[1], ALU.subtract)
                    ins = dve.tensor_tensor(x2, tmp[2], tmp[3], ALU.add)
                    if ready is not None and t == NT - 1:
                        ins.then_inc(ready, 1)
                    else:
                        link(ins)

            rotate(q_mla[:, :, :, DH:DQK], HEADS, mla_q_s)
            sqk = sq[:, 0:NT * HEADS * DH].rearrange("p (t h d) -> p t h d", t=NT, h=HEADS)
            for t in range(NT):
                last = dve.tensor_tensor(sqk[:, t, :, :], kv[:, t, :, 0:DH], kv[:, t, :, 0:DH], ALU.mult)
            link(last)
            link(dve.tensor_reduce(st[:, 80:96], sqk.rearrange("p t h d -> p (t h) d"), AX.X, ALU.add))
            sqr = sq[:, 1024:1024 + NT * ROPE].rearrange("p (t d) -> p t d", t=NT)
            link(dve.tensor_tensor(sqr, kr[:, :, :], kr[:, :, :], ALU.mult))
            link(dve.tensor_reduce(st[:, 96:98], sqr, AX.X, ALU.add))
            for t in range(NT):
                last = dve.tensor_scalar(st[:, 80 + 8 * t:88 + 8 * t], st[:, 80 + 8 * t:88 + 8 * t],
                                         st[:, 96 + t:97 + t], None, ALU.add)
            link(last)
            rstd(3, ((st[:, 80:96], DQK, 22, 38),))
            link(dve.tensor_tensor(krr[:, :, :], kr[:, :, :], gk_bc[:, DH:DQK].unsqueeze(1).to_broadcast([P, NT, ROPE]),
                                   ALU.mult))
            rotate(krr, 0, None)
            dve.wait_ge(filled, FILL_X + 4)
            for t in range(NT):
                rk = inv[:, 22 + 8 * t:30 + 8 * t].unsqueeze(2)
                dve.tensor_tensor(k_mla[:, t, :, 0:DH], kv[:, t, :, 0:DH], rk.to_broadcast([P, HEADS, DH]), ALU.mult)
                link(dve.tensor_tensor(k_mla[:, t, :, DH:DQK], krr[:, t, :].unsqueeze(1).to_broadcast([P, HEADS, ROPE]),
                                       rk.to_broadcast([P, HEADS, ROPE]), ALU.mult))
                ins = dve.tensor_tensor(k_mla[:, t, :, 0:DH], k_mla[:, t, :, 0:DH],
                                        gk_bc[:, 0:DH].unsqueeze(1).to_broadcast([P, HEADS, DH]), ALU.mult)
                ins.then_inc(mla_k_s, 1)
            for h in range(1, HEADS, 2):
                dve.wait_ge(turn_s, h + 1)
                if h == 1:
                    dve.wait_ge(mla_k_s, 2)
                dve.tensor_copy(qkT[0:DQK, h, :, :], ps[0:DQK, TURN[h % 4], :].rearrange("p (a s) -> p a s", a=2)
                                ).then_inc(turn_e[h % 4], 1)
            for h in range(HEADS):
                zb = ps[:, 2 + h % 2, 0:384]
                e, w = stick[:, h % 2, :], stay[:, h % 2, :]
                dve.wait_ge(z_s, h + 1)
                dve.tensor_scalar(e, zb, 40.0, None, ALU.min).then_inc(bound_s, 1)
                dve.wait_ge(s_s, h + 1)
                if h:
                    dve.wait_ge(p_s, h)
                dve.tensor_reduce(st[:, 32:33], ps[:, 5, 0:P], AX.X, ALU.max)
                link(dve.tensor_reduce(st[:, 33:34], ps[:, 5, P:384], AX.X, ALU.max))
                dve.tensor_scalar(st[:, 36:38], st[:, 32:34], -DQK ** -0.5, None, ALU.mult).then_inc(max_s, 1)
                dve.wait_ge(ln_s, h + 1)
                link(dve.tensor_tensor(e, zb, e, ALU.max))
                diag = e.rearrange("p (c s) -> p c s", c=3)[:, 0:3:2, :]
                dve.tensor_tensor(diag, diag, before[:, :].unsqueeze(1).to_broadcast([P, 2, P]),
                                  ALU.mult).then_inc(sp_s, 1)
                dve.wait_ge(p_s, h + 1)
                link(dve.reciprocal(st[:, 44:46], st[:, 40:42]))
                dve.tensor_scalar(prob[:, h % 2, 0:P], prob[:, h % 2, 0:P], st[:, 44:45], None, ALU.mult)
                dve.tensor_scalar(prob[:, h % 2, P:384], prob[:, h % 2, P:384], st[:, 45:46], None,
                                  ALU.mult).then_inc(pn_s, 1)
                dve.wait_ge(r_s, h + 1)
                if h >= 2:
                    dve.wait_ge(av_s, h - 1)
                dve.tensor_tensor(w, zb, cap_mask[:, :], ALU.min).then_inc(cap_s, 1)
            dve.wait_ge(mix_s, 1)
            tmp = stick[:, :, 0:SEQ]
            for m in range(KD):
                n = FILL_MIX + m
                dve.wait_ge(filled, n + 1)
                dve.tensor_tensor(gates[:, m, :, :], gates[:, m, :, :], bank(n).rearrange("p (a s) -> p a s", a=2),
                                  ALU.mult).then_inc(emptied[n % 2], 1)
                dve.wait_ge(emptied[n % 2], n // 2 + 1)
                dve.tensor_tensor(gates[:, m, 0, :], gates[:, m, 0, :], gates[:, m, 1, :], ALU.add).then_inc(mix_s, 1)
            for i in range(4):
                n = FILL_OUT + i
                dve.wait_ge(filled, n + 1)
                xs = xin[:, :, 256 * i:256 * i + 256]
                dve.tensor_tensor(xs, xs, bank(n).rearrange("p (t s) -> p t s", t=NT), ALU.add).then_inc(
                    emptied[n % 2], 1)
                dve.wait_ge(emptied[n % 2], n // 2 + 1)
                dve.sem_inc(x1_s, 1)
            dve.memset(lg[:, :, NE:NE + 4], -BIG_RANK)
            link(dve.memset(key[:, :, TOPK:8], -BIG_RANK))
            dve.wait_ge(sum_in, 4)
            link(dve.tensor_reduce(st[:, 128:130], st[:, 120:128].rearrange("p (t i) -> p t i", t=NT), AX.X, ALU.add))
            rstd(4, ((st[:, 128:130], D, 38, 40),))
            dve.wait_ge(gffn_in, 16)
            for t in range(NT):
                dve.scalar_tensor_tensor(out=hn[:, t, :], in0=xin[:, t, :], scalar=inv[:, 38 + t:39 + t], in1=g_ffn_bc,
                                         op0=ALU.mult, op1=ALU.mult).then_inc(h2_s, 1)
            for n in (FILL_H2 + 1, FILL_H2 + 3):
                dve.wait_ge(filled, n + 1)
                k = 2 * (n - FILL_H2)
                dve.tensor_copy(h2T[:, k:k + 2, :], bank(n).rearrange("p (j s) -> p j s", j=2)).then_inc(emptied[1], 1)
            n = FILL_LOGIT
            dve.wait_ge(filled, n + 1)
            dve.tensor_tensor(lg[:, :, 0:NE], bank(n)[:, 0:NT * NE].rearrange("p (t e) -> p t e", t=NT),
                              br_bc[:, :].unsqueeze(1).to_broadcast([P, NT, NE]), ALU.add).then_inc(emptied[0], 1)
            dve.wait_ge(emptied[0], n // 2 + 1)
            for t in range(NT):
                last = dve.max(top[:, t, :], lg[:, t, 0:NE])
            link(last)
            for t in range(NT):
                last = dve.tensor_scalar(expl[:, t, :], lg[:, t, 0:NE], top[:, t, 0:1], None, ALU.subtract)
            last.then_inc(top_s, 1)
            link(dve.tensor_copy(key[:, :, 0:TOPK], top[:, :, 0:TOPK]))
            for t in range(NT):
                last = dve.match_replace(marked[:, t, :], key[:, t, :], lg[:, t, :], BIG_RANK)
            link(last)
            dve.tensor_scalar(chosen[:, :, :], marked[:, :, 0:NE], BIG_RANK, None, ALU.is_ge).then_inc(chosen_s, 1)
            dve.wait_ge(chosen_s, 1)
            n = FILL_RANK
            dve.wait_ge(filled, n + 1)
            pos = bank(n)[:, 0:NT * NE].rearrange("p (t e) -> p t e", t=NT)
            link(dve.scalar_tensor_tensor(out=rank_in[:, :, 0, :], in0=pos, scalar=1.0, in1=chosen[:, :, :],
                                          op0=ALU.add, op1=ALU.mult))
            for r in range(1, ROUNDS):
                dve.tensor_scalar(rank_in[:, :, r, :], rank_in[:, :, 0, :], -1.0 - CAP * r, None, ALU.add)
            link(dve.tensor_scalar(rank_in[:, :, 0, :], rank_in[:, :, 0, :], -1.0, None, ALU.add))
            build_pick(dve, main, 0, 0)
            dve.tensor_copy(count[:, :], bank(n)[:, NT * NE:NT * NE + NE]).then_inc(count_s, 1)
            dve.wait_ge(expl_s, 1)
            link(dve.tensor_tensor(expl[:, :, :], expl[:, :, :], chosen[:, :, :], ALU.mult))
            link(dve.tensor_reduce(st[:, 132:134], expl[:, :, :], AX.X, ALU.add))
            link(dve.reciprocal(st[:, 134:136], st[:, 132:134]))
            for t in range(NT):
                last = dve.tensor_scalar(gate_w[:, t, :], expl[:, t, :], st[:, 134 + t:135 + t], None, ALU.mult)
            last.then_inc(gw_s, 1)
            dve.wait_ge(gw_s, 1)
            tokens_lo(dve, main, 0)
            bodies(dve, dve_body)

            def start():
                dve.sem_inc(extra.ht_lo, 1)
                dve.sem_inc(extra.u, 1)

            def visit(j, column, e):
                def lo(kind):
                    for k in range(4):
                        c = 4 * PASSES.index(kind) + k
                        split_lo(dve, extra, expert_slot(kind, k), 12 * j + c, c % RING, again[c], j + 1)
                build_pick(dve, extra, j, column)
                tokens_lo(dve, extra, j)
                lo("a")
                lo("b")
                for half in range(2):
                    m = 2 * j + half
                    gate_up(dve, extra, half, m, e)
                    times_sigmoid(dve, extra, m)
                    act_lo(dve, extra, half, m)
                build_put(dve, extra, j, column, e)
                lo("d")
                dve.wait_ge(extra.summed, j + 1 + extra.spare)
            further(dve, start, visit)
            dve.wait_ge(main.summed, NE)
            for t in range(NT):
                for b in range(2):
                    xs = xin[:, t, 512 * b:512 * b + 512]
                    dve.tensor_tensor(xs, xs, ps[:, 4 + 2 * t + b, :], ALU.add).then_inc(out_s, 1)

        @block.tensor
        def _(pe):
            def fill(n):
                if n >= 2:
                    pe.wait_ge(emptied[n % 2], n // 2)

            def weights(c):
                n = number[c]
                pe.wait_ge(loaded[n % SLOTS], 16 * (n // SLOTS + 1))
                return chunk(c)[0]

            pe.wait_ge(consts, 3)
            pe.wait_ge(small_in, 16 * 7)
            pe.transpose(ps[:, 7, 0:KD + QT + KVT], gains[:, :], ident[0:KD + QT + KVT, 0:KD + QT + KVT]
                         ).then_inc(gt_ps, 1)
            pe.wait_ge(xhat_s, NT)
            for n in range(4):
                fill(n)
                for i in range(2):
                    for t in range(NT):
                        k = 2 * n + i
                        mm = pe.transpose(bank(n)[:, SEQ * i + P * t:SEQ * i + P * t + P], hn[:, t, P * k:P * k + P],
                                          ident[:, :])
                mm.then_inc(filled, 1)
            for b in range(2):
                pe.wait_ge(emptied[b], 2)

            def turned(n, i, w, c0):
                for k in range(KD):
                    mm = pe.matmul(bank(n)[:, SEQ * i:SEQ * i + SEQ], w[:, k, c0:c0 + P], hT[:, k, :],
                                   start=k == 0, stop=k == KD - 1)
                return mm

            for i in range(3):
                n = FILL_LAT + i
                fill(n)
                w = weights(("lat", i))
                mm = turned(n, 0, w, 0)
                if i < 2:
                    mm = turned(n, 1, w, P)
                else:
                    for t in range(NT):
                        for k in range(KD):
                            mm = pe.matmul(bank(n)[:, SEQ + ROPE * t:SEQ + ROPE * t + ROPE], hT[:, k, P * t:P * t + P],
                                           w[:, k, P:P + ROPE], start=k == 0, stop=k == KD - 1)
                mm.then_inc(filled, 1)
            pe.wait_ge(emptied[0], 4)
            pe.wait_ge(emptied[1], 3)
            for c, (j0, j1) in enumerate(((0, QT), (QT, QT + KVT))):
                for t in range(NT):
                    for j in range(j0, j1):
                        mm = pe.matmul(ps[:, 7, 2 * c + t:2 * c + t + 1], sqT[:, j, P * t:P * t + P], ones[:, 0:1],
                                       start=j == j0, stop=j == j1 - 1)
            mm.then_inc(lat_ss, 1)
            for i in range(2):
                w = weights(("uq", i))
                for t in range(NT):
                    n = FILL_UP + 2 * i + t
                    fill(n)
                    for k in range(QT):
                        mm = pe.matmul(bank(n)[:, 0:384], cT[:, k, P * t:P * t + P], w[:, k, :],
                                       start=k == 0, stop=k == QT - 1)
                    mm.then_inc(filled, 1)
            w = weights(("ukv", 0))
            for t in range(NT):
                for i in range(2):
                    n = FILL_UP + 4 + 2 * t + i
                    fill(n)
                    for k in range(KVT):
                        mm = pe.matmul(bank(n), cT[:, QT + k, P * t:P * t + P], w[:, k, 512 * i:512 * i + 512],
                                       start=k == 0, stop=k == KVT - 1)
                    mm.then_inc(filled, 1)
            for m in range(6):
                n = FILL_QKV + m
                fill(n)
                w = weights(("qkv", m))
                if m < 4:
                    turned(n, 0, w, 0)
                    mm = turned(n, 1, w, P)
                else:
                    for t in range(NT):
                        for k in range(KD):
                            mm = pe.matmul(bank(n)[:, 256 * t:256 * t + 256], hT[:, k, P * t:P * t + P], w[:, k, :],
                                           start=k == 0, stop=k == KD - 1)
                mm.then_inc(filled, 1)
            pe.wait_ge(mla_q_s, 1)
            pe.wait_ge(mla_k_s, 2)
            for h in range(HEADS):
                if h >= 4:
                    pe.wait_ge(turn_e[h % 4], 1)
                for a, src in enumerate((q_mla, k_mla)):
                    for t in range(NT):
                        c = SEQ * a + P * t
                        mm = pe.transpose(ps[0:DQK, TURN[h % 4], c:c + P], src[:, t, h, :], ident[:, :])
                mm.then_inc(turn_s, 1)
            for b in range(4):
                pe.wait_ge(turn_e[b], 2)
            pe.wait_ge(emptied[0], FILL_GATE // 2)
            pe.wait_ge(consts, CONSTS)
            for h in range(HEADS):
                j, r = h // 2, DH * (h % 2)
                zb = ps[:, 2 + h % 2, :]
                if h >= 2:
                    pe.wait_ge(cap_s, h - 1)
                for t, c in ((0, 0), (1, SEQ)):
                    mm = pe.matmul(zb[:, c:c + SEQ - P * t], kT[r:r + DH, j, P * t:P * t + P],
                                   qT[r:r + DH, j, P * t:SEQ], start=t == 0, stop=t == 1, skip_group_check=True)
                mm.then_inc(z_s, 1)
                if h:
                    pe.wait_ge(p_s, h)
                for t, c in ((0, 0), (1, P)):
                    pe.matmul(ps[:, 5, c:c + P * (t + 1)], qkT[0:DQK, h, 0, P * t:P * t + P],
                              qkT[0:DQK, h, 1, 0:P * (t + 1)], start=True, stop=False, skip_group_check=True)
                    mm = pe.matmul(ps[:, 5, c + P * t:c + P * t + P], row_lo[:, :], col_hi[:, :],
                                   start=False, stop=True, skip_group_check=True)
                mm.then_inc(s_s, 1)
                n = FILL_GATE + h
                fill(n)
                w = weights(("gate", h))
                turned(n, 0, w, 0)
                pe.wait_ge(sp_s, h + 1)
                e = stick[:, h % 2, :]
                pe.matmul(zb[:, 0:SEQ], neg_from[:, :], e[:, 0:SEQ], start=False, stop=False, skip_group_check=True)
                pe.matmul(zb[:, P:SEQ], neg_ones[:, :], e[:, SEQ:384], start=False, stop=False, skip_group_check=True)
                pe.matmul(zb[:, SEQ:384], neg_from[:, :], e[:, SEQ:384], start=False, stop=True,
                          skip_group_check=True).then_inc(r_s, 1)
                pe.wait_ge(pn_s, h + 1)
                if h:
                    pe.wait_ge(pte_s, h)
                for c in range(3):
                    mm = pe.transpose(ps[:, 6, P * (0, 1, 2)[c]:P * c + P], prob[:, h % 2, P * c:P * c + P], ident[:, :])
                mm.then_inc(pt_s, 1)
                mm = turned(n, 1, w, P)
                mm.then_inc(filled, 1)
                if h >= 4 and h % 2 == 0:
                    pe.wait_ge(oe_s, j - 1)
                c = SEQ * (j % 2)
                for sem_in, sem_out, b, a, val in ((a_s, av_s, 4, stay, lambda t: v_sb[:, t, DH * h:DH * h + DH]),
                                                   (pte_s, mv_s, 7, probT, lambda t: kv[:, t, h, DH:2 * DH])):
                    pe.wait_ge(sem_in, h + 1)
                    pe.matmul(ps[r:r + DH, b, c:c + SEQ], val(0), a[:, h % 2, 0:SEQ], start=True, stop=False,
                              skip_group_check=True)
                    pe.matmul(ps[r:r + DH, b, c + P:c + SEQ], val(1), a[:, h % 2, SEQ:384], start=False, stop=True,
                              skip_group_check=True).then_inc(sem_out, 1)
            n = FILL_BUP
            fill(n)
            w = weights(("bup", 0))
            for i in range(16):
                half, g, j = i // 8, i // 4 % 2, i % 4
                c0 = 2 * P * (4 * half + j) + g
                mm = pe.transpose(bank(n)[:, NE * i:NE * i + NE], w[:, c0:c0 + 2 * P - 1:2], ident[0:NE, 0:NE])
            mm.then_inc(filled, 1)
            pe.wait_ge(oe_s, 4)
            for m in range(KD):
                n = FILL_MIX + m
                fill(n)
                for a, (name, o) in enumerate((("osb", o_sb), ("omla", o_mla_sb))):
                    w = weights((name, m // 4))
                    for k in range(4):
                        mm = pe.matmul(bank(n)[:, SEQ * a:SEQ * a + SEQ], w[:, k, P * (m % 4):P * (m % 4) + P],
                                       o[:, k, :], start=k == 0, stop=k == 3)
                mm.then_inc(filled, 1)
            pe.wait_ge(mix_s, 1 + KD)
            for i in range(4):
                n = FILL_OUT + i
                fill(n)
                w = weights(("wout", i))
                for t in range(NT):
                    for k in range(KD):
                        mm = pe.matmul(bank(n)[:, 256 * t:256 * t + 256], gates[:, k, 0, P * t:P * t + P], w[:, k, :],
                                       start=k == 0, stop=k == KD - 1)
                mm.then_inc(filled, 1)
            pe.wait_ge(h2_s, NT)
            for m in range(4):
                n = FILL_H2 + m
                fill(n)
                for i in range(2):
                    for t in range(NT):
                        k = 2 * m + i
                        mm = pe.transpose(bank(n)[:, SEQ * i + P * t:SEQ * i + P * t + P], hn[:, t, P * k:P * k + P],
                                          ident[:, :])
                mm.then_inc(filled, 1)
            n = FILL_LOGIT
            fill(n)
            pe.wait_ge(emptied[1], n // 2)
            w = weights(("router", 0))
            for t in range(NT):
                for k in range(KD):
                    mm = pe.matmul(bank(n)[:, NE * t:NE * t + NE], h2T[:, k, P * t:P * t + P], w[:, k, :],
                                   start=k == 0, stop=k == KD - 1)
            mm.then_inc(filled, 1)
            n = FILL_RANK
            fill(n)
            pe.wait_ge(chosen_s, 1)
            for c, terms in enumerate((((before, 0),), ((ones, 0), (before, 1)), ((ones, 0), (ones, 1)))):
                for i, (mat, t) in enumerate(terms):
                    mm = pe.matmul(bank(n)[:, NE * c:NE * c + NE], mat[:, :], chosen[:, t, :], start=i == 0,
                                   stop=i == len(terms) - 1)
            mm.then_inc(filled, 1)
            gather(pe, main, 0, 0)
            n = FILL_WT
            fill(n)
            pe.wait_ge(gw_s, 1)
            for t in range(NT):
                mm = pe.transpose(ps[0:NE, 0, P * t:P * t + P], gate_w[:, t, :], ident[:, :])
            mm.then_inc(filled, 1)
            pe.wait_ge(wt_s, 1)
            pe.wait_ge(count_s, 1)
            w = weights(("bdown", 0))
            for t in range(NT):
                for b in range(2):
                    mm = pe.matmul(ps[:, 4 + 2 * t + b, :], gate_wT[:, P * t:P * t + P], w[:, 512 * b:512 * b + 512],
                                   start=True, stop=False, skip_group_check=True)
            mm.then_inc(acc_s, 1)
            bodies(pe, pe_body)
            add_visit(pe, main, NE - 1, pass_number(NE, "d"))

            def start():
                pe.sem_inc(extra.w_used, RING)
                pe.sem_inc(extra.gathered, 1)
                pe.sem_inc(extra.gu_turned, 2)
                pe.sem_inc(extra.put_turned, 1)
                pe.sem_inc(extra.summed, 1)

            def visit(j, column, e):
                gather(pe, extra, j, j)
                product(pe, extra, "a", j, 12 * j, 0, 3 * j)
                turn_up(pe, extra, 0, j, 3 * j)
                product(pe, extra, "b", j, 12 * j + 4, 4 % RING, 3 * j + 1)
                turn_up(pe, extra, 1, j, 3 * j + 1)
                product(pe, extra, "d", j, 12 * j + 8, 8 % RING, 3 * j + 2)
                turn_put(pe, extra, j, j + 1)
                add_visit(pe, extra, j, 3 * j + 2)
            further(pe, start, visit)


TURN = (2, 3, 5, 6)
CONSTS = 34
RMS = ((0, 2), (2, 6), (6, 22), (22, 38), (38, 40))

_INS = ['x', 'positions', 'g_mix', 'w_in', 'g_cq', 'w_uq', 'g_ckv', 'w_ukv', 'g_qnorm', 'g_knorm', 'w_o_sb',
        'w_o_mla', 'w_out', 'g_ffn', 'w_router', 'b_router', 'w_up', 'b_up', 'w_down', 'b_down']


def kernel(**inputs):
    import numpy as _np
    import concourse.bacc as _bacc
    from concourse import mybir as _mybir
    from concourse.bass_utils import run_bass_kernel_spmd as _run

    nc = _bacc.Bacc("TRN2", target_bir_lowering=False, num_devices=1)
    arrays, args = {}, []
    for name in _INS:
        a = _np.ascontiguousarray(inputs[name])
        arrays[f"in_{name}_dram"] = a
        args.append(nc.dram_tensor(f"in_{name}_dram", a.shape, _mybir.dt.from_np(a.dtype), kind="ExternalInput").ap())
    args.append(nc.dram_tensor("out_0_dram", inputs["x"].shape, F32, kind="ExternalOutput").ap())
    encoder_block(nc, *args)
    r = _run(nc, [arrays], core_ids=[0])
    return r.results[0]["out_0_dram"]
```

```python
from contextlib import ExitStack
import math

import numpy as np
from concourse import mybir
from concourse.bass import ds

ALU = mybir.AluOpType
ACT = mybir.ActivationFunctionType
AX = mybir.AxisListType
F32 = mybir.dt.float32
F32R = mybir.dt.float32r
I32 = mybir.dt.int32

P = 128
D = 1024
KD = D // P
SEQ = 256
NT = SEQ // P
EPS = 1e-6
HEADS = 8
DH = 64
SBW = HEADS * DH
ROPE = 32
HALF = ROPE // 2
DQK = DH + ROPE
CQ, CKV = 384, 256
QT, KVT = CQ // P, CKV // P
THETA = 10000.0
CHUNK = 64
TOPK = 4
NE = 32
FF = 1024
LIMIT = 7.0
ALPHA = 1.702
NEG = -1.0e30

C_Q, C_K, C_V = 0, SBW, 2 * SBW
C_CQ = 3 * SBW
C_CKV = C_CQ + CQ
C_KR = C_CKV + CKV
C_GA = C_KR + ROPE
C_GB = C_GA + D

SLOTS = 12
SLOT = 2048
PER_EXPERT = 12
CAP = 64
COLS = 64
ROUNDS = SEQ // CAP
MAX_EXTRA = SEQ * TOPK // CAP
RING = 6
STAGE = 2

BIG_RANK = 3.0e38
TWO_PI_1 = 6.28125
TWO_PI_2 = float(np.float32(0.0019350051879882812))
TWO_PI_3 = float(2 * math.pi - TWO_PI_1 - TWO_PI_2)
ROUNDER = 12582912.0


def plan_chunks():
    return ([("lat", i) for i in range(3)] + [("uq", i) for i in range(2)] + [("ukv", 0)]
            + [("qkv", i) for i in range(6)] + [("gate", i) for i in range(8)] + [("bup", 0)]
            + [("osb", 0), ("omla", 0), ("osb", 1), ("omla", 1)]
            + [("wout", i) for i in range(4)] + [("router", 0), ("bdown", 0)])


def encoder_block(nc, x, positions, g_mix, w_in, g_cq, w_uq, g_ckv, w_ukv, g_qnorm, g_knorm, w_o_sb,
                  w_o_mla, w_out, g_ffn, w_router, b_router, w_up, b_up, w_down, b_down, out):
    chunks = plan_chunks()
    NCH = len(chunks)
    number = {c: n for n, c in enumerate(chunks)}

    ctx = ExitStack()
    att = ExitStack()

    def sb(name, shape, dt=F32, stack=ctx):
        return stack.enter_context(nc.sbuf_tensor(name, shape, dt))

    def sem(name):
        return ctx.enter_context(nc.semaphore(name))

    class VisitSemaphores:
        pass

    def visit_semaphores(tag, spare):
        q = VisitSemaphores()
        q.spare = spare
        q.hi, q.lo = sem(tag + "_w_hi"), sem(tag + "_w_lo")
        q.w_used = sem(tag + "_w_used")
        q.p_read = sem(tag + "_product_read")
        q.ht_hi, q.ht_lo = sem(tag + "_ht_hi"), sem(tag + "_ht_lo")
        q.pick, q.put = sem(tag + "_pick"), sem(tag + "_put")
        q.gathered, q.put_turned, q.putT = sem(tag + "_gathered"), sem(tag + "_put_turned"), sem(tag + "_putT")
        q.gu_turned, q.u = sem(tag + "_gu_turned"), sem(tag + "_u")
        q.glu, q.lin, q.gated = sem(tag + "_glu"), sem(tag + "_lin"), sem(tag + "_gated")
        q.sig, q.act = sem(tag + "_sig"), sem(tag + "_act")
        q.act_hi, q.act_lo = sem(tag + "_act_hi"), sem(tag + "_act_lo")
        q.summed = sem(tag + "_summed")
        return q

    with ctx:
        ps = ctx.enter_context(nc.psum_tensor("ps", [P, 8, 512], F32))

        lo_parts = ExitStack()
        slot_lo = [sb(f"slot{s}_lo", [P, SLOT], F32R, lo_parts) for s in range(SLOTS)]
        lo_parts.close()
        slot = [sb(f"slot{s}", [P, SLOT]) for s in range(SLOTS)]
        ident = sb("ident", [P, P])
        ones = sb("ones", [P, P])
        before = sb("before", [P, P])
        xin = sb("xin", [P, NT, D])
        hn = sb("hn", [P, NT, D])
        slot_no = sb("slot_no", [P, 2, COLS])
        fold = sb("fold", [P, COLS])
        b_upT = sb("b_upT", [P, 2, 2, 4, NE])
        rank_in = sb("rank_in", [P, NT, ROUNDS, NE])
        gate_w = sb("gate_w", [P, NT, NE])
        count = sb("count", [P, NE])
        visit_f = sb("visit_f", [1, 3, MAX_EXTRA])
        visit_i = sb("visit_i", [1, 3, MAX_EXTRA], I32)
        var, inv, half_vy = sb("var", [P, 40]), sb("inv", [P, 40]), sb("half_vy", [P, 40])
        br_bc = sb("br_bc", [P, NE])

        def sa(name, shape, dt=F32):
            return sb(name, shape, dt, att)

        hT = sa("hT", [P, KD, SEQ])
        qT = sa("qT", [P, 4, SEQ])
        kT = sa("kT", [P, 4, SEQ])
        v_sb = sa("v_sb", [P, NT, SBW])
        gates = sa("gates", [P, KD, 2, SEQ])
        q_mla = sa("q_mla", [P, NT, HEADS, DQK])
        kv = sa("kv", [P, NT, HEADS, 2 * DH])
        qkT = sa("qkT", [P, HEADS, 2, SEQ])
        stick = sa("stick", [P, 2, 384])
        stay = sa("stay", [P, 2, 384])
        prob = sa("prob", [P, 2, 384])
        probT = sa("probT", [P, 2, 384])
        neg_from = sa("neg_from", [P, P])
        neg_ones = sa("neg_ones", [P, P])
        cap_mask = sa("cap_mask", [P, 384])
        row_lo = sa("row_lo", [P, P])
        col_hi = sa("col_hi", [P, P])
        gains = sa("gains", [KD + QT + KVT, P])
        gT = sa("gT", [P, KD + QT + KVT])
        gq_bc = sa("gq_bc", [P, DQK])
        gk_bc = sa("gk_bc", [P, DQK])
        inv_freq = sa("inv_freq", [P, HALF])
        pos_i = sa("pos_i", [P, NT], I32)
        pos_f = sa("pos_f", [P, NT])
        ang = sa("ang", [P, NT, HALF])
        turns = sa("turns", [P, 2, NT, HALF])
        red = sa("red", [P, 2, NT, HALF])
        cs = sa("cs", [P, 2, NT, HALF])
        kr = sa("kr", [P, NT, ROPE])
        krr = sa("krr", [P, NT, ROPE])
        st = sa("st", [P, 160])
        lg = sa("lg", [P, NT, NE + 4])
        marked = sa("marked", [P, NT, NE + 4])
        top = sa("top", [P, NT, 8])
        key = sa("key", [P, NT, 8])
        chosen = sa("chosen", [P, NT, NE])
        expl = sa("expl", [P, NT, NE])
        o_sb = q_mla[:, :, :, :].rearrange("p t h d -> p (t h d)")[:, 0:4 * SEQ].rearrange("p (j s) -> p j s", j=4)
        o_mla_sb = hn[:, 0, :].rearrange("p (j s) -> p j s", j=4)
        k_mla = hn[:, :, 0:HEADS * DQK].rearrange("p t (h d) -> p t h d", h=HEADS)
        gates_flat = gates[:, :, :, :].rearrange("p k a s -> p (k a) s")
        cT, sqT = gates_flat[:, 0:5, :], gates_flat[:, 5:10, :]
        g_ffn_bc = kv[:, 0, :, :].rearrange("p h d -> p (h d)")
        h2T = hT
        att.close()

        w_hi = sb("w_hi", [P, RING, SLOT], F32R)
        hTs = sb("hTs", [P, KD, 2, COLS], F32R)
        actT = sb("actT", [P, 8, 2, COLS], F32R)
        gu_sb = sb("gu_sb", [P, 2, 1024])
        y_sb = sb("y_sb", [P, D])
        pick = sb("pick", [P, NT, COLS])
        put = sb("put", [P, NT, 2, COLS])
        putT = sb("putT", [P, SEQ])
        u = sb("u", [P, 2, 4, COLS])
        gated = sb("gated", [P, 4, COLS])
        sig = sb("sig", [P, 4, COLS])
        act32 = sb("act32", [P, 4, COLS])
        gate_wT = sb("gate_wT", [NE, SEQ])
        more = sb("more", [1, 3, (ROUNDS - 1) * NE])
        codes = sb("codes", [1, 2, (ROUNDS - 1) * NE])
        found = sb("found", [1, (ROUNDS - 1) * NE])

        loaded = [sem(f"slot{s}_loaded") for s in range(SLOTS)]
        x_in = [sem(f"x_in{t}") for t in range(NT)]
        gains_in, small_in, gffn_in, out_done = sem("gains_in"), sem("small_in"), sem("gffn_in"), sem("out_done")
        consts = sem("consts")
        filled = sem("filled")
        emptied = [sem(f"bank{b}_emptied") for b in range(2)]
        dve_s, act_s = sem("dve_steps"), sem("act_steps")
        ssq_s, xhat_s, gt_ps, gt_s = sem("sumsq"), sem("xhat"), sem("gains_turned"), sem("gains_ready")
        lat_ss, lat_rs = sem("latent_sumsq"), sem("latent_rstd")
        red_s, cs_s = sem("angles_reduced"), sem("sincos")
        mla_q_s, mla_k_s = sem("mla_q_ready"), sem("mla_k_ready")
        turn_s = sem("qk_turned")
        turn_e = [sem(f"qk_bank{b}_emptied") for b in range(4)]
        z_s, bound_s, ln_s, sp_s, r_s, cap_s, a_s, av_s = (sem(n) for n in (
            "sb_scores", "sb_bounded", "sb_log", "sb_softplus", "sb_logweights", "sb_capped", "sb_weights", "sb_pv"))
        s_s, max_s, p_s, pn_s, pt_s, pte_s, mv_s = (sem(n) for n in (
            "mla_scores", "mla_max", "mla_exp", "mla_probs", "mla_probs_turned", "mla_probsT", "mla_pv"))
        oe_s = sem("heads_out")
        recip_s, root_s = sem("rms_recip"), sem("rms_root")
        mix_s, x1_s, h2_s = sem("mixed"), sem("x1_ready"), sem("h2_ready")
        top_s, expl_s, chosen_s, count_s, wt_s = (sem(n) for n in (
            "logits_shifted", "logits_exp", "chosen_ready", "counts_ready", "gate_w_turned"))
        acc_s, pool_s, visits_s, out_s = sem("bias_summed"), sem("pool_steps"), sem("visits_ready"), sem("out_ready")
        gwt_ps, last_s = sem("gate_w_in_psum"), sem("last_expert_summed")
        gw_s, sum_in = sem("gate_w_ready"), sem("x1_squares")
        main = visit_semaphores("v", 0)
        extra = visit_semaphores("x", 1)
        again = [sem(f"chunk{c}_again") for c in range(PER_EXPERT)]

        w_upv = w_up.rearrange("l e (k p) n -> (l e) p k n", p=P)
        w_downv = w_down.rearrange("l e (k p) n -> (l e) p k n", p=P)

        xv = x.rearrange("b (t p) d -> p (b t) d", p=P)
        ov = out.rearrange("b (t p) d -> p (b t) d", p=P)
        posv = positions.rearrange("b (t p) -> p (b t)", p=P)
        w_inv = w_in.rearrange("l (k p) n -> p (l k) n", p=P)
        w_uqv = w_uq.rearrange("l (k p) n -> p (l k) n", p=P)
        w_ukvv = w_ukv.rearrange("l (k p) n -> p (l k) n", p=P)
        w_osv = w_o_sb.rearrange("l (k p) n -> p (l k) n", p=P)
        w_omv = w_o_mla.rearrange("l (k p) n -> p (l k) n", p=P)
        w_outv = w_out.rearrange("l (k p) n -> p (l k) n", p=P)
        w_rv = w_router.rearrange("l (k p) n -> p (l k) n", p=P)

        def chunk(c):
            name, i = c
            t = slot[number[c] % SLOTS]

            def view(k, n):
                return t[:, 0:k * n].rearrange("p (k n) -> p k n", k=k)
            if name == "lat":
                n = 256 if i < 2 else 160
                return view(KD, n), w_inv[:, :, C_CQ + 256 * i:C_CQ + 256 * i + n]
            if name == "uq":
                return view(QT, 384), w_uqv[:, :, 384 * i:384 * i + 384]
            if name == "ukv":
                return view(KVT, 1024), w_ukvv
            if name == "qkv":
                return view(KD, 256), w_inv[:, :, 256 * i:256 * i + 256]
            if name == "gate":
                c0 = (C_GA, C_GB)[i % 2] + 256 * (i // 2)
                return view(KD, 256), w_inv[:, :, c0:c0 + 256]
            if name == "osb":
                return view(4, 512), w_osv[:, :, 512 * i:512 * i + 512]
            if name == "omla":
                return view(4, 512), w_omv[:, :, 512 * i:512 * i + 512]
            if name == "wout":
                return view(KD, 256), w_outv[:, :, 256 * i:256 * i + 256]
            if name == "router":
                return view(KD, NE), w_rv
            if name == "bup":
                return t[0:NE, 0:2 * FF], b_up.rearrange("l e n -> (l e) n")
            return t[0:NE, 0:D], b_down.rearrange("l e n -> (l e) n")

        FILL_X = 0
        FILL_LAT = 4
        FILL_UP = 7
        FILL_QKV = 15
        FILL_GATE = 21
        FILL_BUP = 29
        FILL_MIX = 30
        FILL_OUT = 38
        FILL_H2 = 42
        FILL_LOGIT = 46
        FILL_RANK = 47

        def last_fill(c):
            name, i = c
            return {"lat": FILL_LAT + i, "uq": FILL_UP + 2 * i + 1, "ukv": FILL_UP + 7, "qkv": FILL_QKV + i,
                    "gate": FILL_GATE + i, "bup": FILL_BUP, "osb": FILL_MIX + 4 * i + 3,
                    "omla": FILL_MIX + 4 * i + 3, "wout": FILL_OUT + i, "router": FILL_LOGIT,
                    }[name]

        def bank(n):
            return ps[:, n % 2, :]

        def up_piece(m):
            b = bank(FILL_UP + m)
            if m < 4:
                i, t = m // 2, m % 2
                return (q_mla[:, t, 4 * i:4 * i + 4, :], b[:, 0:384].rearrange("p (h d) -> p h d", h=4),
                        inv[:, 2 + t:3 + t])
            t, i = (m - 4) // 2, m % 2
            return (kv[:, t, 4 * i:4 * i + 4, :], b.rearrange("p (h d) -> p h d", h=4), inv[:, 4 + t:5 + t])


        PASSES = ("a", "b", "d")

        def expert_slot(kind, k, last=False):
            return (NCH + 4 * PASSES.index("a" if last else kind) + k) % SLOTS

        def load_chunk(sp, kind, k, e, s, signal):
            dst = slot[s][:, :].rearrange("p (k n) -> p k n", k=2)
            if kind == "d":
                src = w_downv[e, :, 2 * k:2 * k + 2, :]
            else:
                c0 = 1024 * (kind == "b")
                src = w_upv[e, :, 2 * k:2 * k + 2, c0:c0 + 1024]
            sp.dma_start(dst, src).then_inc(signal, 16)

        def split_hi(act, q, s, n, at, arrived, times):
            act.wait_ge(arrived, 16 * times)
            free(act, q.w_used, n - RING + 1, q.spare * RING)
            act.activation(w_hi[:, at, :], slot[s][:, :], ACT.Copy).then_inc(q.hi, 1)

        def split_lo(dve, q, s, n, at, arrived, times):
            dve.wait_ge(arrived, 16 * times)
            dve.wait_ge(q.hi, n + 1)
            dve.tensor_tensor(slot_lo[s][:, :], slot[s][:, :], w_hi[:, at, :].bitcast(F32),
                              ALU.subtract).then_inc(q.lo, 1)

        def free(eng, s, n, spare):
            if isinstance(n, int) and n + spare <= 0:
                return
            eng.wait_ge(s, n + spare)

        def gather(pe, q, v, puts):
            pe.wait_ge(q.pick, v + 1)
            free(pe, q.ht_hi, v, q.spare)
            free(pe, q.ht_lo, v, q.spare)
            free(pe, q.putT, puts, q.spare)
            for k in range(KD):
                for t in range(NT):
                    mm = pe.matmul(ps[:, 2, COLS * k:COLS * k + COLS], hn[:, t, P * k:P * k + P], pick[:, t, :],
                                   start=t == 0, stop=t == NT - 1)
            mm.then_inc(q.gathered, 1)

        def product(pe, q, kind, v, first, at, pn, last=False):
            free(pe, q.p_read, pn, q.spare)
            if kind == "d":
                x2 = actT
            else:
                x2 = hTs
                pe.wait_ge(q.ht_hi, v + 1 + q.spare)
                pe.wait_ge(q.ht_lo, v + 1 + q.spare)
            for k in range(4):
                if kind == "d" and k % 2 == 0:
                    pe.wait_ge(q.act_hi, 2 * v + k // 2 + 1)
                    pe.wait_ge(q.act_lo, 2 * v + k // 2 + 1)
                pe.wait_ge(q.hi, first + k + 1)
                for i in range(2):
                    lhs = x2[:, 2 * k + i, :, :].rearrange("p a c -> p (a c)")
                    for part, w in enumerate((w_hi[:, (at + k) % RING, :], slot_lo[expert_slot(kind, k, last)])):
                        if i == 0 and part == 1:
                            pe.wait_ge(q.lo, first + k + 1)
                        for b in range(2):
                            c0 = 1024 * i + 512 * b
                            mm = pe.matmul(ps[:, b, :], lhs, w[:, c0:c0 + 512],
                                           start=k + i + part == 0, stop=k + i + part == 5)
                mm.then_inc(q.w_used, 1)

        def turn_up(pe, q, half, v, pn):
            pe.wait_ge(q.p_read, pn + 1 + q.spare)
            free(pe, q.u, 2 * v + half, q.spare)
            for g in range(2):
                for j in range(4):
                    c0 = 2 * P * j + g
                    o = COLS * (4 * g + j)
                    mm = pe.matmul(ps[:, 3, o:o + COLS], gu_sb[:, half, c0:c0 + 2 * P - 1:2], fold[:, :],
                                   start=True, stop=True)
            mm.then_inc(q.gu_turned, 1)

        def turn_put(pe, q, v, gathers):
            pe.wait_ge(q.put, v + 1)
            pe.wait_ge(q.ht_hi, gathers + q.spare)
            pe.wait_ge(q.ht_lo, gathers + q.spare)
            free(pe, q.putT, v, q.spare)
            for t in range(NT):
                mm = pe.transpose(ps[:, 2, P * t:P * t + P], put[:, t, :, :].rearrange("p a c -> p (a c)"), ident[:, :])
            mm.then_inc(q.put_turned, 1)

        def add_visit(pe, q, v, pn, each=None):
            pe.wait_ge(q.p_read, pn + 1 + q.spare)
            pe.wait_ge(q.putT, v + 1 + q.spare)
            for t in range(NT):
                for b in range(2):
                    mm = pe.matmul(ps[:, 4 + 2 * t + b, :], putT[:, P * t:P * t + P], y_sb[:, 512 * b:512 * b + 512],
                                   start=False, stop=False, skip_group_check=True)
                    if each is not None:
                        mm.then_inc(each, 1)
            if each is None:
                mm.then_inc(q.summed, 1)

        def copy_up(act, q, half, v, last):
            act.wait_ge(q.w_used, last + q.spare * RING)
            free(act, q.gu_turned, 2 * v + half - 1, 2 * q.spare)
            act.activation(gu_sb[:, half, :], ps[:, 0:2, :].rearrange("p b n -> p (b n)"), ACT.Copy).then_inc(q.p_read, 1)

        def copy_down(act, q, v, last):
            act.wait_ge(q.w_used, last + q.spare * RING)
            free(act, q.summed, v, q.spare)
            act.activation(y_sb[:, :], ps[:, 0:2, :].rearrange("p b n -> p (b n)"), ACT.Copy).then_inc(q.p_read, 1)

        def copy_put(act, q, v):
            act.wait_ge(q.put_turned, v + 1 + q.spare)
            free(act, q.summed, v, q.spare)
            act.activation(putT[:, :], ps[:, 2, 0:SEQ], ACT.Copy).then_inc(q.putT, 1)

        def tokens_hi(act, q, v):
            act.wait_ge(q.gathered, v + 1 + q.spare)
            act.activation(hTs[:, :, 0, :], ps[:, 2, :].rearrange("p (k c) -> p k c", k=KD), ACT.Copy
                           ).then_inc(q.ht_hi, 1)

        def sigmoid(act, q, m):
            act.wait_ge(q.glu, m + 1)
            act.activation(sig[:, :, :], u[:, 0, :, :], ACT.Sigmoid, scale=ALPHA).then_inc(q.sig, 1)

        def act_hi(act, q, half, m):
            act.wait_ge(q.act, m + 1)
            act.activation(actT[:, 4 * half:4 * half + 4, 0, :], act32[:, :, :], ACT.Copy).then_inc(q.act_hi, 1)

        def build_pick(dve, q, v, column):
            free(dve, q.gathered, v, q.spare)
            for t in range(NT):
                ins = dve.tensor_scalar(pick[:, t, :], slot_no[:, 0, :], rank_v[:, t, ds(column, 1)], None, ALU.is_equal)
            ins.then_inc(q.pick, 1)

        def build_put(dve, q, v, column, e):
            free(dve, q.put_turned, v, q.spare)
            for t in range(NT):
                ins = dve.tensor_scalar(put[:, t, :, :], slot_no[:, :, :], rank_v[:, t, ds(column, 1)],
                                        gate_w[:, t, ds(e, 1)], ALU.is_equal, ALU.mult)
            ins.then_inc(q.put, 1)

        def tokens_lo(dve, q, v):
            dve.wait_ge(q.ht_hi, v + 1 + q.spare)
            dve.tensor_tensor(hTs[:, :, 1, :], ps[:, 2, :].rearrange("p (k c) -> p k c", k=KD),
                              hTs[:, :, 0, :].bitcast(F32), ALU.subtract).then_inc(q.ht_lo, 1)

        def gate_up(dve, q, half, m, e):
            dve.wait_ge(q.gu_turned, m + 1 + 2 * q.spare)
            bias = b_upT[:, half, :, :, ds(e, 1)].to_broadcast([P, 2, 4, COLS])
            dve.tensor_tensor(u[:, :, :, :], ps[:, 3, :].rearrange("p (g j c) -> p g j c", g=2, j=4), bias, ALU.add
                              ).then_inc(q.u, 1)
            dve.wait_ge(q.u, m + 1 + q.spare)
            dve.tensor_scalar(u[:, 0, :, :], u[:, 0, :, :], LIMIT, None, ALU.min).then_inc(q.glu, 1)
            dve.tensor_scalar(u[:, 1, :, :], u[:, 1, :, :], LIMIT, -LIMIT, ALU.min, ALU.max).then_inc(q.lin, 1)
            dve.wait_ge(q.glu, m + 1)
            dve.wait_ge(q.lin, m + 1)
            dve.scalar_tensor_tensor(out=gated[:, :, :], in0=u[:, 1, :, :], scalar=1.0, in1=u[:, 0, :, :],
                                     op0=ALU.add, op1=ALU.mult).then_inc(q.gated, 1)

        def times_sigmoid(dve, q, m):
            dve.wait_ge(q.sig, m + 1)
            dve.wait_ge(q.gated, m + 1)
            dve.tensor_tensor(act32[:, :, :], gated[:, :, :], sig[:, :, :], ALU.mult).then_inc(q.act, 1)

        def act_lo(dve, q, half, m):
            dve.wait_ge(q.act_hi, m + 1)
            dve.tensor_tensor(actT[:, 4 * half:4 * half + 4, 1, :], act32[:, :, :],
                              actT[:, 4 * half:4 * half + 4, 0, :].bitcast(F32), ALU.subtract).then_inc(q.act_lo, 1)

        rank_v = rank_in[:, :, :, :].rearrange("p t r e -> p t (r e)")
        PASS_AT = {"a": 0, "b": 4, "d": 8}

        def first_chunk(i, kind):
            if isinstance(i, int) and i == 0:
                return PASS_AT[kind]
            if isinstance(i, int) and i == NE:
                return 12 * NE - 4
            return 12 * i - 4 + PASS_AT[kind]

        def place(i, kind):
            return (PASS_AT[kind] - 4 * (not (isinstance(i, int) and i == 0))
                    - 8 * (isinstance(i, int) and i == NE)) % RING

        def pass_number(i, kind):
            if isinstance(i, int) and i == 0:
                return PASS_AT[kind] // 4
            if isinstance(i, int) and i == NE:
                return 3 * NE - 1
            return 3 * i - 1 + PASS_AT[kind] // 4

        def arrival(i, kind, k):
            last = isinstance(i, int) and i == NE
            s = expert_slot(kind, k, last)
            before_experts = len(range(s, NCH, SLOTS))
            return s, loaded[s], before_experts + (NE + 1 if last else i if kind == "d" else i + 1)

        def hi(act, i, kind, k):
            s, arrived, times = arrival(i, kind, k)
            split_hi(act, main, s, first_chunk(i, kind) + k, (place(i, kind) + k) % RING, arrived, times)

        def lo(dve, i, kind, k):
            s, arrived, times = arrival(i, kind, k)
            split_lo(dve, main, s, first_chunk(i, kind) + k, (place(i, kind) + k) % RING, arrived, times)

        def main_product(pe, i, kind):
            product(pe, main, kind, i - (kind == "d"), first_chunk(i, kind), place(i, kind), pass_number(i, kind),
                    last=isinstance(i, int) and i == NE)

        def pe_body(pe, i, before2=True):
            main_product(pe, i, "a")
            turn_up(pe, main, 1, i - 1, pass_number(i - 1, "b"))
            if before2:
                add_visit(pe, main, i - 2, pass_number(i - 1, "d"))
            main_product(pe, i, "b")
            gather(pe, main, i + 1, i - 1)
            main_product(pe, i, "d")
            turn_up(pe, main, 0, i, pass_number(i, "a"))
            turn_put(pe, main, i - 1, i + 2)

        def act_up_passes(act, i, before2=True):
            hi(act, i, "a", 0)
            hi(act, i, "a", 1)
            if before2:
                copy_down(act, main, i - 2, first_chunk(i - 1, "d") + 4)
                copy_put(act, main, i - 2)
            hi(act, i, "a", 2)
            sigmoid(act, main, 2 * (i - 1))
            hi(act, i, "a", 3)
            act_hi(act, main, 0, 2 * (i - 1))
            hi(act, i, "b", 0)
            hi(act, i, "b", 1)
            copy_up(act, main, 0, i, first_chunk(i, "a") + 4)
            hi(act, i, "b", 2)
            sigmoid(act, main, 2 * (i - 1) + 1)
            hi(act, i, "b", 3)
            act_hi(act, main, 1, 2 * (i - 1) + 1)
            for k in range(3):
                hi(act, i, "d", k)
            copy_up(act, main, 1, i, first_chunk(i, "b") + 4)

        def act_body(act, i, before2=True):
            act_up_passes(act, i, before2)
            tokens_hi(act, main, i + 1)
            hi(act, i, "d", 3)

        def dve_up_passes(dve, i, picks):
            lo(dve, i, "a", 0)
            lo(dve, i, "a", 1)
            gate_up(dve, main, 0, 2 * (i - 1), i - 1)
            lo(dve, i, "a", 2)
            times_sigmoid(dve, main, 2 * (i - 1))
            lo(dve, i, "a", 3)
            act_lo(dve, main, 0, 2 * (i - 1))
            lo(dve, i, "b", 0)
            lo(dve, i, "b", 1)
            gate_up(dve, main, 1, 2 * (i - 1) + 1, i - 1)
            lo(dve, i, "b", 2)
            times_sigmoid(dve, main, 2 * (i - 1) + 1)
            if picks:
                build_pick(dve, main, i + 1, i + 1)
            lo(dve, i, "b", 3)
            act_lo(dve, main, 1, 2 * (i - 1) + 1)
            lo(dve, i, "d", 0)
            build_put(dve, main, i - 1, i - 1, i - 1)
            lo(dve, i, "d", 1)

        def dve_body(dve, i):
            dve_up_passes(dve, i, True)
            lo(dve, i, "d", 2)
            tokens_lo(dve, main, i + 1)
            lo(dve, i, "d", 3)

        def further(eng, start, body):
            eng.wait_ge(visits_s, 1)
            n = eng.value_load(visit_i[0:1, 2, 0:1], min_val=0, max_val=MAX_EXTRA)
            with eng.If(n > 0):
                start()
                with eng.Fori(0, n) as j:
                    column = eng.value_load(visit_i[0:1, 0, ds(j, 1)], min_val=0, max_val=ROUNDS * NE - 1)
                    e = eng.value_load(visit_i[0:1, 1, ds(j, 1)], min_val=0, max_val=NE - 1)
                    body(j, column, e)
            return n

        block = ctx.enter_context(nc.Block())

        @block.sync
        def _(sp):
            def leave(sp, n):
                if n - SLOTS >= NCH - 1:
                    sp.wait_ge(acc_s, 1)
                elif n >= SLOTS:
                    sp.wait_ge(filled, last_fill(chunks[n - SLOTS]) + 1)

            for t in range(NT):
                sp.dma_start(xin[:, t, :], xv[:, t, :]).then_inc(x_in[t], 16)
            for n, c in enumerate(chunks):
                leave(sp, n)
                if n == 3:
                    sp.dma_start(pos_i[:, :], posv, allow_slow_non_contiguous=True).then_inc(small_in, 16)
                    sp.dma_start(gq_bc[:, :], g_qnorm[0, :].partition_broadcast(P)).then_inc(small_in, 16)
                    sp.dma_start(gk_bc[:, :], g_knorm[0, :].partition_broadcast(P)).then_inc(small_in, 16)
                    sp.dma_start(br_bc[:, :], b_router[0, :].partition_broadcast(P)).then_inc(small_in, 16)
                dst, src = chunk(c)
                sp.dma_start(dst, src).then_inc(loaded[n % SLOTS], 16)
            for kind in ("a", "b"):
                for k in range(4):
                    leave(sp, NCH + 4 * PASSES.index(kind) + k)
                    s, arrived, _ = arrival(0, kind, k)
                    load_chunk(sp, kind, k, 0, s, arrived)

            def again_chunk(i, kind, k, before_kind=None):
                sp.wait_ge(main.w_used, first_chunk(i - 1, before_kind or kind) + k + 1)
                s, arrived, _ = arrival(i, kind, k)
                load_chunk(sp, kind, k, i - (kind == "d"), s, arrived)

            def first_down(k):
                leave(sp, NCH + 8 + k)
                s, arrived, _ = arrival(1, "d", k)
                load_chunk(sp, "d", k, 0, s, arrived)
            for k in range(3):
                first_down(k)
            for kind in ("a", "b"):
                for k in range(4):
                    again_chunk(1, kind, k)
            first_down(3)
            with sp.Fori(2, NE) as i:
                for kind in PASSES:
                    for k in range(4):
                        again_chunk(i, kind, k)
            for k in range(4):
                again_chunk(NE, "d", k, "a")

            def start():
                sp.wait_ge(last_s, 2 * NT)

            def load_again(j, column, e):
                sp.wait_ge(extra.summed, j + extra.spare)
                for kind in PASSES:
                    for k in range(4):
                        load_chunk(sp, kind, k, e, expert_slot(kind, k), again[4 * PASSES.index(kind) + k])
            further(sp, start, load_again)

            for t in range(NT):
                sp.wait_ge(out_s, 2 * (t + 1))
                sp.dma_start(ov[:, t, :], xin[:, t, :]).then_inc(out_done, 16)
            sp.wait_ge(out_done, 16 * NT)

        @block.gpsimd
        def _(pool):
            def const(ins):
                const.n += 1
                ins.then_inc(consts, 1)
                pool.wait_ge(consts, const.n)
            const.n = 0
            const(pool.memset(ident[:, :], 0.0))
            const(pool.affine_select(out=ident[:, :], in_=ident[:, :], compare_op=ALU.not_equal, fill=1.0,
                                     base=0, pattern=[[-1, P]], channel_multiplier=1))
            const(pool.memset(ones[:, :], 1.0))
            for i in range(HALF):
                f = float(np.float32(THETA) ** (-np.float32(i) / np.float32(HALF)))
                const(pool.memset(inv_freq[:, i:i + 1], f))
            const(pool.memset(neg_ones[:, :], -1.0))
            const(pool.affine_select(out=before[:, :], in_=ones[:, :], compare_op=ALU.is_gt, fill=0.0,
                                     base=0, pattern=[[1, P]], channel_multiplier=-1))
            const(pool.affine_select(out=neg_from[:, :], in_=neg_ones[:, :], compare_op=ALU.is_ge, fill=0.0,
                                     base=0, pattern=[[-1, P]], channel_multiplier=1))
            const(pool.memset(cap_mask[:, :], 0.0))
            for c in (0, 256):
                const(pool.affine_select(out=cap_mask[:, c:c + P], in_=cap_mask[:, c:c + P],
                                         compare_op=ALU.is_gt, fill=-1.0e5, base=0, pattern=[[1, P]],
                                         channel_multiplier=-1))
            const(pool.memset(row_lo[:, :], 0.0))
            const(pool.memset(col_hi[:, :], 0.0))
            const(pool.memset(row_lo[0:1, 0:CHUNK], 1.0))
            const(pool.memset(col_hi[0:1, CHUNK:P], NEG))
            const(pool.memset(fold[:, :], 0.0))
            for b in (0, COLS):
                const(pool.affine_select(out=fold[:, :], in_=fold[:, :], compare_op=ALU.not_equal, fill=1.0,
                                         base=-b, pattern=[[-1, COLS]], channel_multiplier=1))
            const(pool.memset(slot_no[:, :, :], 1.0e6))
            const(pool.iota(slot_no[:, :, 0:CAP], pattern=[[0, 2], [1, CAP]], base=0, channel_multiplier=0,
                            allow_small_or_imprecise_dtypes=True))
            assert const.n == CONSTS, const.n

            steps = [0]

            def link(ins):
                steps[0] += 1
                ins.then_inc(pool_s, 1)
                pool.wait_ge(pool_s, steps[0])

            pool.wait_ge(count_s, 1)
            W = (ROUNDS - 1) * NE
            link(pool.iota(codes[:, 0, :], pattern=[[1, W]], base=NE, channel_multiplier=0,
                           allow_small_or_imprecise_dtypes=True))
            link(pool.iota(codes[:, 1, :], pattern=[[0, ROUNDS - 1], [1, NE]], base=0, channel_multiplier=0,
                           allow_small_or_imprecise_dtypes=True))
            for r in range(1, ROUNDS):
                c = NE * (r - 1)
                last = pool.tensor_scalar(more[:, 0, c:c + NE], count[0:1, :], float(CAP * r), None, ALU.is_gt)
            link(last)
            link(pool.tensor_copy(more[:, 1, :], more[:, 0, :]))
            a, b, shift = 1, 2, 1
            while shift < W:
                pool.tensor_copy(more[:, b, 0:shift], more[:, a, 0:shift])
                link(pool.tensor_tensor(more[:, b, shift:W], more[:, a, shift:W], more[:, a, 0:W - shift], ALU.add))
                a, b, shift = b, a, 2 * shift
            link(pool.tensor_copy(visit_f[:, 2, :], more[:, a, W - 1:W].to_broadcast([1, MAX_EXTRA])))
            link(pool.tensor_tensor(more[:, a, :], more[:, a, :], more[:, 0, :], ALU.mult))
            for v in range(MAX_EXTRA):
                for i in range(2):
                    link(pool.tensor_scalar(found[:, :], more[:, a, :], float(v + 1), None, ALU.is_equal))
                    link(pool.tensor_tensor(found[:, :], found[:, :], codes[:, i, :], ALU.mult))
                    link(pool.tensor_reduce(visit_f[:, i, v:v + 1], found[:, :], AX.XYZWC, ALU.add))
            pool.tensor_copy(visit_i[:, :, :], visit_f[:, :, :]).then_inc(visits_s, 1)

        @block.scalar
        def _(act):
            act.preload_act_table(ACT.Sqrt)
            act.dma_start(gains[0:KD, :], g_mix.rearrange("l (k p) -> (l k) p", p=P)).then_inc(gains_in, 16)
            act.dma_start(gains[KD:KD + QT, :], g_cq.rearrange("l (k p) -> (l k) p", p=P)).then_inc(gains_in, 16)
            act.dma_start(gains[KD + QT:, :], g_ckv.rearrange("l (k p) -> (l k) p", p=P)).then_inc(gains_in, 16)

            steps = [0]

            def link(ins):
                steps[0] += 1
                ins.then_inc(act_s, 1)
                act.wait_ge(act_s, steps[0])

            def root(i):
                a, b = RMS[i]
                act.wait_ge(recip_s, i + 1)
                act.activation(inv[:, a:b], inv[:, a:b], ACT.Sqrt).then_inc(root_s, 1)

            for t in range(NT):
                act.wait_ge(x_in[t], 16)
                act.activation(hn[:, t, :], xin[:, t, :], ACT.Square, accum_out=st[:, t:t + 1]).then_inc(ssq_s, 1)
            root(0)
            act.wait_ge(gt_ps, 1)
            act.activation(gT[:, :], ps[:, 7, 0:KD + QT + KVT], ACT.Copy).then_inc(gt_s, 1)
            act.wait_ge(gt_s, 1)
            for n in (0, 2):
                act.wait_ge(filled, FILL_X + n + 1)
                for i in range(2):
                    k = 2 * n + i
                    last = act.activation(hT[:, k, :], bank(n)[:, SEQ * i:SEQ * i + SEQ], ACT.Copy,
                                          scale=gT[:, k:k + 1])
                last.then_inc(emptied[n % 2], 1)
            for n in range(3):
                b = bank(FILL_LAT + n)
                act.wait_ge(filled, FILL_LAT + n + 1)
                w = 2 if n < 2 else 1
                act.activation(sqT[:, 2 * n:2 * n + w, :], b[:, 0:w * SEQ].rearrange("p (j s) -> p j s", j=w),
                               ACT.Square)
                if n == 2:
                    act.activation(kr[:, :, :], b[:, SEQ:SEQ + NT * ROPE].rearrange("p (t d) -> p t d", t=NT),
                                   ACT.Copy)
                for i in range(w):
                    j = 2 * n + i
                    last = act.activation(cT[:, j, :], b[:, SEQ * i:SEQ * i + SEQ], ACT.Copy,
                                          scale=gT[:, KD + j:KD + j + 1])
                last.then_inc(emptied[(FILL_LAT + n) % 2], 1)
            root(1)
            act.wait_ge(red_s, 1)
            act.activation(cs[:, :, :, :], red[:, :, :, :], ACT.Sin).then_inc(cs_s, 1)
            act.wait_ge(lat_rs, 1)
            for m in range(8):
                n = FILL_UP + m
                if n % 2:
                    continue
                act.wait_ge(filled, n + 1)
                dst, src, scale = up_piece(m)
                act.activation(dst, src, ACT.Copy, scale=scale).then_inc(emptied[0], 1)
            for m in range(6):
                if m in (1, 3):
                    root(m // 2 + 2)
                n = FILL_QKV + m
                act.wait_ge(filled, n + 1)
                src = bank(n).rearrange("p (j s) -> p j s", j=2)
                if m < 2:
                    ins = act.activation(qT[:, 2 * m:2 * m + 2, :], src, ACT.Copy, scale=DH ** -0.5)
                elif m < 4:
                    ins = act.activation(kT[:, 2 * m - 4:2 * m - 2, :], src, ACT.Copy)
                else:
                    ins = act.activation(v_sb[:, :, 256 * (m - 4):256 * (m - 4) + 256], src, ACT.Copy)
                ins.then_inc(emptied[n % 2], 1)
            for h in range(0, HEADS, 2):
                act.wait_ge(turn_s, h + 1)
                act.activation(qkT[0:DQK, h, :, :], ps[0:DQK, TURN[h % 4], :].rearrange("p (a s) -> p a s", a=2),
                               ACT.Copy).then_inc(turn_e[h % 4], 1)
            act.preload_act_table_set("natural_log_exp_and_others")
            for h in range(HEADS):
                e = stick[:, h % 2, :]
                act.wait_ge(bound_s, h + 1)
                link(act.activation(e, e, ACT.Exp))
                act.activation(e, e, ACT.Ln, bias=1.0).then_inc(ln_s, 1)
                act.wait_ge(max_s, h + 1)
                act.activation(prob[:, h % 2, 0:P], ps[:, 5, 0:P], ACT.Exp, scale=DQK ** -0.5,
                               bias=st[:, 36:37], accum_out=st[:, 40:41])
                act.activation(prob[:, h % 2, P:384], ps[:, 5, P:384], ACT.Exp, scale=DQK ** -0.5,
                               bias=st[:, 37:38], accum_out=st[:, 41:42]).then_inc(p_s, 1)
                act.wait_ge(cap_s, h + 1)
                act.activation(stay[:, h % 2, :], stay[:, h % 2, :], ACT.Exp).then_inc(a_s, 1)
                act.wait_ge(pt_s, h + 1)
                if h >= 2:
                    act.wait_ge(mv_s, h - 1)
                act.activation(probT[:, h % 2, :], ps[:, 6, 0:384], ACT.Copy).then_inc(pte_s, 1)
                n = FILL_GATE + h
                act.wait_ge(filled, n + 1)
                act.activation(gates[:, h - h % 2:h - h % 2 + 2, h % 2, :], bank(n).rearrange("p (j s) -> p j s", j=2),
                               ACT.Copy).then_inc(emptied[n % 2], 1)
                if h % 2:
                    j = h // 2
                    act.wait_ge(av_s, h + 1)
                    act.wait_ge(mv_s, h + 1)
                    c = SEQ * (j % 2)
                    act.activation(o_sb[:, j, :], ps[:, 4, c:c + SEQ], ACT.Copy)
                    act.activation(o_mla_sb[:, j, :], ps[:, 7, c:c + SEQ], ACT.Copy).then_inc(oe_s, 1)
            act.wait_ge(emptied[0], FILL_BUP // 2 + 1)
            act.wait_ge(emptied[1], FILL_BUP // 2)
            act.activation(gates[:, :, :, :], gates[:, :, :, :], ACT.Sigmoid).then_inc(mix_s, 1)
            n = FILL_BUP
            act.wait_ge(filled, n + 1)
            act.activation(b_upT[:, :, :, :, :], bank(n).rearrange("p (a b j e) -> p a b j e", a=2, b=2, j=4),
                           ACT.Copy).then_inc(emptied[n % 2], 1)
            act.dma_start(g_ffn_bc, g_ffn[0, :].partition_broadcast(P)).then_inc(gffn_in, 16)
            act.preload_act_table(ACT.Sqrt)
            for i in range(4):
                act.wait_ge(x1_s, i + 1)
                for t in range(NT):
                    c = 120 + 4 * t + i
                    last = act.activation(hn[:, t, 256 * i:256 * i + 256], xin[:, t, 256 * i:256 * i + 256],
                                          ACT.Square, accum_out=st[:, c:c + 1])
                last.then_inc(sum_in, 1)
            root(4)
            for n in (FILL_H2, FILL_H2 + 2):
                act.wait_ge(filled, n + 1)
                k = 2 * (n - FILL_H2)
                act.activation(h2T[:, k:k + 2, :], bank(n).rearrange("p (j s) -> p j s", j=2), ACT.Copy
                               ).then_inc(emptied[0], 1)
            act.wait_ge(filled, FILL_LOGIT + 1)
            hi(act, 0, "a", 0)
            hi(act, 0, "a", 1)
            act.wait_ge(top_s, 1)
            act.activation(expl[:, :, :], expl[:, :, :], ACT.Exp).then_inc(expl_s, 1)
            for kind, k in (("a", 2), ("a", 3), ("b", 0), ("b", 1)):
                hi(act, 0, kind, k)
            tokens_hi(act, main, 0)
            act.wait_ge(gwt_ps, 1)
            act.activation(gate_wT[:, :], ps[0:NE, 3, 0:SEQ], ACT.Copy).then_inc(wt_s, 1)
            hi(act, 0, "b", 2)
            copy_up(act, main, 0, 0, first_chunk(0, "a") + 4)
            hi(act, 0, "b", 3)
            copy_up(act, main, 1, 0, first_chunk(0, "b") + 4)
            tokens_hi(act, main, 1)
            act_body(act, 1, before2=False)
            with act.Fori(2, NE - 1) as i:
                act_body(act, i)
            w, v = NE - 2, NE - 1
            act_up_passes(act, v)
            hi(act, v, "d", 3)
            sigmoid(act, main, 2 * v)
            hi(act, NE, "d", 0)
            act.wait_ge(main.w_used, first_chunk(v, "d") + 2)
            act_hi(act, main, 0, 2 * v)
            hi(act, NE, "d", 1)
            hi(act, NE, "d", 2)
            copy_down(act, main, w, first_chunk(v, "d") + 4)
            copy_put(act, main, w)
            sigmoid(act, main, 2 * v + 1)
            hi(act, NE, "d", 3)
            act_hi(act, main, 1, 2 * v + 1)
            copy_put(act, main, v)
            copy_down(act, main, v, first_chunk(NE, "d") + 4)

            def start():
                act.sem_inc(extra.p_read, 1)
                act.sem_inc(extra.ht_hi, 1)
                act.sem_inc(extra.putT, 1)

            def visit(j, column, e):
                def hi(kind):
                    for k in range(4):
                        c = 4 * PASSES.index(kind) + k
                        split_hi(act, extra, expert_slot(kind, k), 12 * j + c, c % RING, again[c], j + 1)
                tokens_hi(act, extra, j)
                hi("a")
                copy_up(act, extra, 0, j, 12 * j + 4)
                hi("b")
                sigmoid(act, extra, 2 * j)
                act_hi(act, extra, 0, 2 * j)
                copy_up(act, extra, 1, j, 12 * j + 8)
                sigmoid(act, extra, 2 * j + 1)
                act_hi(act, extra, 1, 2 * j + 1)
                hi("d")
                copy_down(act, extra, j, 12 * j + 12)
                copy_put(act, extra, j)
            further(act, start, visit)

        @block.vector
        def _(dve):
            steps = [0]

            def link(ins):
                steps[0] += 1
                ins.then_inc(dve_s, 1)
                dve.wait_ge(dve_s, steps[0])

            def rstd(i, parts, ready=None):
                a, b = RMS[i]
                v, y, t = var[:, a:b], inv[:, a:b], half_vy[:, a:b]
                for src, width, c0, c1 in parts:
                    last = dve.tensor_scalar(var[:, c0:c1], src, 1.0 / width, EPS, ALU.mult, ALU.add)
                link(last)
                dve.reciprocal(y, v).then_inc(recip_s, 1)
                dve.wait_ge(root_s, i + 1)
                link(dve.scalar_tensor_tensor(out=t, in0=v, scalar=-0.5, in1=y, op0=ALU.mult, op1=ALU.mult))
                link(dve.tensor_tensor(t, t, y, ALU.mult))
                ins = dve.scalar_tensor_tensor(out=y, in0=t, scalar=1.5, in1=y, op0=ALU.add, op1=ALU.mult)
                if ready is None:
                    link(ins)
                else:
                    ins.then_inc(ready, 1)

            dve.wait_ge(ssq_s, NT)
            for t in range(NT):
                dve.wait_ge(x_in[t], 16)
            rstd(0, ((st[:, 0:2], D, 0, 2),))
            for t in range(NT):
                dve.tensor_scalar(hn[:, t, :], xin[:, t, :], inv[:, t:t + 1], None, ALU.mult).then_inc(xhat_s, 1)
            dve.wait_ge(gt_s, 1)
            for n in (1, 3):
                dve.wait_ge(filled, FILL_X + n + 1)
                for i in range(2):
                    k = 2 * n + i
                    last = dve.tensor_scalar(hT[:, k, :], bank(n)[:, SEQ * i:SEQ * i + SEQ], gT[:, k:k + 1], None,
                                             ALU.mult)
                last.then_inc(emptied[1], 1)
            dve.wait_ge(small_in, 16 * 4)
            dve.wait_ge(consts, CONSTS)
            link(dve.tensor_copy(pos_f[:, :], pos_i[:, :]))
            for t in range(NT):
                last = dve.tensor_scalar(ang[:, t, :], inv_freq[:, :], pos_f[:, t:t + 1], None, ALU.mult)
            link(last)
            dve.tensor_scalar(turns[:, 0, :, :], ang[:, :, :], 1.0 / (2 * math.pi), None, ALU.mult)
            link(dve.tensor_scalar(turns[:, 1, :, :], ang[:, :, :], 1.0 / (2 * math.pi), 0.25, ALU.mult, ALU.add))
            link(dve.tensor_scalar(turns[:, :, :, :], turns[:, :, :, :], ROUNDER, ROUNDER, ALU.add, ALU.subtract))
            for a in range(2):
                last = dve.scalar_tensor_tensor(out=red[:, a, :, :], in0=turns[:, a, :, :], scalar=-TWO_PI_1,
                                                in1=ang[:, :, :], op0=ALU.mult, op1=ALU.add)
            link(last)
            for part in (TWO_PI_2, TWO_PI_3):
                link(dve.scalar_tensor_tensor(out=red[:, :, :, :], in0=turns[:, :, :, :], scalar=-part,
                                              in1=red[:, :, :, :], op0=ALU.mult, op1=ALU.add))
            link(dve.tensor_scalar(red[:, 1, :, :], red[:, 1, :, :], math.pi / 2, None, ALU.add))
            lim = 3.1415925
            dve.tensor_scalar(red[:, :, :, :], red[:, :, :, :], lim, -lim, ALU.min, ALU.max).then_inc(red_s, 1)
            dve.wait_ge(lat_ss, 1)
            rstd(1, ((ps[:, 7, 0:2], CQ, 2, 4), (ps[:, 7, 2:4], CKV, 4, 6)), lat_rs)
            dve.wait_ge(lat_rs, 1)
            for m in range(8):
                n = FILL_UP + m
                if n % 2 == 0:
                    continue
                dve.wait_ge(filled, n + 1)
                dst, src, scale = up_piece(m)
                dve.tensor_scalar(dst, src, scale, None, ALU.mult).then_inc(emptied[1], 1)
            sq = qkT[:, :, :, :].rearrange("p h a s -> p (h a s)")
            qf = q_mla[:, :, :, :].rearrange("p t h d -> p (t h) d")
            sqq = sq[:, 0:NT * HEADS * DQK].rearrange("p (h d) -> p h d", d=DQK)
            dve.wait_ge(emptied[0], (FILL_QKV + 1) // 2)
            dve.wait_ge(emptied[1], FILL_QKV // 2)
            link(dve.tensor_tensor(sqq, qf, qf, ALU.mult))
            link(dve.tensor_reduce(st[:, 48:64], sqq, AX.X, ALU.add))
            rstd(2, ((st[:, 48:64], DQK, 6, 22),))
            link(dve.tensor_tensor(qf, qf, inv[:, 6:22].unsqueeze(2).to_broadcast([P, 16, DQK]), ALU.mult))
            link(dve.tensor_tensor(qf, qf, gq_bc[:, :].unsqueeze(1).to_broadcast([P, 16, DQK]), ALU.mult))
            dve.wait_ge(cs_s, 1)
            t4 = sq[:, 2048:4096].rearrange("p (a t h d) -> p a t h d", a=8, t=NT, h=HEADS)

            def rotate(vec, heads, ready):
                def trig(a, t):
                    c = cs[:, a, t, :]
                    return c.unsqueeze(1).to_broadcast([P, heads, HALF]) if heads else c
                for t in range(NT):
                    tmp = [t4[:, i, t, :, :] if heads else t4[:, i, t, 0, :] for i in range(4)]
                    x1, x2 = (vec[:, t, :, 0:HALF], vec[:, t, :, HALF:ROPE]) if heads else (
                        vec[:, t, 0:HALF], vec[:, t, HALF:ROPE])
                    dve.tensor_tensor(tmp[0], x1, trig(1, t), ALU.mult)
                    dve.tensor_tensor(tmp[1], x2, trig(0, t), ALU.mult)
                    dve.tensor_tensor(tmp[2], x2, trig(1, t), ALU.mult)
                    link(dve.tensor_tensor(tmp[3], x1, trig(0, t), ALU.mult))
                    dve.tensor_tensor(x1, tmp[0], tmp[1], ALU.subtract)
                    ins = dve.tensor_tensor(x2, tmp[2], tmp[3], ALU.add)
                    if ready is not None and t == NT - 1:
                        ins.then_inc(ready, 1)
                    else:
                        link(ins)

            rotate(q_mla[:, :, :, DH:DQK], HEADS, mla_q_s)
            sqk = sq[:, 0:NT * HEADS * DH].rearrange("p (t h d) -> p t h d", t=NT, h=HEADS)
            for t in range(NT):
                last = dve.tensor_tensor(sqk[:, t, :, :], kv[:, t, :, 0:DH], kv[:, t, :, 0:DH], ALU.mult)
            link(last)
            link(dve.tensor_reduce(st[:, 80:96], sqk.rearrange("p t h d -> p (t h) d"), AX.X, ALU.add))
            sqr = sq[:, 1024:1024 + NT * ROPE].rearrange("p (t d) -> p t d", t=NT)
            link(dve.tensor_tensor(sqr, kr[:, :, :], kr[:, :, :], ALU.mult))
            link(dve.tensor_reduce(st[:, 96:98], sqr, AX.X, ALU.add))
            for t in range(NT):
                last = dve.tensor_scalar(st[:, 80 + 8 * t:88 + 8 * t], st[:, 80 + 8 * t:88 + 8 * t],
                                         st[:, 96 + t:97 + t], None, ALU.add)
            link(last)
            rstd(3, ((st[:, 80:96], DQK, 22, 38),))
            link(dve.tensor_tensor(krr[:, :, :], kr[:, :, :], gk_bc[:, DH:DQK].unsqueeze(1).to_broadcast([P, NT, ROPE]),
                                   ALU.mult))
            rotate(krr, 0, None)
            dve.wait_ge(filled, FILL_X + 4)
            for t in range(NT):
                rk = inv[:, 22 + 8 * t:30 + 8 * t].unsqueeze(2)
                dve.tensor_tensor(k_mla[:, t, :, 0:DH], kv[:, t, :, 0:DH], rk.to_broadcast([P, HEADS, DH]), ALU.mult)
                link(dve.tensor_tensor(k_mla[:, t, :, DH:DQK], krr[:, t, :].unsqueeze(1).to_broadcast([P, HEADS, ROPE]),
                                       rk.to_broadcast([P, HEADS, ROPE]), ALU.mult))
                ins = dve.tensor_tensor(k_mla[:, t, :, 0:DH], k_mla[:, t, :, 0:DH],
                                        gk_bc[:, 0:DH].unsqueeze(1).to_broadcast([P, HEADS, DH]), ALU.mult)
                ins.then_inc(mla_k_s, 1)
            for h in range(1, HEADS, 2):
                dve.wait_ge(turn_s, h + 1)
                if h == 1:
                    dve.wait_ge(mla_k_s, 2)
                dve.tensor_copy(qkT[0:DQK, h, :, :], ps[0:DQK, TURN[h % 4], :].rearrange("p (a s) -> p a s", a=2)
                                ).then_inc(turn_e[h % 4], 1)
            for h in range(HEADS):
                zb = ps[:, 2 + h % 2, 0:384]
                e, w = stick[:, h % 2, :], stay[:, h % 2, :]
                dve.wait_ge(z_s, h + 1)
                dve.tensor_scalar(e, zb, 40.0, None, ALU.min).then_inc(bound_s, 1)
                dve.wait_ge(s_s, h + 1)
                if h:
                    dve.wait_ge(p_s, h)
                dve.tensor_reduce(st[:, 32:33], ps[:, 5, 0:P], AX.X, ALU.max)
                link(dve.tensor_reduce(st[:, 33:34], ps[:, 5, P:384], AX.X, ALU.max))
                dve.tensor_scalar(st[:, 36:38], st[:, 32:34], -DQK ** -0.5, None, ALU.mult).then_inc(max_s, 1)
                dve.wait_ge(ln_s, h + 1)
                link(dve.tensor_tensor(e, zb, e, ALU.max))
                diag = e.rearrange("p (c s) -> p c s", c=3)[:, 0:3:2, :]
                dve.tensor_tensor(diag, diag, before[:, :].unsqueeze(1).to_broadcast([P, 2, P]),
                                  ALU.mult).then_inc(sp_s, 1)
                dve.wait_ge(p_s, h + 1)
                link(dve.reciprocal(st[:, 44:46], st[:, 40:42]))
                dve.tensor_scalar(prob[:, h % 2, 0:P], prob[:, h % 2, 0:P], st[:, 44:45], None, ALU.mult)
                dve.tensor_scalar(prob[:, h % 2, P:384], prob[:, h % 2, P:384], st[:, 45:46], None,
                                  ALU.mult).then_inc(pn_s, 1)
                dve.wait_ge(r_s, h + 1)
                if h >= 2:
                    dve.wait_ge(av_s, h - 1)
                dve.tensor_tensor(w, zb, cap_mask[:, :], ALU.min).then_inc(cap_s, 1)
            dve.wait_ge(mix_s, 1)
            tmp = stick[:, :, 0:SEQ]
            for m in range(KD):
                n = FILL_MIX + m
                dve.wait_ge(filled, n + 1)
                dve.tensor_tensor(gates[:, m, :, :], gates[:, m, :, :], bank(n).rearrange("p (a s) -> p a s", a=2),
                                  ALU.mult).then_inc(emptied[n % 2], 1)
                dve.wait_ge(emptied[n % 2], n // 2 + 1)
                dve.tensor_tensor(gates[:, m, 0, :], gates[:, m, 0, :], gates[:, m, 1, :], ALU.add).then_inc(mix_s, 1)
            for i in range(4):
                n = FILL_OUT + i
                dve.wait_ge(filled, n + 1)
                xs = xin[:, :, 256 * i:256 * i + 256]
                dve.tensor_tensor(xs, xs, bank(n).rearrange("p (t s) -> p t s", t=NT), ALU.add).then_inc(
                    emptied[n % 2], 1)
                dve.wait_ge(emptied[n % 2], n // 2 + 1)
                dve.sem_inc(x1_s, 1)
            dve.memset(lg[:, :, NE:NE + 4], -BIG_RANK)
            link(dve.memset(key[:, :, TOPK:8], -BIG_RANK))
            dve.wait_ge(sum_in, 4)
            link(dve.tensor_reduce(st[:, 128:130], st[:, 120:128].rearrange("p (t i) -> p t i", t=NT), AX.X, ALU.add))
            rstd(4, ((st[:, 128:130], D, 38, 40),))
            dve.wait_ge(gffn_in, 16)
            for c in (0, 512):
                for t in range(NT):
                    dve.scalar_tensor_tensor(out=hn[:, t, c:c + 512], in0=xin[:, t, c:c + 512],
                                             scalar=inv[:, 38 + t:39 + t], in1=g_ffn_bc[:, c:c + 512],
                                             op0=ALU.mult, op1=ALU.mult).then_inc(h2_s, 1)
            for n in (FILL_H2 + 1, FILL_H2 + 3):
                dve.wait_ge(filled, n + 1)
                k = 2 * (n - FILL_H2)
                dve.tensor_copy(h2T[:, k:k + 2, :], bank(n).rearrange("p (j s) -> p j s", j=2)).then_inc(emptied[1], 1)
            n = FILL_LOGIT
            dve.wait_ge(filled, n + 1)
            dve.tensor_tensor(lg[:, :, 0:NE], bank(n)[:, 0:NT * NE].rearrange("p (t e) -> p t e", t=NT),
                              br_bc[:, :].unsqueeze(1).to_broadcast([P, NT, NE]), ALU.add).then_inc(emptied[0], 1)
            dve.wait_ge(emptied[0], n // 2 + 1)
            for t in range(NT):
                last = dve.max(top[:, t, :], lg[:, t, 0:NE])
            link(last)
            link(dve.tensor_copy(key[:, :, 0:TOPK], top[:, :, 0:TOPK]))
            for t in range(NT):
                last = dve.match_replace(marked[:, t, :], key[:, t, :], lg[:, t, :], BIG_RANK)
            link(last)
            dve.tensor_scalar(chosen[:, :, :], marked[:, :, 0:NE], BIG_RANK, None, ALU.is_ge).then_inc(chosen_s, 1)
            for t in range(NT):
                last = dve.tensor_scalar(expl[:, t, :], lg[:, t, 0:NE], top[:, t, 0:1], None, ALU.subtract)
            last.then_inc(top_s, 1)
            dve.wait_ge(chosen_s, 1)
            lo(dve, 0, "a", 0)
            n = FILL_RANK
            dve.wait_ge(filled, n + 1)
            pos = bank(n)[:, 0:NT * NE].rearrange("p (t e) -> p t e", t=NT)
            link(dve.scalar_tensor_tensor(out=rank_in[:, :, 0, :], in0=pos, scalar=1.0, in1=chosen[:, :, :],
                                          op0=ALU.add, op1=ALU.mult))
            link(dve.tensor_scalar(rank_in[:, :, 0, :], rank_in[:, :, 0, :], -1.0, None, ALU.add))
            build_pick(dve, main, 0, 0)
            for r in range(1, ROUNDS):
                dve.tensor_scalar(rank_in[:, :, r, :], rank_in[:, :, 0, :], -CAP * r, None, ALU.add)
            dve.tensor_copy(count[:, :], bank(n)[:, NT * NE:NT * NE + NE]).then_inc(count_s, 1)
            lo(dve, 0, "a", 1)
            dve.wait_ge(expl_s, 1)
            link(dve.tensor_tensor(expl[:, :, :], expl[:, :, :], chosen[:, :, :], ALU.mult))
            link(dve.tensor_reduce(st[:, 132:134], expl[:, :, :], AX.X, ALU.add))
            link(dve.reciprocal(st[:, 134:136], st[:, 132:134]))
            for t in range(NT):
                last = dve.tensor_scalar(gate_w[:, t, :], expl[:, t, :], st[:, 134 + t:135 + t], None, ALU.mult)
            last.then_inc(gw_s, 1)
            dve.wait_ge(gw_s, 1)
            lo(dve, 0, "a", 2)
            lo(dve, 0, "a", 3)
            tokens_lo(dve, main, 0)
            lo(dve, 0, "b", 0)
            build_pick(dve, main, 1, 1)
            for k in range(1, 4):
                lo(dve, 0, "b", k)
            tokens_lo(dve, main, 1)
            dve_body(dve, 1)
            with dve.Fori(2, NE - 1) as i:
                dve_body(dve, i)
            v = NE - 1
            dve_up_passes(dve, v, False)
            gate_up(dve, main, 0, 2 * v, v)
            lo(dve, v, "d", 2)
            times_sigmoid(dve, main, 2 * v)
            lo(dve, v, "d", 3)
            act_lo(dve, main, 0, 2 * v)
            for k in range(3):
                lo(dve, NE, "d", k)
            build_put(dve, main, v, v, v)
            gate_up(dve, main, 1, 2 * v + 1, v)
            times_sigmoid(dve, main, 2 * v + 1)
            lo(dve, NE, "d", 3)
            act_lo(dve, main, 1, 2 * v + 1)

            def start():
                dve.sem_inc(extra.ht_lo, 1)
                dve.sem_inc(extra.u, 1)

            def visit(j, column, e):
                def lo(kind):
                    for k in range(4):
                        c = 4 * PASSES.index(kind) + k
                        split_lo(dve, extra, expert_slot(kind, k), 12 * j + c, c % RING, again[c], j + 1)
                build_pick(dve, extra, j, column)
                tokens_lo(dve, extra, j)
                lo("a")
                lo("b")
                for half in range(2):
                    m = 2 * j + half
                    gate_up(dve, extra, half, m, e)
                    times_sigmoid(dve, extra, m)
                    act_lo(dve, extra, half, m)
                build_put(dve, extra, j, column, e)
                lo("d")
                dve.wait_ge(extra.summed, j + 1 + extra.spare)
            further(dve, start, visit)
            for t in range(NT):
                for b in range(2):
                    dve.wait_ge(last_s, 2 * t + b + 1)
                    xs = xin[:, t, 512 * b:512 * b + 512]
                    dve.tensor_tensor(xs, xs, ps[:, 4 + 2 * t + b, :], ALU.add).then_inc(out_s, 1)

        @block.tensor
        def _(pe):
            def fill(n):
                if n >= 2:
                    pe.wait_ge(emptied[n % 2], n // 2)

            def weights(c):
                n = number[c]
                pe.wait_ge(loaded[n % SLOTS], 16 * (n // SLOTS + 1))
                return chunk(c)[0]

            pe.wait_ge(consts, 3)
            pe.wait_ge(gains_in, 16 * 3)
            pe.transpose(ps[:, 7, 0:KD + QT + KVT], gains[:, :], ident[0:KD + QT + KVT, 0:KD + QT + KVT]
                         ).then_inc(gt_ps, 1)
            pe.wait_ge(xhat_s, NT)
            for n in range(4):
                fill(n)
                for i in range(2):
                    for t in range(NT):
                        k = 2 * n + i
                        mm = pe.transpose(bank(n)[:, SEQ * i + P * t:SEQ * i + P * t + P], hn[:, t, P * k:P * k + P],
                                          ident[:, :])
                mm.then_inc(filled, 1)
            for b in range(2):
                pe.wait_ge(emptied[b], 2)

            def turned(n, i, w, c0):
                for k in range(KD):
                    mm = pe.matmul(bank(n)[:, SEQ * i:SEQ * i + SEQ], w[:, k, c0:c0 + P], hT[:, k, :],
                                   start=k == 0, stop=k == KD - 1)
                return mm

            for i in range(3):
                n = FILL_LAT + i
                fill(n)
                w = weights(("lat", i))
                mm = turned(n, 0, w, 0)
                if i < 2:
                    mm = turned(n, 1, w, P)
                else:
                    for t in range(NT):
                        for k in range(KD):
                            mm = pe.matmul(bank(n)[:, SEQ + ROPE * t:SEQ + ROPE * t + ROPE], hT[:, k, P * t:P * t + P],
                                           w[:, k, P:P + ROPE], start=k == 0, stop=k == KD - 1)
                mm.then_inc(filled, 1)
            pe.wait_ge(emptied[0], 4)
            pe.wait_ge(emptied[1], 3)
            for c, (j0, j1) in enumerate(((0, QT), (QT, QT + KVT))):
                for t in range(NT):
                    for j in range(j0, j1):
                        mm = pe.matmul(ps[:, 7, 2 * c + t:2 * c + t + 1], sqT[:, j, P * t:P * t + P], ones[:, 0:1],
                                       start=j == j0, stop=j == j1 - 1)
            mm.then_inc(lat_ss, 1)
            for i in range(2):
                w = weights(("uq", i))
                for t in range(NT):
                    n = FILL_UP + 2 * i + t
                    fill(n)
                    for k in range(QT):
                        mm = pe.matmul(bank(n)[:, 0:384], cT[:, k, P * t:P * t + P], w[:, k, :],
                                       start=k == 0, stop=k == QT - 1)
                    mm.then_inc(filled, 1)
            w = weights(("ukv", 0))
            for t in range(NT):
                for i in range(2):
                    n = FILL_UP + 4 + 2 * t + i
                    fill(n)
                    for k in range(KVT):
                        mm = pe.matmul(bank(n), cT[:, QT + k, P * t:P * t + P], w[:, k, 512 * i:512 * i + 512],
                                       start=k == 0, stop=k == KVT - 1)
                    mm.then_inc(filled, 1)
            for m in range(6):
                n = FILL_QKV + m
                fill(n)
                w = weights(("qkv", m))
                if m < 4:
                    turned(n, 0, w, 0)
                    mm = turned(n, 1, w, P)
                else:
                    for t in range(NT):
                        for k in range(KD):
                            mm = pe.matmul(bank(n)[:, 256 * t:256 * t + 256], hT[:, k, P * t:P * t + P], w[:, k, :],
                                           start=k == 0, stop=k == KD - 1)
                mm.then_inc(filled, 1)
            pe.wait_ge(mla_q_s, 1)
            pe.wait_ge(mla_k_s, 2)
            for h in range(HEADS):
                if h >= 4:
                    pe.wait_ge(turn_e[h % 4], 1)
                for a, src in enumerate((q_mla, k_mla)):
                    for t in range(NT):
                        c = SEQ * a + P * t
                        mm = pe.transpose(ps[0:DQK, TURN[h % 4], c:c + P], src[:, t, h, :], ident[:, :])
                mm.then_inc(turn_s, 1)
            for b in range(4):
                pe.wait_ge(turn_e[b], 2)
            pe.wait_ge(emptied[0], FILL_GATE // 2)
            pe.wait_ge(consts, CONSTS)
            for h in range(HEADS):
                j, r = h // 2, DH * (h % 2)
                zb = ps[:, 2 + h % 2, :]
                if h >= 2:
                    pe.wait_ge(cap_s, h - 1)
                for t, c in ((0, 0), (1, SEQ)):
                    mm = pe.matmul(zb[:, c:c + SEQ - P * t], kT[r:r + DH, j, P * t:P * t + P],
                                   qT[r:r + DH, j, P * t:SEQ], start=t == 0, stop=t == 1, skip_group_check=True)
                mm.then_inc(z_s, 1)
                if h:
                    pe.wait_ge(p_s, h)
                for t, c in ((0, 0), (1, P)):
                    pe.matmul(ps[:, 5, c:c + P * (t + 1)], qkT[0:DQK, h, 0, P * t:P * t + P],
                              qkT[0:DQK, h, 1, 0:P * (t + 1)], start=True, stop=False, skip_group_check=True)
                    mm = pe.matmul(ps[:, 5, c + P * t:c + P * t + P], row_lo[:, :], col_hi[:, :],
                                   start=False, stop=True, skip_group_check=True)
                mm.then_inc(s_s, 1)
                n = FILL_GATE + h
                fill(n)
                w = weights(("gate", h))
                turned(n, 0, w, 0)
                pe.wait_ge(sp_s, h + 1)
                e = stick[:, h % 2, :]
                pe.matmul(zb[:, 0:SEQ], neg_from[:, :], e[:, 0:SEQ], start=False, stop=False, skip_group_check=True)
                pe.matmul(zb[:, P:SEQ], neg_ones[:, :], e[:, SEQ:384], start=False, stop=False, skip_group_check=True)
                pe.matmul(zb[:, SEQ:384], neg_from[:, :], e[:, SEQ:384], start=False, stop=True,
                          skip_group_check=True).then_inc(r_s, 1)
                pe.wait_ge(pn_s, h + 1)
                if h:
                    pe.wait_ge(pte_s, h)
                for c in range(3):
                    mm = pe.transpose(ps[:, 6, P * (0, 1, 2)[c]:P * c + P], prob[:, h % 2, P * c:P * c + P], ident[:, :])
                mm.then_inc(pt_s, 1)
                mm = turned(n, 1, w, P)
                mm.then_inc(filled, 1)
                if h >= 4 and h % 2 == 0:
                    pe.wait_ge(oe_s, j - 1)
                c = SEQ * (j % 2)
                for sem_in, sem_out, b, a, val in ((a_s, av_s, 4, stay, lambda t: v_sb[:, t, DH * h:DH * h + DH]),
                                                   (pte_s, mv_s, 7, probT, lambda t: kv[:, t, h, DH:2 * DH])):
                    pe.wait_ge(sem_in, h + 1)
                    pe.matmul(ps[r:r + DH, b, c:c + SEQ], val(0), a[:, h % 2, 0:SEQ], start=True, stop=False,
                              skip_group_check=True)
                    pe.matmul(ps[r:r + DH, b, c + P:c + SEQ], val(1), a[:, h % 2, SEQ:384], start=False, stop=True,
                              skip_group_check=True).then_inc(sem_out, 1)
            n = FILL_BUP
            fill(n)
            w = weights(("bup", 0))
            for i in range(16):
                half, g, j = i // 8, i // 4 % 2, i % 4
                c0 = 2 * P * (4 * half + j) + g
                mm = pe.transpose(bank(n)[:, NE * i:NE * i + NE], w[:, c0:c0 + 2 * P - 1:2], ident[0:NE, 0:NE])
            mm.then_inc(filled, 1)
            pe.wait_ge(oe_s, 4)
            for m in range(KD):
                n = FILL_MIX + m
                fill(n)
                for a, (name, o) in enumerate((("osb", o_sb), ("omla", o_mla_sb))):
                    w = weights((name, m // 4))
                    for k in range(4):
                        mm = pe.matmul(bank(n)[:, SEQ * a:SEQ * a + SEQ], w[:, k, P * (m % 4):P * (m % 4) + P],
                                       o[:, k, :], start=k == 0, stop=k == 3)
                mm.then_inc(filled, 1)
            pe.wait_ge(mix_s, 1 + KD)
            for i in range(4):
                n = FILL_OUT + i
                fill(n)
                w = weights(("wout", i))
                for t in range(NT):
                    for k in range(KD):
                        mm = pe.matmul(bank(n)[:, 256 * t:256 * t + 256], gates[:, k, 0, P * t:P * t + P], w[:, k, :],
                                       start=k == 0, stop=k == KD - 1)
                mm.then_inc(filled, 1)
            for m in range(4):
                if m % 2 == 0:
                    pe.wait_ge(h2_s, NT * (m // 2 + 1))
                n = FILL_H2 + m
                fill(n)
                for i in range(2):
                    for t in range(NT):
                        k = 2 * m + i
                        mm = pe.transpose(bank(n)[:, SEQ * i + P * t:SEQ * i + P * t + P], hn[:, t, P * k:P * k + P],
                                          ident[:, :])
                mm.then_inc(filled, 1)
            n = FILL_LOGIT
            fill(n)
            pe.wait_ge(emptied[1], n // 2)
            w = weights(("router", 0))
            for t in range(NT):
                for k in range(KD):
                    mm = pe.matmul(bank(n)[:, NE * t:NE * t + NE], h2T[:, k, P * t:P * t + P], w[:, k, :],
                                   start=k == 0, stop=k == KD - 1)
            mm.then_inc(filled, 1)
            n = FILL_RANK
            fill(n)
            pe.wait_ge(chosen_s, 1)
            for c, terms in enumerate((((before, 0),), ((ones, 0), (before, 1)), ((ones, 0), (ones, 1)))):
                for i, (mat, t) in enumerate(terms):
                    mm = pe.matmul(bank(n)[:, NE * c:NE * c + NE], mat[:, :], chosen[:, t, :], start=i == 0,
                                   stop=i == len(terms) - 1)
            mm.then_inc(filled, 1)
            gather(pe, main, 0, 0)
            pe.wait_ge(gw_s, 1)
            for t in range(NT):
                mm = pe.transpose(ps[0:NE, 3, P * t:P * t + P], gate_w[:, t, :], ident[:, :])
            mm.then_inc(gwt_ps, 1)
            pe.wait_ge(count_s, 1)
            main_product(pe, 0, "a")
            main_product(pe, 0, "b")
            gather(pe, main, 1, 0)
            pe.wait_ge(wt_s, 1)
            turn_up(pe, main, 0, 0, pass_number(0, "a"))
            w = weights(("bdown", 0))
            for t in range(NT):
                for b in range(2):
                    mm = pe.matmul(ps[:, 4 + 2 * t + b, :], gate_wT[:, P * t:P * t + P], w[:, 512 * b:512 * b + 512],
                                   start=True, stop=False, skip_group_check=True)
            mm.then_inc(acc_s, 1)
            pe_body(pe, 1, before2=False)
            with pe.Fori(2, NE - 1) as i:
                pe_body(pe, i)
            w, v = NE - 2, NE - 1
            main_product(pe, v, "a")
            turn_up(pe, main, 1, w, pass_number(w, "b"))
            add_visit(pe, main, NE - 3, pass_number(w, "d"))
            main_product(pe, v, "b")
            turn_up(pe, main, 0, v, pass_number(v, "a"))
            main_product(pe, v, "d")
            turn_put(pe, main, w, NE)
            turn_up(pe, main, 1, v, pass_number(v, "b"))
            add_visit(pe, main, w, pass_number(v, "d"))
            turn_put(pe, main, v, NE)
            main_product(pe, NE, "d")
            add_visit(pe, main, v, pass_number(NE, "d"), last_s)

            def start():
                pe.sem_inc(extra.w_used, RING)
                pe.sem_inc(extra.gathered, 1)
                pe.sem_inc(extra.gu_turned, 2)
                pe.sem_inc(extra.put_turned, 1)
                pe.sem_inc(extra.summed, 1)

            def visit(j, column, e):
                gather(pe, extra, j, j)
                product(pe, extra, "a", j, 12 * j, 0, 3 * j)
                turn_up(pe, extra, 0, j, 3 * j)
                product(pe, extra, "b", j, 12 * j + 4, 4 % RING, 3 * j + 1)
                turn_up(pe, extra, 1, j, 3 * j + 1)
                product(pe, extra, "d", j, 12 * j + 8, 8 % RING, 3 * j + 2)
                turn_put(pe, extra, j, j + 1)
                add_visit(pe, extra, j, 3 * j + 2)
            further(pe, start, visit)


TURN = (2, 3, 5, 6)
CONSTS = 34
RMS = ((0, 2), (2, 6), (6, 22), (22, 38), (38, 40))

_INS = ['x', 'positions', 'g_mix', 'w_in', 'g_cq', 'w_uq', 'g_ckv', 'w_ukv', 'g_qnorm', 'g_knorm', 'w_o_sb',
        'w_o_mla', 'w_out', 'g_ffn', 'w_router', 'b_router', 'w_up', 'b_up', 'w_down', 'b_down']


def kernel(**inputs):
    import numpy as _np
    import concourse.bacc as _bacc
    from concourse import mybir as _mybir
    from concourse.bass_utils import run_bass_kernel_spmd as _run

    nc = _bacc.Bacc("TRN2", target_bir_lowering=False, num_devices=1)
    arrays, args = {}, []
    for name in _INS:
        a = _np.ascontiguousarray(inputs[name])
        arrays[f"in_{name}_dram"] = a
        args.append(nc.dram_tensor(f"in_{name}_dram", a.shape, _mybir.dt.from_np(a.dtype), kind="ExternalInput").ap())
    args.append(nc.dram_tensor("out_0_dram", inputs["x"].shape, F32, kind="ExternalOutput").ap())
    encoder_block(nc, *args)
    r = _run(nc, [arrays], core_ids=[0])
    return r.results[0]["out_0_dram"]
```

```python
from contextlib import ExitStack
import math

import numpy as np
from concourse import mybir
from concourse.bass import ds

ALU = mybir.AluOpType
ACT = mybir.ActivationFunctionType
AX = mybir.AxisListType
F32 = mybir.dt.float32
F32R = mybir.dt.float32r
I32 = mybir.dt.int32

P = 128
D = 1024
KD = D // P
SEQ = 256
NT = SEQ // P
EPS = 1e-6
HEADS = 8
DH = 64
SBW = HEADS * DH
ROPE = 32
HALF = ROPE // 2
DQK = DH + ROPE
CQ, CKV = 384, 256
QT, KVT = CQ // P, CKV // P
THETA = 10000.0
CHUNK = 64
TOPK = 4
NE = 32
FF = 1024
LIMIT = 7.0
ALPHA = 1.702
NEG = -1.0e30

C_CQ = 3 * SBW
C_CKV = C_CQ + CQ
C_KR = C_CKV + CKV
C_GA = C_KR + ROPE
C_GB = C_GA + D

SLOTS = 12
RAW = 6
HI_AT, HI_RING = RAW, 4
X_LO = 10
ROUTER_AT = 11
SLOT = 2048
PER_EXPERT = 12
CAP = 64
COLS = 64
ROUNDS = SEQ // CAP
MAX_EXTRA = SEQ * TOPK // CAP
RING = 6

BIG_RANK = 3.0e38
TWO_PI_1 = 6.28125
TWO_PI_2 = float(np.float32(0.0019350051879882812))
TWO_PI_3 = float(2 * math.pi - TWO_PI_1 - TWO_PI_2)
ROUNDER = 12582912.0


def plan_chunks():
    return ([("lat", i) for i in range(3)] + [("uq", i) for i in range(2)] + [("ukv", 0)]
            + [("qkv", i) for i in range(6)] + [("gate", i) for i in range(8)] + [("bup", 0)]
            + [("osb", 0), ("omla", 0), ("osb", 1), ("omla", 1)]
            + [("wout", i) for i in range(4)])


def encoder_block(nc, x, positions, g_mix, w_in, g_cq, w_uq, g_ckv, w_ukv, g_qnorm, g_knorm, w_o_sb,
                  w_o_mla, w_out, g_ffn, w_router, b_router, w_up, b_up, w_down, b_down, out):
    chunks = plan_chunks()
    NCH = len(chunks)
    number = {c: n for n, c in enumerate(chunks)}
    split = [c for c in chunks if c[0] != "bup"]
    split_number = {c: n for n, c in enumerate(split)}

    ctx = ExitStack()
    att = ExitStack()

    def sb(name, shape, dt=F32, stack=ctx):
        return stack.enter_context(nc.sbuf_tensor(name, shape, dt))

    def sem(name):
        return ctx.enter_context(nc.semaphore(name))

    class VisitSemaphores:
        pass

    def visit_semaphores(tag, spare):
        q = VisitSemaphores()
        q.spare = spare
        q.hi, q.lo = sem(tag + "_w_hi"), sem(tag + "_w_lo")
        q.w_used = sem(tag + "_w_used")
        q.p_read = sem(tag + "_product_read")
        q.ht_hi, q.ht_lo = sem(tag + "_ht_hi"), sem(tag + "_ht_lo")
        q.pick, q.put = sem(tag + "_pick"), sem(tag + "_put")
        q.gathered, q.put_turned, q.putT = sem(tag + "_gathered"), sem(tag + "_put_turned"), sem(tag + "_putT")
        q.gu_turned, q.u = sem(tag + "_gu_turned"), sem(tag + "_u")
        q.glu, q.lin, q.gated = sem(tag + "_glu"), sem(tag + "_lin"), sem(tag + "_gated")
        q.sig, q.act = sem(tag + "_sig"), sem(tag + "_act")
        q.act_hi, q.act_lo = sem(tag + "_act_hi"), sem(tag + "_act_lo")
        q.summed = sem(tag + "_summed")
        return q

    with ctx:
        ps = ctx.enter_context(nc.psum_tensor("ps", [P, 8, 512], F32))

        lo_parts = ExitStack()
        slot_lo = [sb(f"slot{s}_lo", [P, SLOT], F32R, lo_parts) for s in range(SLOTS)]
        lo_parts.close()
        slot = [sb(f"slot{s}", [P, SLOT]) for s in range(SLOTS)]
        ident = sb("ident", [P, P])
        ones = sb("ones", [P, P])
        before = sb("before", [P, P])
        xin = sb("xin", [P, NT, D])
        hn_parts = ExitStack()
        o_hi = sb("o_hi", [P, 2, 4, SEQ], F32R, hn_parts)
        hn_parts.close()
        hn = sb("hn", [P, NT, D])
        slot_no = sb("slot_no", [P, 2, COLS])
        fold = sb("fold", [P, COLS])
        b_upT = sb("b_upT", [P, 2, 2, 4, NE])
        rank_in = sb("rank_in", [P, NT, ROUNDS, NE])
        gate_w = sb("gate_w", [P, NT, NE])
        count = sb("count", [P, NE])
        visit_f = sb("visit_f", [1, 3, MAX_EXTRA])
        visit_i = sb("visit_i", [1, 3, MAX_EXTRA], I32)
        var, inv, half_vy = sb("var", [P, 40]), sb("inv", [P, 40]), sb("half_vy", [P, 40])
        br_bc = sb("br_bc", [P, NE])

        def sa(name, shape, dt=F32):
            return sb(name, shape, dt, att)

        x_hi = sa("x_hi", [P, KD, SEQ], F32R)
        x_lo = slot_lo[X_LO][:, :].rearrange("p (k s) -> p k s", k=KD)
        qT = sa("qT", [P, 4, SEQ])
        kT = sa("kT", [P, 4, SEQ])
        v_sb = sa("v_sb", [P, NT, SBW])
        lat_parts = ExitStack()
        lat = sb("latents", [P, 2, QT + KVT, SEQ], F32R, lat_parts)
        lat_parts.close()
        gates = sa("gates", [P, KD, 2, SEQ])
        q_parts = ExitStack()
        o_lo = sb("o_lo", [P, 2, 4, SEQ], F32R, q_parts)
        q_parts.close()
        q_room = sa("q_room", [P, 2 * 4 * SEQ])
        q_mla = q_room[:, 0:NT * HEADS * DQK].rearrange("p (t h d) -> p t h d", t=NT, h=HEADS)
        kv = sa("kv", [P, NT, HEADS, 2 * DH])
        qkT = sa("qkT", [P, HEADS, 2, SEQ])
        stick = sa("stick", [P, 2, 384])
        stay = sa("stay", [P, 2, 384])
        prob = sa("prob", [P, 2, 384])
        probT = sa("probT", [P, 2, 384])
        neg_from = sa("neg_from", [P, P])
        neg_ones = sa("neg_ones", [P, P])
        cap_mask = sa("cap_mask", [P, 384])
        row_lo = sa("row_lo", [P, P])
        col_hi = sa("col_hi", [P, P])
        gains = sa("gains", [KD + QT + KVT, P])
        gT = sa("gT", [P, KD + QT + KVT])
        gq_bc = sa("gq_bc", [P, DQK])
        gk_bc = sa("gk_bc", [P, DQK])
        inv_freq = sa("inv_freq", [P, HALF])
        pos_i = sa("pos_i", [P, NT], I32)
        pos_f = sa("pos_f", [P, NT])
        ang = sa("ang", [P, NT, HALF])
        turns = sa("turns", [P, 2, NT, HALF])
        red = sa("red", [P, 2, NT, HALF])
        cs = sa("cs", [P, 2, NT, HALF])
        kr = sa("kr", [P, NT, ROPE])
        krr = sa("krr", [P, NT, ROPE])
        st = sa("st", [P, 160])
        lg = sa("lg", [P, NT, NE + 4])
        top = sa("top", [P, NT, 8])
        key = sa("key", [P, NT, 8])
        chosen = sa("chosen", [P, NT, NE])
        k_mla = hn[:, :, 0:HEADS * DQK].rearrange("p t (h d) -> p t h d", h=HEADS)
        gates_flat = gates[:, :, :, :].rearrange("p k a s -> p (k a) s")
        sqT = gates_flat[:, 2 * (QT + KVT):3 * (QT + KVT), :]
        g_ffn_bc = kv[:, 0, :, :].rearrange("p h d -> p (h d)")
        marked = prob[:, 0, 0:NT * (NE + 4)].rearrange("p (t e) -> p t e", t=NT)
        expl = prob[:, 1, 0:NT * NE].rearrange("p (t e) -> p t e", t=NT)
        h2T = gates_flat[:, 0:KD, :]
        att.close()

        w_hi = sb("w_hi", [P, RING, SLOT], F32R)
        hTs = sb("hTs", [P, KD, 2, COLS], F32R)
        actT = sb("actT", [P, 8, 2, COLS], F32R)
        gu_sb = sb("gu_sb", [P, 2, 1024])
        y_sb = sb("y_sb", [P, D])
        pick = sb("pick", [P, NT, COLS])
        put = sb("put", [P, NT, 2, COLS])
        putT = sb("putT", [P, SEQ])
        u = sb("u", [P, 2, 4, COLS])
        gated = sb("gated", [P, 4, COLS])
        sig = sb("sig", [P, 4, COLS])
        act32 = sb("act32", [P, 4, COLS])
        gate_wT = sb("gate_wT", [NE, SEQ])
        more = sb("more", [1, 3, (ROUNDS - 1) * NE])
        codes = sb("codes", [1, 2, (ROUNDS - 1) * NE])
        found = sb("found", [1, (ROUNDS - 1) * NE])

        loaded = [sem(f"slot{s}_loaded") for s in range(SLOTS)]
        x_in = [sem(f"x_in{t}") for t in range(NT)]
        gains_in, small_in, gffn_in, out_done = sem("gains_in"), sem("small_in"), sem("gffn_in"), sem("out_done")
        consts = sem("consts")
        filled = sem("filled")
        emptied = [sem(f"bank{b}_emptied") for b in range(2)]
        dve_s, act_s = sem("dve_steps"), sem("act_steps")
        ssq_s, xhat_s, gt_ps, gt_s = sem("sumsq"), sem("xhat"), sem("gains_turned"), sem("gains_ready")
        lat_ss, lat_rs = sem("latent_sumsq"), sem("latent_rstd")
        red_s, cs_s = sem("angles_reduced"), sem("sincos")
        mla_q_s, mla_k_s = sem("mla_q_ready"), sem("mla_k_ready")
        turn_s = sem("qk_turned")
        turn_e = [sem(f"qk_bank{b}_emptied") for b in range(4)]
        z_s, bound_s, ln_s, sp_s, r_s, cap_s, a_s, av_s = (sem(n) for n in (
            "sb_scores", "sb_bounded", "sb_log", "sb_softplus", "sb_logweights", "sb_capped", "sb_weights", "sb_pv"))
        s_s, max_s, p_s, pn_s, pt_s, pte_s, mv_s = (sem(n) for n in (
            "mla_scores", "mla_max", "mla_exp", "mla_probs", "mla_probs_turned", "mla_probsT", "mla_pv"))
        oe_s = sem("heads_out")
        recip_s, root_s = sem("rms_recip"), sem("rms_root")
        mix_s, x1_s, h2_s = sem("mixed"), sem("x1_ready"), sem("h2_ready")
        w_hi_s, w_lo_s = sem("attention_w_hi"), sem("attention_w_lo")
        lat_hi = sem("latents_hi")
        x_hi_s, o_lo_s, gate_sig = sem("x_hi_ready"), sem("heads_out_lo"), sem("gates_sigmoid")
        mix_hi, mix_lo = sem("mixed_hi"), sem("mixed_lo")
        top_s, expl_s, chosen_s, count_s, wt_s = (sem(n) for n in (
            "logits_shifted", "logits_exp", "chosen_ready", "counts_ready", "gate_w_turned"))
        bdown_in = sem("bdown_in")
        pool_s, visits_s, out_s = sem("pool_steps"), sem("visits_ready"), sem("out_ready")
        gwt_ps, last_s = sem("gate_w_in_psum"), sem("last_expert_summed")
        gw_s, sum_in = sem("gate_w_ready"), sem("x1_squares")
        main = visit_semaphores("v", 0)
        extra = visit_semaphores("x", 1)
        again = [sem(f"chunk{c}_again") for c in range(PER_EXPERT)]

        w_upv = w_up.rearrange("l e (k p) n -> (l e) p k n", p=P)
        w_downv = w_down.rearrange("l e (k p) n -> (l e) p k n", p=P)

        xv = x.rearrange("b (t p) d -> p (b t) d", p=P)
        ov = out.rearrange("b (t p) d -> p (b t) d", p=P)
        posv = positions.rearrange("b (t p) -> p (b t)", p=P)
        w_inv = w_in.rearrange("l (k p) n -> p (l k) n", p=P)
        w_uqv = w_uq.rearrange("l (k p) n -> p (l k) n", p=P)
        w_ukvv = w_ukv.rearrange("l (k p) n -> p (l k) n", p=P)
        w_osv = w_o_sb.rearrange("l (k p) n -> p (l k) n", p=P)
        w_omv = w_o_mla.rearrange("l (k p) n -> p (l k) n", p=P)
        w_outv = w_out.rearrange("l (k p) n -> p (l k) n", p=P)
        w_rv = w_router.rearrange("l (k p) n -> p (l k) n", p=P)

        def chunk(c):
            name, i = c
            t = slot[number[c] % RAW if c in number else ROUTER_AT]

            def view(k, n):
                return t[:, 0:k * n].rearrange("p (k n) -> p k n", k=k)
            if name == "lat":
                n = 256 if i < 2 else 160
                return view(KD, n), w_inv[:, :, C_CQ + 256 * i:C_CQ + 256 * i + n]
            if name == "uq":
                return view(QT, 384), w_uqv[:, :, 384 * i:384 * i + 384]
            if name == "ukv":
                return view(KVT, 1024), w_ukvv
            if name == "qkv":
                return view(KD, 256), w_inv[:, :, 256 * i:256 * i + 256]
            if name == "gate":
                c0 = (C_GA, C_GB)[i % 2] + 256 * (i // 2)
                return view(KD, 256), w_inv[:, :, c0:c0 + 256]
            if name == "osb":
                return view(4, 512), w_osv[:, :, 512 * i:512 * i + 512]
            if name == "omla":
                return view(4, 512), w_omv[:, :, 512 * i:512 * i + 512]
            if name == "wout":
                return view(KD, 256), w_outv[:, :, 256 * i:256 * i + 256]
            if name == "router":
                return view(KD, NE), w_rv
            return t[0:NE, 0:2 * FF], b_up.rearrange("l e n -> (l e) n")

        def chunk_parts(c):
            dst, _ = chunk(c)
            _, k, n = dst.shape
            return (k, n, slot[number[c] % RAW][:, 0:k * n], slot_lo[HI_AT + split_number[c] % HI_RING][:, 0:k * n],
                    slot_lo[number[c] % RAW][:, 0:k * n])

        FILL_X = 0
        FILL_LAT = 4
        FILL_UP = 7
        FILL_QKV = 15
        FILL_GATE = 21
        FILL_BUP = 29
        FILL_MIX = 30
        FILL_OUT = 38
        FILL_H2 = 42
        FILL_LOGIT = 46
        FILL_RANK = 47

        def last_fill(c):
            name, i = c
            return {"lat": FILL_LAT + i, "uq": FILL_UP + 2 * i + 1, "ukv": FILL_UP + 7, "qkv": FILL_QKV + i,
                    "gate": FILL_GATE + i, "bup": FILL_BUP, "osb": FILL_MIX + 4 * i + 3,
                    "omla": FILL_MIX + 4 * i + 3, "wout": FILL_OUT + i, "router": FILL_LOGIT,
                    }[name]

        def bank(n):
            return ps[:, n if n < FILL_LAT else n % 2, :]

        def up_piece(m):
            b = bank(FILL_UP + m)
            if m < 4:
                i, t = m // 2, m % 2
                return (q_mla[:, t, 4 * i:4 * i + 4, :], b[:, 0:384].rearrange("p (h d) -> p h d", h=4),
                        inv[:, 2 + t:3 + t])
            t, i = (m - 4) // 2, m % 2
            return (kv[:, t, 4 * i:4 * i + 4, :], b.rearrange("p (h d) -> p h d", h=4), inv[:, 4 + t:5 + t])


        PASSES = ("a", "b", "d")

        def expert_slot(kind, k, last=False):
            j = 4 * PASSES.index("a" if last else kind) + k
            return (NCH + j) % RAW if j < RAW else j

        def load_chunk(sp, kind, k, e, s, signal):
            dst = slot[s][:, :].rearrange("p (k n) -> p k n", k=2)
            if kind == "d":
                src = w_downv[e, :, 2 * k:2 * k + 2, :]
            else:
                c0 = 1024 * (kind == "b")
                src = w_upv[e, :, 2 * k:2 * k + 2, c0:c0 + 1024]
            sp.dma_start(dst, src).then_inc(signal, 16)

        def split_hi(act, q, s, n, at, arrived, times):
            act.wait_ge(arrived, 16 * times)
            free(act, q.w_used, n - RING + 1, q.spare * RING)
            act.activation(w_hi[:, at, :], slot[s][:, :], ACT.Copy).then_inc(q.hi, 1)

        def split_lo(dve, q, s, n, at, arrived, times):
            dve.wait_ge(arrived, 16 * times)
            dve.wait_ge(q.hi, n + 1)
            dve.tensor_tensor(slot_lo[s][:, :], slot[s][:, :], w_hi[:, at, :].bitcast(F32),
                              ALU.subtract).then_inc(q.lo, 1)

        def free(eng, s, n, spare):
            if isinstance(n, int) and n + spare <= 0:
                return
            eng.wait_ge(s, n + spare)

        def gather(pe, q, v, puts):
            pe.wait_ge(q.pick, v + 1)
            free(pe, q.ht_hi, v, q.spare)
            free(pe, q.ht_lo, v, q.spare)
            free(pe, q.putT, puts, q.spare)
            for k in range(KD):
                for t in range(NT):
                    mm = pe.matmul(ps[:, 2, COLS * k:COLS * k + COLS], hn[:, t, P * k:P * k + P], pick[:, t, :],
                                   start=t == 0, stop=t == NT - 1)
            mm.then_inc(q.gathered, 1)

        def product(pe, q, kind, v, first, at, pn, last=False, ks=range(4)):
            free(pe, q.p_read, pn, q.spare)
            if kind == "d":
                x2 = actT
            else:
                x2 = hTs
                pe.wait_ge(q.ht_hi, v + 1 + q.spare)
                pe.wait_ge(q.ht_lo, v + 1 + q.spare)
            for k in ks:
                if kind == "d" and k % 2 == 0:
                    pe.wait_ge(q.act_hi, 2 * v + k // 2 + 1)
                    pe.wait_ge(q.act_lo, 2 * v + k // 2 + 1)
                pe.wait_ge(q.hi, first + k + 1)
                for i in range(2):
                    lhs = x2[:, 2 * k + i, :, :].rearrange("p a c -> p (a c)")
                    for part, w in enumerate((w_hi[:, (at + k) % RING, :], slot_lo[expert_slot(kind, k, last)])):
                        if i == 0 and part == 1:
                            pe.wait_ge(q.lo, first + k + 1)
                        for b in range(2):
                            c0 = 1024 * i + 512 * b
                            mm = pe.matmul(ps[:, b, :], lhs, w[:, c0:c0 + 512],
                                           start=k + i + part == 0, stop=k + i + part == 5)
                mm.then_inc(q.w_used, 1)

        def turn_up(pe, q, half, v, pn):
            pe.wait_ge(q.p_read, pn + 1 + q.spare)
            free(pe, q.u, 2 * v + half, q.spare)
            for g in range(2):
                for j in range(4):
                    c0 = 2 * P * j + g
                    o = COLS * (4 * g + j)
                    mm = pe.matmul(ps[:, 3, o:o + COLS], gu_sb[:, half, c0:c0 + 2 * P - 1:2], fold[:, :],
                                   start=True, stop=True)
            mm.then_inc(q.gu_turned, 1)

        def turn_put(pe, q, v, gathers):
            pe.wait_ge(q.put, v + 1)
            pe.wait_ge(q.ht_hi, gathers + q.spare)
            pe.wait_ge(q.ht_lo, gathers + q.spare)
            free(pe, q.putT, v, q.spare)
            for t in range(NT):
                mm = pe.transpose(ps[:, 2, P * t:P * t + P], put[:, t, :, :].rearrange("p a c -> p (a c)"), ident[:, :])
            mm.then_inc(q.put_turned, 1)

        def add_visit(pe, q, v, pn, each=None):
            pe.wait_ge(q.p_read, pn + 1 + q.spare)
            pe.wait_ge(q.putT, v + 1 + q.spare)
            for t in range(NT):
                for b in range(2):
                    mm = pe.matmul(ps[:, 4 + 2 * t + b, :], putT[:, P * t:P * t + P], y_sb[:, 512 * b:512 * b + 512],
                                   start=False, stop=False, skip_group_check=True)
                    if each is not None:
                        mm.then_inc(each, 1)
            if each is None:
                mm.then_inc(q.summed, 1)

        def copy_up(act, q, half, v, last):
            act.wait_ge(q.w_used, last + q.spare * RING)
            free(act, q.gu_turned, 2 * v + half - 1, 2 * q.spare)
            act.activation(gu_sb[:, half, :], ps[:, 0:2, :].rearrange("p b n -> p (b n)"), ACT.Copy).then_inc(q.p_read, 1)

        def copy_down(act, q, v, last):
            act.wait_ge(q.w_used, last + q.spare * RING)
            free(act, q.summed, v, q.spare)
            act.activation(y_sb[:, :], ps[:, 0:2, :].rearrange("p b n -> p (b n)"), ACT.Copy).then_inc(q.p_read, 1)

        def copy_put(act, q, v):
            act.wait_ge(q.put_turned, v + 1 + q.spare)
            free(act, q.summed, v, q.spare)
            act.activation(putT[:, :], ps[:, 2, 0:SEQ], ACT.Copy).then_inc(q.putT, 1)

        def tokens_hi(act, q, v):
            act.wait_ge(q.gathered, v + 1 + q.spare)
            act.activation(hTs[:, :, 0, :], ps[:, 2, :].rearrange("p (k c) -> p k c", k=KD), ACT.Copy
                           ).then_inc(q.ht_hi, 1)

        def sigmoid(act, q, m):
            act.wait_ge(q.glu, m + 1)
            act.activation(sig[:, :, :], u[:, 0, :, :], ACT.Sigmoid, scale=ALPHA).then_inc(q.sig, 1)

        def act_hi(act, q, half, m):
            act.wait_ge(q.act, m + 1)
            act.activation(actT[:, 4 * half:4 * half + 4, 0, :], act32[:, :, :], ACT.Copy).then_inc(q.act_hi, 1)

        def build_pick(dve, q, v, column):
            free(dve, q.gathered, v, q.spare)
            for t in range(NT):
                ins = dve.tensor_scalar(pick[:, t, :], slot_no[:, 0, :], rank_v[:, t, ds(column, 1)], None, ALU.is_equal)
            ins.then_inc(q.pick, 1)

        def build_put(dve, q, v, column, e):
            free(dve, q.put_turned, v, q.spare)
            for t in range(NT):
                ins = dve.tensor_scalar(put[:, t, :, :], slot_no[:, :, :], rank_v[:, t, ds(column, 1)],
                                        gate_w[:, t, ds(e, 1)], ALU.is_equal, ALU.mult)
            ins.then_inc(q.put, 1)

        def tokens_lo(dve, q, v):
            dve.wait_ge(q.ht_hi, v + 1 + q.spare)
            dve.tensor_tensor(hTs[:, :, 1, :], ps[:, 2, :].rearrange("p (k c) -> p k c", k=KD),
                              hTs[:, :, 0, :].bitcast(F32), ALU.subtract).then_inc(q.ht_lo, 1)

        def gate_up(dve, q, half, m, e):
            dve.wait_ge(q.gu_turned, m + 1 + 2 * q.spare)
            bias = b_upT[:, half, :, :, ds(e, 1)].to_broadcast([P, 2, 4, COLS])
            dve.tensor_tensor(u[:, :, :, :], ps[:, 3, :].rearrange("p (g j c) -> p g j c", g=2, j=4), bias, ALU.add
                              ).then_inc(q.u, 1)
            dve.wait_ge(q.u, m + 1 + q.spare)
            dve.tensor_scalar(u[:, 0, :, :], u[:, 0, :, :], LIMIT, None, ALU.min).then_inc(q.glu, 1)
            dve.tensor_scalar(u[:, 1, :, :], u[:, 1, :, :], LIMIT, -LIMIT, ALU.min, ALU.max).then_inc(q.lin, 1)
            dve.wait_ge(q.glu, m + 1)
            dve.wait_ge(q.lin, m + 1)
            dve.scalar_tensor_tensor(out=gated[:, :, :], in0=u[:, 1, :, :], scalar=1.0, in1=u[:, 0, :, :],
                                     op0=ALU.add, op1=ALU.mult).then_inc(q.gated, 1)

        def times_sigmoid(dve, q, m):
            dve.wait_ge(q.sig, m + 1)
            dve.wait_ge(q.gated, m + 1)
            dve.tensor_tensor(act32[:, :, :], gated[:, :, :], sig[:, :, :], ALU.mult).then_inc(q.act, 1)

        def act_lo(dve, q, half, m):
            dve.wait_ge(q.act_hi, m + 1)
            dve.tensor_tensor(actT[:, 4 * half:4 * half + 4, 1, :], act32[:, :, :],
                              actT[:, 4 * half:4 * half + 4, 0, :].bitcast(F32), ALU.subtract).then_inc(q.act_lo, 1)

        rank_v = rank_in[:, :, :, :].rearrange("p t r e -> p t (r e)")
        PASS_AT = {"a": 0, "b": 4, "d": 8}

        def first_chunk(i, kind):
            if isinstance(i, int) and i == 0:
                return PASS_AT[kind]
            if isinstance(i, int) and i == NE:
                return 12 * NE - 4
            return 12 * i - 4 + PASS_AT[kind]

        def place(i, kind):
            return (PASS_AT[kind] - 4 * (not (isinstance(i, int) and i == 0))
                    - 8 * (isinstance(i, int) and i == NE)) % RING

        def pass_number(i, kind):
            if isinstance(i, int) and i == 0:
                return PASS_AT[kind] // 4
            if isinstance(i, int) and i == NE:
                return 3 * NE - 1
            return 3 * i - 1 + PASS_AT[kind] // 4

        def arrival(i, kind, k):
            last = isinstance(i, int) and i == NE
            s = expert_slot(kind, k, last)
            before_experts = len(range(s, NCH, RAW)) if s < RAW else int(s == ROUTER_AT)
            return s, loaded[s], before_experts + (NE + 1 if last else i if kind == "d" else i + 1)

        def hi(act, i, kind, k):
            s, arrived, times = arrival(i, kind, k)
            split_hi(act, main, s, first_chunk(i, kind) + k, (place(i, kind) + k) % RING, arrived, times)

        def lo(dve, i, kind, k):
            s, arrived, times = arrival(i, kind, k)
            split_lo(dve, main, s, first_chunk(i, kind) + k, (place(i, kind) + k) % RING, arrived, times)

        def main_product(pe, i, kind, ks=range(4)):
            product(pe, main, kind, i - (kind == "d"), first_chunk(i, kind), place(i, kind), pass_number(i, kind),
                    last=isinstance(i, int) and i == NE, ks=ks)

        def open_sums(pe):
            pe.wait_ge(bdown_in, 16)
            for t in range(NT):
                for b in range(2):
                    mm = pe.matmul(ps[:, 4 + 2 * t + b, :], gate_wT[:, P * t:P * t + P],
                                   y_sb[0:NE, 512 * b:512 * b + 512],
                                   start=True, stop=False, skip_group_check=True)

        def pe_body(pe, i, before2=True):
            main_product(pe, i, "a")
            turn_up(pe, main, 1, i - 1, pass_number(i - 1, "b"))
            if before2:
                add_visit(pe, main, i - 2, pass_number(i - 1, "d"))
            else:
                open_sums(pe)
            main_product(pe, i, "b")
            gather(pe, main, i + 1, i - 1)
            main_product(pe, i, "d")
            turn_up(pe, main, 0, i, pass_number(i, "a"))
            turn_put(pe, main, i - 1, i + 2)

        def act_up_passes(act, i, before2=True):
            if before2:
                hi(act, i, "a", 0)
                hi(act, i, "a", 1)
                copy_down(act, main, i - 2, first_chunk(i - 1, "d") + 4)
                copy_put(act, main, i - 2)
            hi(act, i, "a", 2)
            sigmoid(act, main, 2 * (i - 1))
            hi(act, i, "a", 3)
            act_hi(act, main, 0, 2 * (i - 1))
            hi(act, i, "b", 0)
            hi(act, i, "b", 1)
            copy_up(act, main, 0, i, first_chunk(i, "a") + 4)
            hi(act, i, "b", 2)
            sigmoid(act, main, 2 * (i - 1) + 1)
            hi(act, i, "b", 3)
            act_hi(act, main, 1, 2 * (i - 1) + 1)
            for k in range(3):
                hi(act, i, "d", k)
            copy_up(act, main, 1, i, first_chunk(i, "b") + 4)

        def act_body(act, i, before2=True):
            act_up_passes(act, i, before2)
            tokens_hi(act, main, i + 1)
            hi(act, i, "d", 3)

        def dve_up_passes(dve, i, picks=True, begun=False):
            if not begun:
                lo(dve, i, "a", 0)
                lo(dve, i, "a", 1)
            gate_up(dve, main, 0, 2 * (i - 1), i - 1)
            lo(dve, i, "a", 2)
            times_sigmoid(dve, main, 2 * (i - 1))
            lo(dve, i, "a", 3)
            act_lo(dve, main, 0, 2 * (i - 1))
            lo(dve, i, "b", 0)
            lo(dve, i, "b", 1)
            gate_up(dve, main, 1, 2 * (i - 1) + 1, i - 1)
            lo(dve, i, "b", 2)
            times_sigmoid(dve, main, 2 * (i - 1) + 1)
            if picks:
                build_pick(dve, main, i + 1, i + 1)
            lo(dve, i, "b", 3)
            act_lo(dve, main, 1, 2 * (i - 1) + 1)
            lo(dve, i, "d", 0)
            build_put(dve, main, i - 1, i - 1, i - 1)
            lo(dve, i, "d", 1)

        def dve_body(dve, i, begun=False):
            dve_up_passes(dve, i, begun=begun)
            lo(dve, i, "d", 2)
            tokens_lo(dve, main, i + 1)
            lo(dve, i, "d", 3)

        def further(eng, start, body):
            eng.wait_ge(visits_s, 1)
            n = eng.value_load(visit_i[0:1, 2, 0:1], min_val=0, max_val=MAX_EXTRA)
            with eng.If(n > 0):
                start()
                with eng.Fori(0, n) as j:
                    column = eng.value_load(visit_i[0:1, 0, ds(j, 1)], min_val=0, max_val=ROUNDS * NE - 1)
                    e = eng.value_load(visit_i[0:1, 1, ds(j, 1)], min_val=0, max_val=NE - 1)
                    body(j, column, e)
            return n

        block = ctx.enter_context(nc.Block())

        @block.sync
        def _(sp):
            def leave(sp, n):
                if n >= RAW:
                    sp.wait_ge(filled, last_fill(chunks[n - RAW]) + 1)

            def leave_first(sp, kind, k):
                s = expert_slot(kind, k)
                if s < RAW:
                    leave(sp, NCH + 4 * PASSES.index(kind) + k)
                elif s < ROUTER_AT:
                    sp.wait_ge(filled, FILL_OUT + 4)
                else:
                    sp.wait_ge(filled, FILL_LOGIT + 1)

            for t in range(NT):
                sp.dma_start(xin[:, t, :], xv[:, t, :]).then_inc(x_in[t], 16)
            for n, c in enumerate(chunks):
                if n == RAW:
                    dst, src = chunk(("router", 0))
                    sp.dma_start(dst, src).then_inc(loaded[ROUTER_AT], 16)
                leave(sp, n)
                if n == 3:
                    sp.dma_start(pos_i[:, :], posv, allow_slow_non_contiguous=True).then_inc(small_in, 16)
                    sp.dma_start(gq_bc[:, :], g_qnorm[0, :].partition_broadcast(P)).then_inc(small_in, 16)
                    sp.dma_start(gk_bc[:, :], g_knorm[0, :].partition_broadcast(P)).then_inc(small_in, 16)
                    sp.dma_start(br_bc[:, :], b_router[0, :].partition_broadcast(P)).then_inc(small_in, 16)
                dst, src = chunk(c)
                sp.dma_start(dst, src).then_inc(loaded[n % RAW], 16)
            for kind in ("a", "b"):
                for k in range(4):
                    leave_first(sp, kind, k)
                    s, arrived, _ = arrival(0, kind, k)
                    load_chunk(sp, kind, k, 0, s, arrived)

            def again_chunk(i, kind, k, before_kind=None):
                sp.wait_ge(main.w_used, first_chunk(i - 1, before_kind or kind) + k + 1)
                s, arrived, _ = arrival(i, kind, k)
                load_chunk(sp, kind, k, i - (kind == "d"), s, arrived)

            for k in range(4):
                leave_first(sp, "d", k)
                s, arrived, _ = arrival(1, "d", k)
                load_chunk(sp, "d", k, 0, s, arrived)
            for kind in ("a", "b"):
                for k in range(4):
                    again_chunk(1, kind, k)
            with sp.Fori(2, NE) as i:
                for kind in PASSES:
                    for k in range(4):
                        again_chunk(i, kind, k)
            for k in range(4):
                again_chunk(NE, "d", k, "a")

            def start():
                sp.wait_ge(last_s, 2 * NT)

            def load_again(j, column, e):
                sp.wait_ge(extra.summed, j + extra.spare)
                for kind in PASSES:
                    for k in range(4):
                        load_chunk(sp, kind, k, e, expert_slot(kind, k), again[4 * PASSES.index(kind) + k])
            further(sp, start, load_again)

            for t in range(NT):
                sp.wait_ge(out_s, 2 * (t + 1))
                sp.dma_start(ov[:, t, :], xin[:, t, :]).then_inc(out_done, 16)
            sp.wait_ge(out_done, 16 * NT)

        @block.gpsimd
        def _(pool):
            def const(ins):
                const.n += 1
                ins.then_inc(consts, 1)
                pool.wait_ge(consts, const.n)
            const.n = 0
            const(pool.memset(ident[:, :], 0.0))
            const(pool.affine_select(out=ident[:, :], in_=ident[:, :], compare_op=ALU.not_equal, fill=1.0,
                                     base=0, pattern=[[-1, P]], channel_multiplier=1))
            const(pool.memset(ones[:, :], 1.0))
            for i in range(HALF):
                f = float(np.float32(THETA) ** (-np.float32(i) / np.float32(HALF)))
                const(pool.memset(inv_freq[:, i:i + 1], f))
            const(pool.memset(neg_ones[:, :], -1.0))
            const(pool.affine_select(out=before[:, :], in_=ones[:, :], compare_op=ALU.is_gt, fill=0.0,
                                     base=0, pattern=[[1, P]], channel_multiplier=-1))
            const(pool.affine_select(out=neg_from[:, :], in_=neg_ones[:, :], compare_op=ALU.is_ge, fill=0.0,
                                     base=0, pattern=[[-1, P]], channel_multiplier=1))
            const(pool.memset(cap_mask[:, :], 0.0))
            for c in (0, 256):
                const(pool.affine_select(out=cap_mask[:, c:c + P], in_=cap_mask[:, c:c + P],
                                         compare_op=ALU.is_gt, fill=-1.0e5, base=0, pattern=[[1, P]],
                                         channel_multiplier=-1))
            const(pool.memset(row_lo[:, :], 0.0))
            const(pool.memset(col_hi[:, :], 0.0))
            const(pool.memset(row_lo[0:1, 0:CHUNK], 1.0))
            const(pool.memset(col_hi[0:1, CHUNK:P], NEG))
            const(pool.memset(fold[:, :], 0.0))
            for b in (0, COLS):
                const(pool.affine_select(out=fold[:, :], in_=fold[:, :], compare_op=ALU.not_equal, fill=1.0,
                                         base=-b, pattern=[[-1, COLS]], channel_multiplier=1))
            const(pool.memset(slot_no[:, :, :], 1.0e6))
            const(pool.iota(slot_no[:, :, 0:CAP], pattern=[[0, 2], [1, CAP]], base=0, channel_multiplier=0,
                            allow_small_or_imprecise_dtypes=True))
            assert const.n == CONSTS, const.n

            for n, c in enumerate(split):
                _, _, raw, w_h, w_l = chunk_parts(c)
                pool.wait_ge(loaded[number[c] % RAW], 16 * (number[c] // RAW + 1))
                pool.wait_ge(w_hi_s, n + 1)
                pool.tensor_tensor(w_l, raw, w_h.bitcast(F32), ALU.subtract).then_inc(w_lo_s, 1)

            steps = [0]

            def link(ins):
                steps[0] += 1
                ins.then_inc(pool_s, 1)
                pool.wait_ge(pool_s, steps[0])

            pool.wait_ge(count_s, 1)
            W = (ROUNDS - 1) * NE
            link(pool.iota(codes[:, 0, :], pattern=[[1, W]], base=NE, channel_multiplier=0,
                           allow_small_or_imprecise_dtypes=True))
            link(pool.iota(codes[:, 1, :], pattern=[[0, ROUNDS - 1], [1, NE]], base=0, channel_multiplier=0,
                           allow_small_or_imprecise_dtypes=True))
            for r in range(1, ROUNDS):
                c = NE * (r - 1)
                last = pool.tensor_scalar(more[:, 0, c:c + NE], count[0:1, :], float(CAP * r), None, ALU.is_gt)
            link(last)
            link(pool.tensor_copy(more[:, 1, :], more[:, 0, :]))
            a, b, shift = 1, 2, 1
            while shift < W:
                pool.tensor_copy(more[:, b, 0:shift], more[:, a, 0:shift])
                link(pool.tensor_tensor(more[:, b, shift:W], more[:, a, shift:W], more[:, a, 0:W - shift], ALU.add))
                a, b, shift = b, a, 2 * shift
            link(pool.tensor_copy(visit_f[:, 2, :], more[:, a, W - 1:W].to_broadcast([1, MAX_EXTRA])))
            link(pool.tensor_tensor(more[:, a, :], more[:, a, :], more[:, 0, :], ALU.mult))
            for v in range(MAX_EXTRA):
                for i in range(2):
                    link(pool.tensor_scalar(found[:, :], more[:, a, :], float(v + 1), None, ALU.is_equal))
                    link(pool.tensor_tensor(found[:, :], found[:, :], codes[:, i, :], ALU.mult))
                    link(pool.tensor_reduce(visit_f[:, i, v:v + 1], found[:, :], AX.XYZWC, ALU.add))
            pool.tensor_copy(visit_i[:, :, :], visit_f[:, :, :]).then_inc(visits_s, 1)

        @block.scalar
        def _(act):
            act.preload_act_table(ACT.Sqrt)
            act.dma_start(gains[0:KD, :], g_mix.rearrange("l (k p) -> (l k) p", p=P)).then_inc(gains_in, 16)
            act.dma_start(gains[KD:KD + QT, :], g_cq.rearrange("l (k p) -> (l k) p", p=P)).then_inc(gains_in, 16)
            act.dma_start(gains[KD + QT:, :], g_ckv.rearrange("l (k p) -> (l k) p", p=P)).then_inc(gains_in, 16)

            steps = [0]

            def link(ins):
                steps[0] += 1
                ins.then_inc(act_s, 1)
                act.wait_ge(act_s, steps[0])

            def root(i):
                a, b = RMS[i]
                act.wait_ge(recip_s, i + 1)
                act.activation(inv[:, a:b], inv[:, a:b], ACT.Sqrt).then_inc(root_s, 1)

            def weights_hi(n):
                c = split[n]
                _, _, raw, w_h, _ = chunk_parts(c)
                act.wait_ge(loaded[number[c] % RAW], 16 * (number[c] // RAW + 1))
                if n >= HI_RING:
                    act.wait_ge(filled, last_fill(split[n - HI_RING]) + 1)
                act.activation(w_h, raw, ACT.Copy).then_inc(w_hi_s, 1)

            for t in range(NT):
                act.wait_ge(x_in[t], 16)
                act.activation(hn[:, t, :], xin[:, t, :], ACT.Square, accum_out=st[:, t:t + 1]).then_inc(ssq_s, 1)
            root(0)
            act.wait_ge(gt_ps, 1)
            act.activation(gT[:, :], ps[:, 7, 0:KD + QT + KVT], ACT.Copy).then_inc(gt_s, 1)
            act.wait_ge(gt_s, 1)
            for n in range(4):
                act.wait_ge(filled, FILL_X + n + 1)
                for i in range(2):
                    k = 2 * n + i
                    last = act.activation(x_hi[:, k, :], bank(n)[:, SEQ * i:SEQ * i + SEQ], ACT.Copy,
                                          scale=gT[:, k:k + 1])
                last.then_inc(x_hi_s, 1)
                if n == 0:
                    weights_hi(0)
            for n in (1, 2, 3):
                weights_hi(n)
            for n in range(3):
                b = bank(FILL_LAT + n)
                act.wait_ge(filled, FILL_LAT + n + 1)
                w = 2 if n < 2 else 1
                act.activation(sqT[:, 2 * n:2 * n + w, :], b[:, 0:w * SEQ].rearrange("p (j s) -> p j s", j=w),
                               ACT.Square)
                if n == 2:
                    act.activation(kr[:, :, :], b[:, SEQ:SEQ + NT * ROPE].rearrange("p (t d) -> p t d", t=NT),
                                   ACT.Copy)
                for i in range(w):
                    j = 2 * n + i
                    last = act.activation(lat[:, 0, j, :], b[:, SEQ * i:SEQ * i + SEQ], ACT.Copy,
                                          scale=gT[:, KD + j:KD + j + 1])
                last.then_inc(lat_hi, 1)
                if n < 2:
                    weights_hi(4 + n)
            root(1)
            weights_hi(6)
            act.wait_ge(red_s, 1)
            act.activation(cs[:, :, :, :], red[:, :, :, :], ACT.Sin).then_inc(cs_s, 1)
            act.wait_ge(lat_rs, 1)
            for m in range(8):
                n = FILL_UP + m
                if n % 2:
                    continue
                act.wait_ge(filled, n + 1)
                dst, src, scale = up_piece(m)
                act.activation(dst, src, ACT.Copy, scale=scale).then_inc(emptied[0], 1)
                if m != 5:
                    weights_hi({1: 7, 3: 8, 7: 9}[m])
            for m in range(6):
                if m in (1, 3):
                    root(m // 2 + 2)
                n = FILL_QKV + m
                act.wait_ge(filled, n + 1)
                src = bank(n).rearrange("p (j s) -> p j s", j=2)
                if m < 2:
                    ins = act.activation(qT[:, 2 * m:2 * m + 2, :], src, ACT.Copy, scale=DH ** -0.5)
                elif m < 4:
                    ins = act.activation(kT[:, 2 * m - 4:2 * m - 2, :], src, ACT.Copy)
                else:
                    ins = act.activation(v_sb[:, :, 256 * (m - 4):256 * (m - 4) + 256], src, ACT.Copy)
                ins.then_inc(emptied[n % 2], 1)
                weights_hi(10 + m)
            for h in range(0, HEADS, 2):
                act.wait_ge(turn_s, h + 1)
                act.activation(qkT[0:DQK, h, :, :], ps[0:DQK, TURN[h % 4], :].rearrange("p (a s) -> p a s", a=2),
                               ACT.Copy).then_inc(turn_e[h % 4], 1)
            act.preload_act_table_set("natural_log_exp_and_others")
            for h in range(HEADS):
                e = stick[:, h % 2, :]
                act.wait_ge(bound_s, h + 1)
                link(act.activation(e, e, ACT.Exp))
                act.activation(e, e, ACT.Ln, bias=1.0).then_inc(ln_s, 1)
                act.wait_ge(max_s, h + 1)
                act.activation(prob[:, h % 2, 0:P], ps[:, 5, 0:P], ACT.Exp, scale=DQK ** -0.5,
                               bias=st[:, 36:37], accum_out=st[:, 40:41])
                act.activation(prob[:, h % 2, P:384], ps[:, 5, P:384], ACT.Exp, scale=DQK ** -0.5,
                               bias=st[:, 37:38], accum_out=st[:, 41:42]).then_inc(p_s, 1)
                act.wait_ge(cap_s, h + 1)
                act.activation(stay[:, h % 2, :], stay[:, h % 2, :], ACT.Exp).then_inc(a_s, 1)
                act.wait_ge(pt_s, h + 1)
                if h >= 2:
                    act.wait_ge(mv_s, h - 1)
                act.activation(probT[:, h % 2, :], ps[:, 6, 0:384], ACT.Copy).then_inc(pte_s, 1)
                n = FILL_GATE + h
                act.wait_ge(filled, n + 1)
                act.activation(gates[:, h - h % 2:h - h % 2 + 2, h % 2, :], bank(n).rearrange("p (j s) -> p j s", j=2),
                               ACT.Copy).then_inc(emptied[n % 2], 1)
                if h % 2:
                    j = h // 2
                    act.wait_ge(av_s, h + 1)
                    act.wait_ge(mv_s, h + 1)
                    c = SEQ * (j % 2)
                    act.activation(o_hi[:, 0, j, :], ps[:, 4, c:c + SEQ], ACT.Copy)
                    act.activation(o_hi[:, 1, j, :], ps[:, 7, c:c + SEQ], ACT.Copy).then_inc(oe_s, 1)
                weights_hi(16 + h)
            n = FILL_BUP
            act.wait_ge(filled, n + 1)
            act.activation(b_upT[:, :, :, :, :], bank(n).rearrange("p (a b j e) -> p a b j e", a=2, b=2, j=4),
                           ACT.Copy).then_inc(emptied[n % 2], 1)
            act.wait_ge(emptied[0], FILL_BUP // 2 + 1)
            act.wait_ge(emptied[1], FILL_BUP // 2)
            for k in range(0, KD, 2):
                act.activation(gates[:, k:k + 2, :, :], gates[:, k:k + 2, :, :], ACT.Sigmoid).then_inc(gate_sig, 1)
            act.dma_start(g_ffn_bc, g_ffn[0, :].partition_broadcast(P)).then_inc(gffn_in, 16)
            act.dma_start(y_sb[0:NE, :], b_down.rearrange("l e n -> (l e) n")).then_inc(bdown_in, 16)
            for m in range(KD):
                act.wait_ge(mix_s, m + 1)
                act.activation(x_hi[:, m, :], gates[:, m, 0, :], ACT.Copy).then_inc(mix_hi, 1)
                if m == 3:
                    weights_hi(24)
                    weights_hi(25)
            weights_hi(26)
            act.preload_act_table(ACT.Sqrt)
            for i in range(4):
                act.wait_ge(x1_s, i + 1)
                for t in range(NT):
                    c = 120 + 4 * t + i
                    last = act.activation(hn[:, t, 256 * i:256 * i + 256], xin[:, t, 256 * i:256 * i + 256],
                                          ACT.Square, accum_out=st[:, c:c + 1])
                last.then_inc(sum_in, 1)
                if i == 0:
                    weights_hi(27)
            root(4)
            for n in (FILL_H2, FILL_H2 + 2):
                act.wait_ge(filled, n + 1)
                k = 2 * (n - FILL_H2)
                act.activation(h2T[:, k:k + 2, :], bank(n).rearrange("p (j s) -> p j s", j=2), ACT.Copy
                               ).then_inc(emptied[0], 1)
            act.wait_ge(filled, FILL_LOGIT + 1)
            hi(act, 0, "a", 0)
            hi(act, 0, "a", 1)
            act.wait_ge(top_s, 1)
            act.activation(expl[:, :, :], expl[:, :, :], ACT.Exp).then_inc(expl_s, 1)
            act.preload_act_table(ACT.Sigmoid)
            hi(act, 0, "a", 2)
            hi(act, 0, "a", 3)
            tokens_hi(act, main, 0)
            act.wait_ge(gwt_ps, 1)
            act.activation(gate_wT[:, :], ps[0:NE, 3, 0:SEQ], ACT.Copy).then_inc(wt_s, 1)
            for k in range(4):
                hi(act, 0, "b", k)
            copy_up(act, main, 0, 0, first_chunk(0, "a") + 4)
            hi(act, 1, "a", 0)
            hi(act, 1, "a", 1)
            copy_up(act, main, 1, 0, first_chunk(0, "b") + 4)
            tokens_hi(act, main, 1)
            act_body(act, 1, before2=False)
            with act.Fori(2, NE - 1) as i:
                act_body(act, i)
            w, v = NE - 2, NE - 1
            act_up_passes(act, v)
            hi(act, v, "d", 3)
            sigmoid(act, main, 2 * v)
            hi(act, NE, "d", 0)
            hi(act, NE, "d", 1)
            act.wait_ge(main.w_used, first_chunk(v, "d") + 2)
            act_hi(act, main, 0, 2 * v)
            hi(act, NE, "d", 2)
            copy_down(act, main, w, first_chunk(v, "d") + 4)
            copy_put(act, main, w)
            sigmoid(act, main, 2 * v + 1)
            hi(act, NE, "d", 3)
            act_hi(act, main, 1, 2 * v + 1)
            copy_put(act, main, v)
            copy_down(act, main, v, first_chunk(NE, "d") + 4)

            def start():
                act.sem_inc(extra.p_read, 1)
                act.sem_inc(extra.ht_hi, 1)
                act.sem_inc(extra.putT, 1)

            def visit(j, column, e):
                def hi(kind):
                    for k in range(4):
                        c = 4 * PASSES.index(kind) + k
                        split_hi(act, extra, expert_slot(kind, k), 12 * j + c, c % RING, again[c], j + 1)
                tokens_hi(act, extra, j)
                hi("a")
                copy_up(act, extra, 0, j, 12 * j + 4)
                hi("b")
                sigmoid(act, extra, 2 * j)
                act_hi(act, extra, 0, 2 * j)
                copy_up(act, extra, 1, j, 12 * j + 8)
                sigmoid(act, extra, 2 * j + 1)
                act_hi(act, extra, 1, 2 * j + 1)
                hi("d")
                copy_down(act, extra, j, 12 * j + 12)
                copy_put(act, extra, j)
            further(act, start, visit)

        @block.vector
        def _(dve):
            steps = [0]

            def link(ins):
                steps[0] += 1
                ins.then_inc(dve_s, 1)
                dve.wait_ge(dve_s, steps[0])

            def rstd(i, parts, ready=None):
                a, b = RMS[i]
                v, y, t = var[:, a:b], inv[:, a:b], half_vy[:, a:b]
                for src, width, c0, c1 in parts:
                    last = dve.tensor_scalar(var[:, c0:c1], src, 1.0 / width, EPS, ALU.mult, ALU.add)
                link(last)
                dve.reciprocal(y, v).then_inc(recip_s, 1)
                dve.wait_ge(root_s, i + 1)
                link(dve.scalar_tensor_tensor(out=t, in0=v, scalar=-0.5, in1=y, op0=ALU.mult, op1=ALU.mult))
                link(dve.tensor_tensor(t, t, y, ALU.mult))
                ins = dve.scalar_tensor_tensor(out=y, in0=t, scalar=1.5, in1=y, op0=ALU.add, op1=ALU.mult)
                if ready is None:
                    link(ins)
                else:
                    ins.then_inc(ready, 1)

            dve.wait_ge(ssq_s, NT)
            for t in range(NT):
                dve.wait_ge(x_in[t], 16)
            rstd(0, ((st[:, 0:2], D, 0, 2),))
            for t in range(NT):
                dve.tensor_scalar(hn[:, t, :], xin[:, t, :], inv[:, t:t + 1], None, ALU.mult).then_inc(xhat_s, 1)
            dve.wait_ge(gt_s, 1)
            for n in range(4):
                dve.wait_ge(x_hi_s, n + 1)
                for i in range(2):
                    k = 2 * n + i
                    last = dve.scalar_tensor_tensor(out=x_lo[:, k, :], in0=bank(n)[:, SEQ * i:SEQ * i + SEQ],
                                                    scalar=gT[:, k:k + 1], in1=x_hi[:, k, :].bitcast(F32),
                                                    op0=ALU.mult, op1=ALU.subtract)
                last.then_inc(emptied[n % 2], 1)
            dve.wait_ge(small_in, 16 * 4)
            dve.wait_ge(consts, CONSTS)
            link(dve.tensor_copy(pos_f[:, :], pos_i[:, :]))
            for t in range(NT):
                last = dve.tensor_scalar(ang[:, t, :], inv_freq[:, :], pos_f[:, t:t + 1], None, ALU.mult)
            link(last)
            dve.tensor_scalar(turns[:, 0, :, :], ang[:, :, :], 1.0 / (2 * math.pi), None, ALU.mult)
            link(dve.tensor_scalar(turns[:, 1, :, :], ang[:, :, :], 1.0 / (2 * math.pi), 0.25, ALU.mult, ALU.add))
            link(dve.tensor_scalar(turns[:, :, :, :], turns[:, :, :, :], ROUNDER, ROUNDER, ALU.add, ALU.subtract))
            for a in range(2):
                last = dve.scalar_tensor_tensor(out=red[:, a, :, :], in0=turns[:, a, :, :], scalar=-TWO_PI_1,
                                                in1=ang[:, :, :], op0=ALU.mult, op1=ALU.add)
            link(last)
            for part in (TWO_PI_2, TWO_PI_3):
                link(dve.scalar_tensor_tensor(out=red[:, :, :, :], in0=turns[:, :, :, :], scalar=-part,
                                              in1=red[:, :, :, :], op0=ALU.mult, op1=ALU.add))
            link(dve.tensor_scalar(red[:, 1, :, :], red[:, 1, :, :], math.pi / 2, None, ALU.add))
            lim = 3.1415925
            dve.tensor_scalar(red[:, :, :, :], red[:, :, :, :], lim, -lim, ALU.min, ALU.max).then_inc(red_s, 1)
            for n in range(3):
                dve.wait_ge(lat_hi, n + 1)
                for j in range(2 * n, min(2 * n + 2, QT + KVT)):
                    c = SEQ * (j % 2)
                    last = dve.scalar_tensor_tensor(out=lat[:, 1, j, :], in0=bank(FILL_LAT + n)[:, c:c + SEQ],
                                                    scalar=gT[:, KD + j:KD + j + 1],
                                                    in1=lat[:, 0, j, :].bitcast(F32), op0=ALU.mult,
                                                    op1=ALU.subtract)
                last.then_inc(emptied[(FILL_LAT + n) % 2], 1)
            dve.wait_ge(lat_ss, 1)
            rstd(1, ((ps[:, 7, 0:2], CQ, 2, 4), (ps[:, 7, 2:4], CKV, 4, 6)), lat_rs)
            dve.wait_ge(lat_rs, 1)
            for m in range(8):
                n = FILL_UP + m
                if n % 2 == 0:
                    continue
                dve.wait_ge(filled, n + 1)
                dst, src, scale = up_piece(m)
                dve.tensor_scalar(dst, src, scale, None, ALU.mult).then_inc(emptied[1], 1)
            sq = qkT[:, :, :, :].rearrange("p h a s -> p (h a s)")
            qf = q_mla[:, :, :, :].rearrange("p t h d -> p (t h) d")
            sqq = sq[:, 0:NT * HEADS * DQK].rearrange("p (h d) -> p h d", d=DQK)
            dve.wait_ge(emptied[0], (FILL_QKV + 1) // 2)
            dve.wait_ge(emptied[1], FILL_QKV // 2)
            link(dve.tensor_tensor(sqq, qf, qf, ALU.mult))
            link(dve.tensor_reduce(st[:, 48:64], sqq, AX.X, ALU.add))
            rstd(2, ((st[:, 48:64], DQK, 6, 22),))
            link(dve.tensor_tensor(qf, qf, inv[:, 6:22].unsqueeze(2).to_broadcast([P, 16, DQK]), ALU.mult))
            link(dve.tensor_tensor(qf, qf, gq_bc[:, :].unsqueeze(1).to_broadcast([P, 16, DQK]), ALU.mult))
            dve.wait_ge(cs_s, 1)
            t4 = sq[:, 2048:4096].rearrange("p (a t h d) -> p a t h d", a=8, t=NT, h=HEADS)

            def rotate(vec, heads, ready):
                def trig(a, t):
                    c = cs[:, a, t, :]
                    return c.unsqueeze(1).to_broadcast([P, heads, HALF]) if heads else c
                for t in range(NT):
                    tmp = [t4[:, i, t, :, :] if heads else t4[:, i, t, 0, :] for i in range(4)]
                    x1, x2 = (vec[:, t, :, 0:HALF], vec[:, t, :, HALF:ROPE]) if heads else (
                        vec[:, t, 0:HALF], vec[:, t, HALF:ROPE])
                    dve.tensor_tensor(tmp[0], x1, trig(1, t), ALU.mult)
                    dve.tensor_tensor(tmp[1], x2, trig(0, t), ALU.mult)
                    dve.tensor_tensor(tmp[2], x2, trig(1, t), ALU.mult)
                    link(dve.tensor_tensor(tmp[3], x1, trig(0, t), ALU.mult))
                    dve.tensor_tensor(x1, tmp[0], tmp[1], ALU.subtract)
                    ins = dve.tensor_tensor(x2, tmp[2], tmp[3], ALU.add)
                    if ready is not None and t == NT - 1:
                        ins.then_inc(ready, 1)
                    else:
                        link(ins)

            rotate(q_mla[:, :, :, DH:DQK], HEADS, mla_q_s)
            sqk = sq[:, 0:NT * HEADS * DH].rearrange("p (t h d) -> p t h d", t=NT, h=HEADS)
            for t in range(NT):
                last = dve.tensor_tensor(sqk[:, t, :, :], kv[:, t, :, 0:DH], kv[:, t, :, 0:DH], ALU.mult)
            link(last)
            link(dve.tensor_reduce(st[:, 80:96], sqk.rearrange("p t h d -> p (t h) d"), AX.X, ALU.add))
            sqr = sq[:, 1024:1024 + NT * ROPE].rearrange("p (t d) -> p t d", t=NT)
            link(dve.tensor_tensor(sqr, kr[:, :, :], kr[:, :, :], ALU.mult))
            link(dve.tensor_reduce(st[:, 96:98], sqr, AX.X, ALU.add))
            for t in range(NT):
                last = dve.tensor_scalar(st[:, 80 + 8 * t:88 + 8 * t], st[:, 80 + 8 * t:88 + 8 * t],
                                         st[:, 96 + t:97 + t], None, ALU.add)
            link(last)
            rstd(3, ((st[:, 80:96], DQK, 22, 38),))
            link(dve.tensor_tensor(krr[:, :, :], kr[:, :, :], gk_bc[:, DH:DQK].unsqueeze(1).to_broadcast([P, NT, ROPE]),
                                   ALU.mult))
            rotate(krr, 0, None)
            dve.wait_ge(filled, FILL_X + 4)
            for t in range(NT):
                rk = inv[:, 22 + 8 * t:30 + 8 * t].unsqueeze(2)
                dve.tensor_tensor(k_mla[:, t, :, 0:DH], kv[:, t, :, 0:DH], rk.to_broadcast([P, HEADS, DH]), ALU.mult)
                link(dve.tensor_tensor(k_mla[:, t, :, DH:DQK], krr[:, t, :].unsqueeze(1).to_broadcast([P, HEADS, ROPE]),
                                       rk.to_broadcast([P, HEADS, ROPE]), ALU.mult))
                ins = dve.tensor_tensor(k_mla[:, t, :, 0:DH], k_mla[:, t, :, 0:DH],
                                        gk_bc[:, 0:DH].unsqueeze(1).to_broadcast([P, HEADS, DH]), ALU.mult)
                ins.then_inc(mla_k_s, 1)
            for h in range(1, HEADS, 2):
                dve.wait_ge(turn_s, h + 1)
                if h == 1:
                    dve.wait_ge(mla_k_s, 2)
                dve.tensor_copy(qkT[0:DQK, h, :, :], ps[0:DQK, TURN[h % 4], :].rearrange("p (a s) -> p a s", a=2)
                                ).then_inc(turn_e[h % 4], 1)

            def heads_lo(j):
                dve.wait_ge(oe_s, j + 1)
                c = SEQ * (j % 2)
                for a, b in enumerate((4, 7)):
                    ins = dve.tensor_tensor(o_lo[:, a, j, :], ps[:, b, c:c + SEQ], o_hi[:, a, j, :].bitcast(F32),
                                            ALU.subtract)
                ins.then_inc(o_lo_s, 1)

            for h in range(HEADS):
                zb = ps[:, 2 + h % 2, 0:384]
                e, w = stick[:, h % 2, :], stay[:, h % 2, :]
                dve.wait_ge(z_s, h + 1)
                dve.tensor_scalar(e, zb, 40.0, None, ALU.min).then_inc(bound_s, 1)
                dve.wait_ge(s_s, h + 1)
                if h:
                    dve.wait_ge(p_s, h)
                dve.tensor_reduce(st[:, 32:33], ps[:, 5, 0:P], AX.X, ALU.max)
                link(dve.tensor_reduce(st[:, 33:34], ps[:, 5, P:384], AX.X, ALU.max))
                dve.tensor_scalar(st[:, 36:38], st[:, 32:34], -DQK ** -0.5, None, ALU.mult).then_inc(max_s, 1)
                dve.wait_ge(ln_s, h + 1)
                link(dve.tensor_tensor(e, zb, e, ALU.max))
                diag = e.rearrange("p (c s) -> p c s", c=3)[:, 0:3:2, :]
                dve.tensor_tensor(diag, diag, before[:, :].unsqueeze(1).to_broadcast([P, 2, P]),
                                  ALU.mult).then_inc(sp_s, 1)
                if h and h % 2 == 0:
                    heads_lo(h // 2 - 1)
                dve.wait_ge(p_s, h + 1)
                link(dve.reciprocal(st[:, 44:46], st[:, 40:42]))
                dve.tensor_scalar(prob[:, h % 2, 0:P], prob[:, h % 2, 0:P], st[:, 44:45], None, ALU.mult)
                dve.tensor_scalar(prob[:, h % 2, P:384], prob[:, h % 2, P:384], st[:, 45:46], None,
                                  ALU.mult).then_inc(pn_s, 1)
                dve.wait_ge(r_s, h + 1)
                if h >= 2:
                    dve.wait_ge(av_s, h - 1)
                dve.tensor_tensor(w, zb, cap_mask[:, :], ALU.min).then_inc(cap_s, 1)
            heads_lo(3)

            def mixed_lo(m):
                dve.wait_ge(mix_hi, m + 1)
                dve.tensor_tensor(x_lo[:, m, :], gates[:, m, 0, :], x_hi[:, m, :].bitcast(F32),
                                  ALU.subtract).then_inc(mix_lo, 1)
            for m in range(KD):
                n = FILL_MIX + m
                dve.wait_ge(gate_sig, m // 2 + 1)
                dve.wait_ge(filled, n + 1)
                dve.tensor_tensor(gates[:, m, :, :], gates[:, m, :, :], bank(n).rearrange("p (a s) -> p a s", a=2),
                                  ALU.mult).then_inc(emptied[n % 2], 1)
                dve.wait_ge(emptied[n % 2], n // 2 + 1)
                dve.tensor_tensor(gates[:, m, 0, :], gates[:, m, 0, :], gates[:, m, 1, :], ALU.add).then_inc(mix_s, 1)
                if m:
                    mixed_lo(m - 1)
            mixed_lo(KD - 1)
            for i in range(4):
                n = FILL_OUT + i
                dve.wait_ge(filled, n + 1)
                xs = xin[:, :, 256 * i:256 * i + 256]
                dve.tensor_tensor(xs, xs, bank(n).rearrange("p (t s) -> p t s", t=NT), ALU.add).then_inc(
                    emptied[n % 2], 1)
                dve.wait_ge(emptied[n % 2], n // 2 + 1)
                dve.sem_inc(x1_s, 1)
            dve.memset(lg[:, :, NE:NE + 4], -BIG_RANK)
            link(dve.memset(key[:, :, TOPK:8], -BIG_RANK))
            dve.wait_ge(sum_in, 4)
            link(dve.tensor_reduce(st[:, 128:130], st[:, 120:128].rearrange("p (t i) -> p t i", t=NT), AX.X, ALU.add))
            rstd(4, ((st[:, 128:130], D, 38, 40),))
            dve.wait_ge(gffn_in, 16)
            for c in (0, 512):
                for t in range(NT):
                    dve.scalar_tensor_tensor(out=hn[:, t, c:c + 512], in0=xin[:, t, c:c + 512],
                                             scalar=inv[:, 38 + t:39 + t], in1=g_ffn_bc[:, c:c + 512],
                                             op0=ALU.mult, op1=ALU.mult).then_inc(h2_s, 1)
            for n in (FILL_H2 + 1, FILL_H2 + 3):
                dve.wait_ge(filled, n + 1)
                k = 2 * (n - FILL_H2)
                dve.tensor_copy(h2T[:, k:k + 2, :], bank(n).rearrange("p (j s) -> p j s", j=2)).then_inc(emptied[1], 1)
            n = FILL_LOGIT
            dve.wait_ge(filled, n + 1)
            dve.tensor_tensor(lg[:, :, 0:NE], bank(n)[:, 0:NT * NE].rearrange("p (t e) -> p t e", t=NT),
                              br_bc[:, :].unsqueeze(1).to_broadcast([P, NT, NE]), ALU.add).then_inc(emptied[0], 1)
            dve.wait_ge(emptied[0], n // 2 + 1)
            for t in range(NT):
                last = dve.max(top[:, t, :], lg[:, t, 0:NE])
            link(last)
            link(dve.tensor_copy(key[:, :, 0:TOPK], top[:, :, 0:TOPK]))
            for t in range(NT):
                last = dve.match_replace(marked[:, t, :], key[:, t, :], lg[:, t, :], BIG_RANK)
            link(last)
            dve.tensor_scalar(chosen[:, :, :], marked[:, :, 0:NE], BIG_RANK, None, ALU.is_ge).then_inc(chosen_s, 1)
            for t in range(NT):
                last = dve.tensor_scalar(expl[:, t, :], lg[:, t, 0:NE], top[:, t, 0:1], None, ALU.subtract)
            last.then_inc(top_s, 1)
            dve.wait_ge(chosen_s, 1)
            lo(dve, 0, "a", 0)
            n = FILL_RANK
            dve.wait_ge(filled, n + 1)
            pos = bank(n)[:, 0:NT * NE].rearrange("p (t e) -> p t e", t=NT)
            link(dve.scalar_tensor_tensor(out=rank_in[:, :, 0, :], in0=pos, scalar=1.0, in1=chosen[:, :, :],
                                          op0=ALU.add, op1=ALU.mult))
            link(dve.tensor_scalar(rank_in[:, :, 0, :], rank_in[:, :, 0, :], -1.0, None, ALU.add))
            build_pick(dve, main, 0, 0)
            for r in range(1, ROUNDS):
                dve.tensor_scalar(rank_in[:, :, r, :], rank_in[:, :, 0, :], -CAP * r, None, ALU.add)
            dve.tensor_copy(count[:, :], bank(n)[:, NT * NE:NT * NE + NE]).then_inc(count_s, 1)
            lo(dve, 0, "a", 1)
            dve.wait_ge(expl_s, 1)
            link(dve.tensor_tensor(expl[:, :, :], expl[:, :, :], chosen[:, :, :], ALU.mult))
            link(dve.tensor_reduce(st[:, 132:134], expl[:, :, :], AX.X, ALU.add))
            link(dve.reciprocal(st[:, 134:136], st[:, 132:134]))
            for t in range(NT):
                last = dve.tensor_scalar(gate_w[:, t, :], expl[:, t, :], st[:, 134 + t:135 + t], None, ALU.mult)
            last.then_inc(gw_s, 1)
            dve.wait_ge(gw_s, 1)
            tokens_lo(dve, main, 0)
            lo(dve, 0, "a", 2)
            lo(dve, 0, "a", 3)
            lo(dve, 0, "b", 0)
            build_pick(dve, main, 1, 1)
            for k in range(1, 4):
                lo(dve, 0, "b", k)
            lo(dve, 1, "a", 0)
            tokens_lo(dve, main, 1)
            lo(dve, 1, "a", 1)
            dve_body(dve, 1, begun=True)
            with dve.Fori(2, NE - 1) as i:
                dve_body(dve, i)
            v = NE - 1
            dve_up_passes(dve, v, picks=False)
            gate_up(dve, main, 0, 2 * v, v)
            lo(dve, v, "d", 2)
            times_sigmoid(dve, main, 2 * v)
            lo(dve, v, "d", 3)
            lo(dve, NE, "d", 0)
            act_lo(dve, main, 0, 2 * v)
            lo(dve, NE, "d", 1)
            lo(dve, NE, "d", 2)
            build_put(dve, main, v, v, v)
            gate_up(dve, main, 1, 2 * v + 1, v)
            times_sigmoid(dve, main, 2 * v + 1)
            lo(dve, NE, "d", 3)
            act_lo(dve, main, 1, 2 * v + 1)

            def start():
                dve.sem_inc(extra.ht_lo, 1)
                dve.sem_inc(extra.u, 1)

            def visit(j, column, e):
                def lo(kind):
                    for k in range(4):
                        c = 4 * PASSES.index(kind) + k
                        split_lo(dve, extra, expert_slot(kind, k), 12 * j + c, c % RING, again[c], j + 1)
                build_pick(dve, extra, j, column)
                tokens_lo(dve, extra, j)
                lo("a")
                lo("b")
                for half in range(2):
                    m = 2 * j + half
                    gate_up(dve, extra, half, m, e)
                    times_sigmoid(dve, extra, m)
                    act_lo(dve, extra, half, m)
                build_put(dve, extra, j, column, e)
                lo("d")
                dve.wait_ge(extra.summed, j + 1 + extra.spare)
            further(dve, start, visit)
            for t in range(NT):
                for b in range(2):
                    dve.wait_ge(last_s, 2 * t + b + 1)
                    xs = xin[:, t, 512 * b:512 * b + 512]
                    dve.tensor_tensor(xs, xs, ps[:, 4 + 2 * t + b, :], ALU.add).then_inc(out_s, 1)

        @block.tensor
        def _(pe):
            def fill(n):
                if n >= 2:
                    pe.wait_ge(emptied[n % 2], n // 2)

            def weights(c):
                if c in number:
                    pe.wait_ge(loaded[number[c] % RAW], 16 * (number[c] // RAW + 1))
                else:
                    pe.wait_ge(loaded[ROUTER_AT], 16)
                return chunk(c)[0]

            def weights_parts(c):
                pe.wait_ge(w_hi_s, split_number[c] + 1)
                k, n, _, w_h, w_l = chunk_parts(c)
                return tuple(w.rearrange("p (k n) -> p k n", k=k) for w in (w_h, w_l))

            def lo_part(c):
                pe.wait_ge(w_lo_s, split_number[c] + 1)

            def keep_warm(n):
                for _ in range(n):
                    pe.matmul(ps[:, 6, 0:P], ident[:, :], ones[:, :], start=True, stop=True,
                              skip_group_check=True)

            pe.wait_ge(consts, 3)
            keep_warm(WARM[0])
            pe.wait_ge(gains_in, 16 * 3)
            pe.transpose(ps[:, 7, 0:KD + QT + KVT], gains[:, :], ident[0:KD + QT + KVT, 0:KD + QT + KVT]
                         ).then_inc(gt_ps, 1)
            pe.wait_ge(xhat_s, NT)
            for n in range(4):
                for i in range(2):
                    for t in range(NT):
                        k = 2 * n + i
                        mm = pe.transpose(bank(n)[:, SEQ * i + P * t:SEQ * i + P * t + P], hn[:, t, P * k:P * k + P],
                                          ident[:, :])
                mm.then_inc(filled, 1)
            keep_warm(WARM[1])
            for b in range(2):
                pe.wait_ge(emptied[b], 2)

            def turned(out, c, w, c0, x, ks):
                terms = [(0, 0, k) for k in ks] + [(0, 1, k) for k in ks] + [(1, 0, k) for k in ks]
                for i, (wp, xp, k) in enumerate(terms):
                    if i == 2 * len(ks):
                        lo_part(c)
                    mm = pe.matmul(out, w[wp][:, k, c0:c0 + P], x[xp][:, k, :], start=i == 0,
                                   stop=i == len(terms) - 1)
                return mm

            def upright(out, c, w, cols, x, t, ks=range(KD), ready=None):
                terms = [(0, 0, k) for k in ks] + [(0, 1, k) for k in ks] + [(1, 0, k) for k in ks]
                for i, (wp, xp, k) in enumerate(terms):
                    if i == 2 * len(ks):
                        lo_part(c)
                    if ready is not None and i < 2 * len(ks):
                        pe.wait_ge(ready[xp], k + 1)
                    mm = pe.matmul(out, x[xp][:, k, P * t:P * t + P], w[wp][:, k, cols], start=i == 0,
                                   stop=i == len(terms) - 1)
                return mm

            x_parts = (x_hi, x_lo)

            for i in range(3):
                n = FILL_LAT + i
                fill(n)
                c = ("lat", i)
                w = weights_parts(c)
                mm = turned(bank(n)[:, 0:SEQ], c, w, 0, x_parts, range(KD))
                if i < 2:
                    mm = turned(bank(n)[:, SEQ:2 * SEQ], c, w, P, x_parts, range(KD))
                else:
                    for t in range(NT):
                        mm = upright(bank(n)[:, SEQ + ROPE * t:SEQ + ROPE * t + ROPE], c, w, slice(P, P + ROPE),
                                     x_parts, t)
                mm.then_inc(filled, 1)
            pe.wait_ge(emptied[0], 4)
            pe.wait_ge(emptied[1], 3)
            for c, (j0, j1) in enumerate(((0, QT), (QT, QT + KVT))):
                for t in range(NT):
                    for j in range(j0, j1):
                        mm = pe.matmul(ps[:, 7, 2 * c + t:2 * c + t + 1], sqT[:, j, P * t:P * t + P], ones[:, 0:1],
                                       start=j == j0, stop=j == j1 - 1)
            mm.then_inc(lat_ss, 1)
            for i in range(2):
                c = ("uq", i)
                w = weights_parts(c)
                for t in range(NT):
                    n = FILL_UP + 2 * i + t
                    fill(n)
                    upright(bank(n)[:, 0:384], c, w, slice(0, 384), (lat[:, 0, 0:QT, :], lat[:, 1, 0:QT, :]), t,
                            range(QT)).then_inc(filled, 1)
            c = ("ukv", 0)
            w = weights_parts(c)
            for t in range(NT):
                for i in range(2):
                    n = FILL_UP + 4 + 2 * t + i
                    fill(n)
                    upright(bank(n), c, w, slice(512 * i, 512 * i + 512), (lat[:, 0, QT:, :], lat[:, 1, QT:, :]), t,
                            range(KVT)).then_inc(filled, 1)
            for m in range(6):
                n = FILL_QKV + m
                fill(n)
                c = ("qkv", m)
                w = weights_parts(c)
                for i in range(2):
                    out_half = bank(n)[:, 256 * i:256 * i + 256]
                    if m < 4:
                        mm = turned(out_half, c, w, P * i, x_parts, range(KD))
                    else:
                        mm = upright(out_half, c, w, slice(0, 256), x_parts, i)
                mm.then_inc(filled, 1)
            pe.wait_ge(mla_q_s, 1)
            pe.wait_ge(mla_k_s, 2)
            for h in range(HEADS):
                if h >= 4:
                    pe.wait_ge(turn_e[h % 4], 1)
                for a, src in enumerate((q_mla, k_mla)):
                    for t in range(NT):
                        c = SEQ * a + P * t
                        mm = pe.transpose(ps[0:DQK, TURN[h % 4], c:c + P], src[:, t, h, :], ident[:, :])
                mm.then_inc(turn_s, 1)
            for b in range(4):
                pe.wait_ge(turn_e[b], 2)
            pe.wait_ge(emptied[0], FILL_GATE // 2)
            pe.wait_ge(consts, CONSTS)
            for h in range(HEADS):
                j, r = h // 2, DH * (h % 2)
                zb = ps[:, 2 + h % 2, :]
                if h >= 2:
                    pe.wait_ge(cap_s, h - 1)
                for t, c in ((0, 0), (1, SEQ)):
                    mm = pe.matmul(zb[:, c:c + SEQ - P * t], kT[r:r + DH, j, P * t:P * t + P],
                                   qT[r:r + DH, j, P * t:SEQ], start=t == 0, stop=t == 1, skip_group_check=True)
                mm.then_inc(z_s, 1)
                if h:
                    pe.wait_ge(p_s, h)
                for t, c in ((0, 0), (1, P)):
                    pe.matmul(ps[:, 5, c:c + P * (t + 1)], qkT[0:DQK, h, 0, P * t:P * t + P],
                              qkT[0:DQK, h, 1, 0:P * (t + 1)], start=True, stop=False, skip_group_check=True)
                    mm = pe.matmul(ps[:, 5, c + P * t:c + P * t + P], row_lo[:, :], col_hi[:, :],
                                   start=False, stop=True, skip_group_check=True)
                mm.then_inc(s_s, 1)
                n = FILL_GATE + h
                fill(n)
                gate = ("gate", h)
                w = weights_parts(gate)
                turned(bank(n)[:, 0:SEQ], gate, w, 0, x_parts, range(KD))
                pe.wait_ge(sp_s, h + 1)
                e = stick[:, h % 2, :]
                pe.matmul(zb[:, 0:SEQ], neg_from[:, :], e[:, 0:SEQ], start=False, stop=False, skip_group_check=True)
                pe.matmul(zb[:, P:SEQ], neg_ones[:, :], e[:, SEQ:384], start=False, stop=False, skip_group_check=True)
                pe.matmul(zb[:, SEQ:384], neg_from[:, :], e[:, SEQ:384], start=False, stop=True,
                          skip_group_check=True).then_inc(r_s, 1)
                pe.wait_ge(pn_s, h + 1)
                if h:
                    pe.wait_ge(pte_s, h)
                for c in range(3):
                    mm = pe.transpose(ps[:, 6, P * (0, 1, 2)[c]:P * c + P], prob[:, h % 2, P * c:P * c + P], ident[:, :])
                mm.then_inc(pt_s, 1)
                mm = turned(bank(n)[:, SEQ:2 * SEQ], gate, w, P, x_parts, range(KD))
                mm.then_inc(filled, 1)
                if h >= 4 and h % 2 == 0:
                    pe.wait_ge(oe_s, j - 1)
                    pe.wait_ge(o_lo_s, j - 1)
                c = SEQ * (j % 2)
                for sem_in, sem_out, b, a, val in ((a_s, av_s, 4, stay, lambda t: v_sb[:, t, DH * h:DH * h + DH]),
                                                   (pte_s, mv_s, 7, probT, lambda t: kv[:, t, h, DH:2 * DH])):
                    pe.wait_ge(sem_in, h + 1)
                    pe.matmul(ps[r:r + DH, b, c:c + SEQ], val(0), a[:, h % 2, 0:SEQ], start=True, stop=False,
                              skip_group_check=True)
                    pe.matmul(ps[r:r + DH, b, c + P:c + SEQ], val(1), a[:, h % 2, SEQ:384], start=False, stop=True,
                              skip_group_check=True).then_inc(sem_out, 1)
            n = FILL_BUP
            fill(n)
            w = weights(("bup", 0))
            for i in range(16):
                half, g, j = i // 8, i // 4 % 2, i % 4
                c0 = 2 * P * (4 * half + j) + g
                mm = pe.transpose(bank(n)[:, NE * i:NE * i + NE], w[:, c0:c0 + 2 * P - 1:2], ident[0:NE, 0:NE])
            mm.then_inc(filled, 1)
            pe.wait_ge(oe_s, 4)
            pe.wait_ge(o_lo_s, 4)
            for m in range(KD):
                n = FILL_MIX + m
                fill(n)
                for a, name in enumerate(("osb", "omla")):
                    c = (name, m // 4)
                    mm = turned(bank(n)[:, SEQ * a:SEQ * a + SEQ], c, weights_parts(c), P * (m % 4),
                                (o_hi[:, a, :, :], o_lo[:, a, :, :]), range(4))
                mm.then_inc(filled, 1)
            for i in range(4):
                n = FILL_OUT + i
                fill(n)
                c = ("wout", i)
                w = weights_parts(c)
                for t in range(NT):
                    mm = upright(bank(n)[:, 256 * t:256 * t + 256], c, w, slice(0, 256), x_parts, t,
                                 ready=(mix_hi, mix_lo) if i + t == 0 else None)
                mm.then_inc(filled, 1)
            keep_warm(WARM[2])
            for m in range(4):
                if m % 2 == 0:
                    pe.wait_ge(h2_s, NT * (m // 2 + 1))
                n = FILL_H2 + m
                fill(n)
                for i in range(2):
                    for t in range(NT):
                        k = 2 * m + i
                        mm = pe.transpose(bank(n)[:, SEQ * i + P * t:SEQ * i + P * t + P], hn[:, t, P * k:P * k + P],
                                          ident[:, :])
                mm.then_inc(filled, 1)
            n = FILL_LOGIT
            fill(n)
            pe.wait_ge(emptied[1], n // 2)
            w = weights(("router", 0))
            for t in range(NT):
                for k in range(KD):
                    mm = pe.matmul(bank(n)[:, NE * t:NE * t + NE], h2T[:, k, P * t:P * t + P], w[:, k, :],
                                   start=k == 0, stop=k == KD - 1)
            mm.then_inc(filled, 1)
            keep_warm(WARM[3])
            n = FILL_RANK
            fill(n)
            pe.wait_ge(chosen_s, 1)
            for c, terms in enumerate((((before, 0),), ((ones, 0), (before, 1)), ((ones, 0), (ones, 1)))):
                for i, (mat, t) in enumerate(terms):
                    mm = pe.matmul(bank(n)[:, NE * c:NE * c + NE], mat[:, :], chosen[:, t, :], start=i == 0,
                                   stop=i == len(terms) - 1)
            mm.then_inc(filled, 1)
            keep_warm(WARM[4])
            gather(pe, main, 0, 0)
            pe.wait_ge(gw_s, 1)
            for t in range(NT):
                mm = pe.transpose(ps[0:NE, 3, P * t:P * t + P], gate_w[:, t, :], ident[:, :])
            mm.then_inc(gwt_ps, 1)
            pe.wait_ge(count_s, 1)
            main_product(pe, 0, "a")
            main_product(pe, 0, "b")
            gather(pe, main, 1, 0)
            pe.wait_ge(wt_s, 1)
            turn_up(pe, main, 0, 0, pass_number(0, "a"))
            pe_body(pe, 1, before2=False)
            with pe.Fori(2, NE - 1) as i:
                pe_body(pe, i)
            w, v = NE - 2, NE - 1
            main_product(pe, v, "a")
            turn_up(pe, main, 1, w, pass_number(w, "b"))
            add_visit(pe, main, NE - 3, pass_number(w, "d"))
            main_product(pe, v, "b")
            turn_up(pe, main, 0, v, pass_number(v, "a"))
            main_product(pe, v, "d")
            turn_put(pe, main, w, NE)
            turn_up(pe, main, 1, v, pass_number(v, "b"))
            main_product(pe, NE, "d", range(2))
            add_visit(pe, main, w, pass_number(v, "d"))
            turn_put(pe, main, v, NE)
            main_product(pe, NE, "d", range(2, 4))
            add_visit(pe, main, v, pass_number(NE, "d"), last_s)

            def start():
                pe.sem_inc(extra.w_used, RING)
                pe.sem_inc(extra.gathered, 1)
                pe.sem_inc(extra.gu_turned, 2)
                pe.sem_inc(extra.put_turned, 1)
                pe.sem_inc(extra.summed, 1)

            def visit(j, column, e):
                gather(pe, extra, j, j)
                product(pe, extra, "a", j, 12 * j, 0, 3 * j)
                turn_up(pe, extra, 0, j, 3 * j)
                product(pe, extra, "b", j, 12 * j + 4, 4 % RING, 3 * j + 1)
                turn_up(pe, extra, 1, j, 3 * j + 1)
                product(pe, extra, "d", j, 12 * j + 8, 8 % RING, 3 * j + 2)
                turn_put(pe, extra, j, j + 1)
                add_visit(pe, extra, j, 3 * j + 2)
            further(pe, start, visit)


WARM = (16, 20, 20, 7, 7)
TURN = (2, 3, 5, 6)
CONSTS = 34
RMS = ((0, 2), (2, 6), (6, 22), (22, 38), (38, 40))

_INS = ['x', 'positions', 'g_mix', 'w_in', 'g_cq', 'w_uq', 'g_ckv', 'w_ukv', 'g_qnorm', 'g_knorm', 'w_o_sb',
        'w_o_mla', 'w_out', 'g_ffn', 'w_router', 'b_router', 'w_up', 'b_up', 'w_down', 'b_down']


def kernel(**inputs):
    import numpy as _np
    import concourse.bacc as _bacc
    from concourse import mybir as _mybir
    from concourse.bass_utils import run_bass_kernel_spmd as _run

    nc = _bacc.Bacc("TRN2", target_bir_lowering=False, num_devices=1)
    arrays, args = {}, []
    for name in _INS:
        a = _np.ascontiguousarray(inputs[name])
        arrays[f"in_{name}_dram"] = a
        args.append(nc.dram_tensor(f"in_{name}_dram", a.shape, _mybir.dt.from_np(a.dtype), kind="ExternalInput").ap())
    args.append(nc.dram_tensor("out_0_dram", inputs["x"].shape, F32, kind="ExternalOutput").ap())
    encoder_block(nc, *args)
    r = _run(nc, [arrays], core_ids=[0])
    return r.results[0]["out_0_dram"]
```
